# Optimizing a Trainium2 kernel written in Bass

```python
import math
import jax, jax.numpy as jnp
from jax import lax
import numpy as np

D_MODEL = 1024
BATCH = 1
SEQ = 256
DEPTH = 2

D_FF = 2816
NORM_EPS = 1e-6

HY_WIDTH = D_MODEL // 4
HY_ORDER = 2
HY_SHORT = 3
HY_BANDS = 16
HY_EMB = 1 + 2 * HY_BANDS
HY_FILTER_HIDDEN = 64
HY_FAST_DECAY_PCT = 0.3
HY_SLOW_DECAY_PCT = 1.5
HY_DECAY_TARGET = 1e-2
HY_DECAY_SHIFT = 0.0
HY_IN = (HY_ORDER + 1) * HY_WIDTH

MLA_HEADS = 4
MLA_QK_NOPE = 128
MLA_QK_ROPE = 64
MLA_V_HEAD = 128
MLA_Q_LORA = D_MODEL // 4
MLA_KV_LORA = D_MODEL // 8
MLA_WIDTH = MLA_HEADS * MLA_V_HEAD
ROPE_BASE = 10000.0
Q_BLOCK = 128

GLA_HEADS = 4
GLA_WIDTH = D_MODEL // 4
GLA_KEY = GLA_WIDTH // 2
GLA_DK = GLA_KEY // GLA_HEADS
GLA_DV = GLA_WIDTH // GLA_HEADS
GLA_GATE_RANK = 16
GLA_GATE_NORM = 16.0
GLA_CHUNK = 64

MIX_WIDTH = HY_WIDTH + MLA_WIDTH + GLA_WIDTH
IN_SPLITS = (HY_IN, MLA_Q_LORA, MLA_KV_LORA, MLA_QK_ROPE, GLA_KEY, GLA_KEY, GLA_WIDTH, GLA_GATE_RANK, GLA_GATE_RANK, GLA_WIDTH)
IN_WIDTH = sum(IN_SPLITS)

kernel_name = 'hybrid_hyena_mla_gla_macaron_encoder'

def rms_norm(x, g):
    xf = x.astype(jnp.float32)
    y = xf * lax.rsqrt(jnp.mean(xf * xf, axis=-1, keepdims=True) + NORM_EPS)
    return (y * g.astype(jnp.float32)).astype(x.dtype)

def swiglu_ffn(x, w_gate, w_up, w_down):
    return (jax.nn.silu(x @ w_gate) * (x @ w_up)) @ w_down

def centred_short_conv(u, w, b):
    L = u.shape[1]
    pad = HY_SHORT // 2
    up = jnp.pad(u, ((0, 0), (pad, HY_SHORT - 1 - pad), (0, 0)))
    y = b
    for tap in range(HY_SHORT):
        y = y + up[:, tap:tap + L] * w[tap]
    return y

def hyena_filters(L, w1, b1, f1, w2, b2, f2, w3):
    pos = jnp.arange(L, dtype=jnp.float32)
    t = pos / (L - 1)
    bands = jnp.linspace(1e-4, HY_BANDS - 1, HY_BANDS, dtype=jnp.float32)
    ang = (2.0 * math.pi * pos / L)[:, None] * bands[None, :]
    z = jnp.concatenate([t[:, None], jnp.cos(ang), -jnp.sin(ang)], axis=-1)
    h = jnp.sin(f1 * (z @ w1 + b1))
    h = jnp.sin(f2 * (h @ w2 + b2))
    h = (h @ w3).astype(jnp.float32).reshape(L, HY_ORDER, 2, HY_WIDTH)
    max_decay = math.log(HY_DECAY_TARGET) / HY_FAST_DECAY_PCT
    min_decay = math.log(HY_DECAY_TARGET) / HY_SLOW_DECAY_PCT
    deltas = jnp.abs(jnp.linspace(min_decay, max_decay, HY_WIDTH, dtype=jnp.float32))
    window = jnp.exp(-t[:, None] * deltas[None, :]) + HY_DECAY_SHIFT
    h = h * window[:, None, None, :]
    h_fwd = h[:, :, 0]
    h_bwd = h[1:, :, 1][::-1]
    return jnp.concatenate([h_fwd, jnp.zeros_like(h_fwd[:1]), h_bwd], axis=0)

def fft_long_conv(u, kern, skip):
    L = u.shape[1]
    U = jnp.fft.rfft(u, n=2 * L, axis=1)
    K = jnp.fft.rfft(kern, n=2 * L, axis=0)
    y = jnp.fft.irfft(U * K[None], n=2 * L, axis=1)[:, :L]
    return y + u * skip.astype(jnp.float32)

def hyena_mixer(u_proj, conv_w, conv_b, w1, b1, f1, w2, b2, f2, w3, skip, out_norm):
    dtype = u_proj.dtype
    L = u_proj.shape[1]
    u = centred_short_conv(u_proj, conv_w, conv_b).astype(jnp.float32)
    v, x1, x2 = jnp.split(u, HY_ORDER + 1, axis=-1)
    kern = hyena_filters(L, w1, b1, f1, w2, b2, f2, w3)
    z = x1 * fft_long_conv(v, kern[:, 0], skip[0])
    y = x2 * fft_long_conv(z, kern[:, 1], skip[1])
    return rms_norm(y.astype(dtype), out_norm)

def rope(x, pos):
    half = x.shape[-1] // 2
    inv = ROPE_BASE ** (-jnp.arange(half, dtype=jnp.float32) * 2.0 / x.shape[-1])
    ang = pos[:, None] * inv[None, :]
    cos = jnp.cos(ang)[None, :, None, :]
    sin = jnp.sin(ang)[None, :, None, :]
    xf = x.astype(jnp.float32)
    a, b = xf[..., :half], xf[..., half:]
    return jnp.concatenate([a * cos - b * sin, a * sin + b * cos], axis=-1).astype(x.dtype)

def mla_mixer(cq_in, ckv_in, kr_in, q_norm, w_uq, kv_norm, w_ukv, out_norm):
    B, S, _ = cq_in.shape
    dqk = MLA_QK_NOPE + MLA_QK_ROPE
    pos = jnp.arange(S, dtype=jnp.float32)
    q = (rms_norm(cq_in, q_norm) @ w_uq).reshape(B, S, MLA_HEADS, dqk)
    q = jnp.concatenate([q[..., :MLA_QK_NOPE], rope(q[..., MLA_QK_NOPE:], pos)], axis=-1)
    kv = (rms_norm(ckv_in, kv_norm) @ w_ukv).reshape(B, S, MLA_HEADS, MLA_QK_NOPE + MLA_V_HEAD)
    k_nope, v = kv[..., :MLA_QK_NOPE], kv[..., MLA_QK_NOPE:]
    k_rope = rope(kr_in[:, :, None, :], pos)
    k = jnp.concatenate([k_nope, jnp.broadcast_to(k_rope, (B, S, MLA_HEADS, MLA_QK_ROPE))], axis=-1)
    scale = dqk ** -0.5
    qb = q.reshape(B, S // Q_BLOCK, Q_BLOCK, MLA_HEADS, dqk).transpose(1, 0, 2, 3, 4)

    def attend_block(q_blk):
        s = jnp.einsum('bqhd,bkhd->bhqk', q_blk, k).astype(jnp.float32) * scale
        p = jax.nn.softmax(s, axis=-1).astype(v.dtype)
        return jnp.einsum('bhqk,bkhe->bqhe', p, v)

    o = lax.map(attend_block, qb)
    o = o.transpose(1, 0, 2, 3, 4).reshape(B, S, MLA_WIDTH)
    return rms_norm(o, out_norm)

def gla_chunk_scan(q, k, v, g, inclusive):
    B, S, H, dk = q.shape
    dv = v.shape[-1]
    n_chunks = S // GLA_CHUNK

    def to_chunks(t):
        return t.reshape(B, n_chunks, GLA_CHUNK, H, t.shape[-1]).transpose(1, 0, 3, 2, 4)

    mask = jnp.tril(jnp.ones((GLA_CHUNK, GLA_CHUNK), dtype=bool), k=0 if inclusive else -1)

    def step(state, inp):
        qc, kc, vc, gc = inp
        b = lax.cumsum(gc, axis=2)
        o_inter = jnp.einsum('bhcd,bhde->bhce', qc * jnp.exp(b), state)
        diff = b[:, :, :, None, :] - b[:, :, None, :, :]
        decay = jnp.exp(jnp.where(mask[:, :, None], diff, -jnp.inf))
        attn = jnp.einsum('bhid,bhjd,bhijd->bhij', qc, kc, decay)
        o_intra = jnp.einsum('bhij,bhje->bhie', attn, vc)
        b_last = b[:, :, -1:, :]
        state = jnp.exp(b_last[:, :, 0, :, None]) * state + jnp.einsum('bhcd,bhce->bhde', kc * jnp.exp(b_last - b), vc)
        return state, o_inter + o_intra

    init = jnp.zeros((B, H, dk, dv), jnp.float32)
    _, o = lax.scan(step, init, (to_chunks(q), to_chunks(k), to_chunks(v), to_chunks(g)))
    return o.transpose(1, 0, 3, 2, 4).reshape(B, S, H, dv)

def gla_mixer(q_in, k_in, v_in, gf_in, gb_in, r_in, w_gf, b_gf, w_gb, b_gb, head_norm):
    dtype = q_in.dtype
    B, S, _ = q_in.shape
    f32 = jnp.float32

    def heads(t, d):
        return t.astype(f32).reshape(B, S, GLA_HEADS, d)

    q = heads(q_in, GLA_DK) * (GLA_DK ** -0.5)
    k = heads(k_in, GLA_DK)
    v = heads(v_in, GLA_DV)
    g_f = heads(jax.nn.log_sigmoid(gf_in.astype(f32) @ w_gf.astype(f32) + b_gf.astype(f32)) / GLA_GATE_NORM, GLA_DK)
    g_b = heads(jax.nn.log_sigmoid(gb_in.astype(f32) @ w_gb.astype(f32) + b_gb.astype(f32)) / GLA_GATE_NORM, GLA_DK)
    o_f = gla_chunk_scan(q, k, v, g_f, True)
    o_b = gla_chunk_scan(q[:, ::-1], k[:, ::-1], v[:, ::-1], g_b[:, ::-1], False)[:, ::-1]
    o = rms_norm(o_f + o_b, head_norm).reshape(B, S, GLA_WIDTH)
    return (o * jax.nn.silu(r_in.astype(f32))).astype(dtype)

def hybrid_layer(x, ffn1_norm, ffn1_w_gate, ffn1_w_up, ffn1_w_down, mix_norm, w_in,
                 hy_conv_w, hy_conv_b, hy_filt_w1, hy_filt_b1, hy_filt_freq1, hy_filt_w2, hy_filt_b2,
                 hy_filt_freq2, hy_filt_w3, hy_skip, hy_out_norm,
                 mla_q_norm, mla_w_uq, mla_kv_norm, mla_w_ukv, mla_out_norm,
                 gla_w_gate_fwd, gla_b_gate_fwd, gla_w_gate_bwd, gla_b_gate_bwd, gla_head_norm,
                 w_out, ffn2_norm, ffn2_w_gate, ffn2_w_up, ffn2_w_down):
    x = x + 0.5 * swiglu_ffn(rms_norm(x, ffn1_norm), ffn1_w_gate, ffn1_w_up, ffn1_w_down)
    proj = rms_norm(x, mix_norm) @ w_in
    offsets = [int(o) for o in np.cumsum(IN_SPLITS)[:-1]]
    (hy_in, mla_cq, mla_ckv, mla_kr, gla_q, gla_k, gla_v, gla_gf, gla_gb, gla_r) = jnp.split(proj, offsets, axis=-1)
    y_hy = hyena_mixer(hy_in, hy_conv_w, hy_conv_b, hy_filt_w1, hy_filt_b1, hy_filt_freq1, hy_filt_w2,
                       hy_filt_b2, hy_filt_freq2, hy_filt_w3, hy_skip, hy_out_norm)
    y_mla = mla_mixer(mla_cq, mla_ckv, mla_kr, mla_q_norm, mla_w_uq, mla_kv_norm, mla_w_ukv, mla_out_norm)
    y_gla = gla_mixer(gla_q, gla_k, gla_v, gla_gf, gla_gb, gla_r, gla_w_gate_fwd, gla_b_gate_fwd,
                      gla_w_gate_bwd, gla_b_gate_bwd, gla_head_norm)
    x = x + jnp.concatenate([y_hy, y_mla, y_gla], axis=-1) @ w_out
    x = x + 0.5 * swiglu_ffn(rms_norm(x, ffn2_norm), ffn2_w_gate, ffn2_w_up, ffn2_w_down)
    return x

def setup_inputs(seed: int = 0) -> dict:
    key = jax.random.key(seed)
    ks = iter(jax.random.split(key, 40))

    def nrm(shape, scale):
        return scale * jax.random.normal(next(ks), shape, jnp.float32)

    def gain(shape):
        return 1.0 + nrm(shape, 0.02)

    L = DEPTH
    Hf = HY_FILTER_HIDDEN
    return {
        'x': nrm((BATCH, SEQ, D_MODEL), 1.0),
        'ffn1_norm': gain((L, D_MODEL)),
        'ffn1_w_gate': nrm((L, D_MODEL, D_FF), D_MODEL ** -0.5),
        'ffn1_w_up': nrm((L, D_MODEL, D_FF), D_MODEL ** -0.5),
        'ffn1_w_down': nrm((L, D_FF, D_MODEL), D_FF ** -0.5),
        'mix_norm': gain((L, D_MODEL)),
        'w_in': nrm((L, D_MODEL, IN_WIDTH), D_MODEL ** -0.5),
        'hy_conv_w': nrm((L, HY_SHORT, HY_IN), HY_SHORT ** -0.5),
        'hy_conv_b': nrm((L, HY_IN), 0.02),
        'hy_filt_w1': nrm((L, HY_EMB, Hf), HY_EMB ** -0.5),
        'hy_filt_b1': nrm((L, Hf), 0.02),
        'hy_filt_freq1': gain((L, Hf)),
        'hy_filt_w2': nrm((L, Hf, Hf), Hf ** -0.5),
        'hy_filt_b2': nrm((L, Hf), 0.02),
        'hy_filt_freq2': gain((L, Hf)),
        'hy_filt_w3': nrm((L, Hf, HY_ORDER * 2 * HY_WIDTH), Hf ** -0.5),
        'hy_skip': nrm((L, HY_ORDER, HY_WIDTH), 1.0),
        'hy_out_norm': gain((L, HY_WIDTH)),
        'mla_q_norm': gain((L, MLA_Q_LORA)),
        'mla_w_uq': nrm((L, MLA_Q_LORA, MLA_HEADS * (MLA_QK_NOPE + MLA_QK_ROPE)), MLA_Q_LORA ** -0.5),
        'mla_kv_norm': gain((L, MLA_KV_LORA)),
        'mla_w_ukv': nrm((L, MLA_KV_LORA, MLA_HEADS * (MLA_QK_NOPE + MLA_V_HEAD)), MLA_KV_LORA ** -0.5),
        'mla_out_norm': gain((L, MLA_WIDTH)),
        'gla_w_gate_fwd': nrm((L, GLA_GATE_RANK, GLA_KEY), GLA_GATE_RANK ** -0.5),
        'gla_b_gate_fwd': nrm((L, GLA_KEY), 0.1),
        'gla_w_gate_bwd': nrm((L, GLA_GATE_RANK, GLA_KEY), GLA_GATE_RANK ** -0.5),
        'gla_b_gate_bwd': nrm((L, GLA_KEY), 0.1),
        'gla_head_norm': gain((L, GLA_DV)),
        'w_out': nrm((L, MIX_WIDTH, D_MODEL), MIX_WIDTH ** -0.5),
        'ffn2_norm': gain((L, D_MODEL)),
        'ffn2_w_gate': nrm((L, D_MODEL, D_FF), D_MODEL ** -0.5),
        'ffn2_w_up': nrm((L, D_MODEL, D_FF), D_MODEL ** -0.5),
        'ffn2_w_down': nrm((L, D_FF, D_MODEL), D_FF ** -0.5),
        'final_norm': gain((D_MODEL,)),
    }

def reference(x, ffn1_norm, ffn1_w_gate, ffn1_w_up, ffn1_w_down, mix_norm, w_in,
              hy_conv_w, hy_conv_b, hy_filt_w1, hy_filt_b1, hy_filt_freq1, hy_filt_w2, hy_filt_b2,
              hy_filt_freq2, hy_filt_w3, hy_skip, hy_out_norm,
              mla_q_norm, mla_w_uq, mla_kv_norm, mla_w_ukv, mla_out_norm,
              gla_w_gate_fwd, gla_b_gate_fwd, gla_w_gate_bwd, gla_b_gate_bwd, gla_head_norm,
              w_out, ffn2_norm, ffn2_w_gate, ffn2_w_up, ffn2_w_down, final_norm):
    for l in range(DEPTH):
        x = hybrid_layer(x, ffn1_norm[l], ffn1_w_gate[l], ffn1_w_up[l], ffn1_w_down[l], mix_norm[l], w_in[l],
                         hy_conv_w[l], hy_conv_b[l], hy_filt_w1[l], hy_filt_b1[l], hy_filt_freq1[l],
                         hy_filt_w2[l], hy_filt_b2[l], hy_filt_freq2[l], hy_filt_w3[l], hy_skip[l], hy_out_norm[l],
                         mla_q_norm[l], mla_w_uq[l], mla_kv_norm[l], mla_w_ukv[l], mla_out_norm[l],
                         gla_w_gate_fwd[l], gla_b_gate_fwd[l], gla_w_gate_bwd[l], gla_b_gate_bwd[l], gla_head_norm[l],
                         w_out[l], ffn2_norm[l], ffn2_w_gate[l], ffn2_w_up[l], ffn2_w_down[l])
    return rms_norm(x, final_norm)


_drawn_inputs = setup_inputs


def setup_inputs(seed=0):
    import zlib

    import numpy as np

    out = dict(_drawn_inputs(seed))
    spreads = {}
    factors = {'ffn1_norm': 3.724,
     'hy_filt_freq1': 5.763,
     'hy_filt_freq2': 5.478,
     'hy_out_norm': 20.63,
     'mla_q_norm': 4.885,
     'mla_out_norm': 13.946,
     'gla_b_gate_fwd': 5.748,
     'gla_b_gate_bwd': 6.342,
     'gla_head_norm': 35.936,
     'ffn2_norm': 6.869,
     'final_norm': 8.019}
    for name, (base, spread) in spreads.items():
        noise = np.random.default_rng([zlib.crc32(name.encode()), seed]).standard_normal(out[name].shape)
        drawn = base * np.exp(spread * noise) if base else spread * noise
        out[name] = __import__('jax').numpy.asarray(drawn.astype(out[name].dtype))
    for name, factor in factors.items():
        out[name] = (out[name] * factor).astype(out[name].dtype)
    return out
```

```python
from contextlib import ExitStack
import math

import numpy as np
import concourse.bass as bass
from concourse import mybir

F32 = mybir.dt.float32
F32R = mybir.dt.float32r
U8 = mybir.dt.uint8
ACT = mybir.ActivationFunctionType
ALU = mybir.AluOpType
AX = mybir.AxisListType

P = 128
SEQ, D, FF, DEPTH = 256, 1024, 2816, 2
T = SEQ // P
KD = D // P
CH = FF // 256
RING = 3
SLOT = 4 * 512
FFN_SLOTS = 3 * CH
MIX = FFN_SLOTS
MIX_SLOTS = 15
FFN2 = MIX + MIX_SLOTS
SLOTS = FFN2 + FFN_SLOTS
S_G2, S_G3, S_G1, S_UQN, S_UQR, S_UKV, S_G4, S_WO = (MIX + n for n in (0, 2, 4, 6, 7, 8, 9, 11))
assert SLOTS % RING == 0 and CH % 2 == 1

HYW, HYE, HYF = 256, 33, 64
H, DN, DR, DV = 4, 128, 64, 128
GDK, GDV = 32, 64
LEVELS = 8
EPS = 1e-6
MLA_SCALE = float(DN + DR) ** -0.5

(C_G1, C_GM, C_G2, C_QN, C_KVN, C_GO, C_W0, C_W1, C_W2, C_CB, C_BG, C_FB1, C_FF1, C_FB2, C_FF2,
 NPAR) = np.cumsum([0, 8, 8, 8, 2, 1, 8, 6, 6, 6, 6, 2, 1, 1, 1, 1]).tolist()
I_D, I_CQ, I_M, I_H, I_G, I_EPS, I_POW, NCST = (128 + np.cumsum([0, 2, 4, 2, 2, 8, 8, 8])).tolist()
F_WIN, F_Z, F_W1, F_W2, F_W3, F_DFT, F_SKIP, NFIL = np.cumsum([0, 1024, 256, 64, 64, 1024, 768, 512]).tolist()
T_SS, T_R, T_S4, T_R4, T_SM, T_RM, T_SH, T_RH, T_S8, T_R8, T_MX, T_RS, T_RR, NST = np.cumsum(
    [0, 2, 2, 4, 4, 2, 2, 2, 2, 8, 8, 8, 8, 8]).tolist()
TWO_PI_A, TWO_PI_B = 6.28125, 2029.0 / 2 ** 20
TWO_PI_C = 2 * math.pi - TWO_PI_A - TWO_PI_B
ROUND = 1.5 * 2 ** 23
PI_F = 3.1415925
Y_TILES = [(2, 3), (4, 5), (0, 1), (6, 7)]
Y_BANKS = [4, 5, 6, 4]
NORMS = 3
TURNS = 4
LINKS = {"dve": 24, "pool": 43, "act": 2}


class Mark:

    def __init__(self, sem, per):
        self.sem, self.per = sem, per

    def at(self, l, v=1):
        return l * self.per + v


def pos(n):
    return (n + 1) % RING


def build(nc, x_d, w_d, par_d, cst_d, fil_d, gate_d, dft_d, rope_d, mask_d, fin_d, out_d):
    with ExitStack() as ctx:
        def sb(name, shape, dt=F32):
            return ctx.enter_context(nc.sbuf_tensor(name, shape, dt))

        def mark(name, per):
            return Mark(ctx.enter_context(nc.semaphore(name)), per)

        raw = [sb(f"w_raw{i}", [P, 4, 512]) for i in range(RING)]
        WH = [sb(f"w_high{i}", [P, 4, 512], F32R) for i in range(RING)]
        WL = [sb(f"w_low{i}", [P, 4, 512], F32R) for i in range(RING)]
        x = sb("x", [P, T, D])
        xn = sb("x_normed", [P, T, D])
        XH = sb("xT_high", [P, KD, SEQ], F32R)
        XL = sb("xT_low", [P, KD, SEQ], F32R)
        sg = sb("silu_gate", [P, T, 256])
        hid = sb("hidden", [P, T, 256])
        HH = sb("hT_high", [P, 2, SEQ], F32R)
        HL = sb("hT_low", [P, 2, SEQ], F32R)
        KVH = sb("kvT_high", [P, SEQ], F32R)
        KVL = sb("kvT_low", [P, SEQ], F32R)
        par_all = sb("par_all", [P, DEPTH, NPAR])
        par = sb("par", [P, NPAR])
        cst = sb("constants", [P, NCST])
        ident = cst[:, 0:P]
        st = sb("statistics", [P, NST])
        dft = sb("dft", [P, T, 512])
        idft = sb("inverse_dft", [P, 4, SEQ])
        rope = sb("rope", [P, 2, T, DR])
        mask = sb("level_masks", [P, LEVELS - 1, P], U8)
        wg = sb("gate_weights", [P, 2, P])
        KA = sb("filter_re", [P, 2, 512])
        KI = sb("filter_im", [P, 2, 512])
        KB = sb("filter_nyquist", [P, 512])
        scratch = sb("mixer_scratch", [P, 16896])
        cols = [0]

        def view(*dims, at=None):
            n = int(np.prod(dims))
            a = cols[0] if at is None else at
            if at is None:
                cols[0] += n
            v = scratch[:, a:a + n]
            if len(dims) == 2:
                v = v.rearrange("p (a b) -> p a b", b=dims[1])
            if len(dims) == 3:
                v = v.rearrange("p (a b c) -> p a b c", b=dims[1], c=dims[2])
            return v

        QN, QR, KN = view(H, SEQ), view(H, SEQ), view(H, SEQ)
        VM = view(T, H * DV)
        PE_ = view(H, SEQ)
        PT = view(2, H, P)
        AD = view(H, T, P)
        AC = view(H, T, P)
        Z = AC.rearrange("p h t c -> p (h t c)").rearrange("p (a b c) -> p a b c", a=2, b=2)
        Y = view(4, SEQ)
        TT = view(4, SEQ)
        filter_cols = cols[0]
        KR = view(SEQ)
        QK = view(2, SEQ)
        G0 = cols[0]
        G = view(4, SEQ)
        QKL = [view(2, SEQ), view(2, SEQ)]
        VG, RG = view(T, 256), view(T, 256)
        C = view(4, SEQ)
        NV = view(3, T, 256)
        KT = view(2, T, DR)
        MASK_AT = G0
        assert cols[0] <= 16896, cols[0]
        fil = scratch[:, 0:NFIL]
        at = NFIL
        H1, H2 = view(SEQ, at=at), view(SEQ, at=at + SEQ)
        ARG, TURN = view(SEQ, at=at + 2 * SEQ), view(SEQ, at=at + 3 * SEQ)
        HW = view(2, T, 512, at=at + 4 * SEQ)
        HS = view(T, 512, at=at + 4 * SEQ + 2048)
        HD = view(T, 512, at=at + 4 * SEQ + 3072)
        assert at + 4 * SEQ + 4096 <= filter_cols

        PS = ctx.enter_context(nc.psum_tensor("psum", [P, 8, 512], F32))

        s_in = mark("inputs_landed", 0)
        landed = [mark(f"slot_landed{i}", SLOTS // RING * 16) for i in range(RING)]
        s_hi, s_lo, s_used = mark("slot_high", SLOTS), mark("slot_low", SLOTS), mark("slot_used", SLOTS)
        s_par = mark("params_copied", 1)
        s_fil = mark("filter_pack_landed", 32)
        s_x = mark("x_updated", 2 * NORMS)
        s_ss, s_rstd, s_xn = mark("squares_summed", 2 * NORMS), mark("rstd", NORMS), mark("x_scaled", 2 * NORMS)
        s_tr, s_xh, s_xl = (mark(n, 4 * TURNS) for n in ("turned", "turned_high", "turned_low"))
        s_gu, s_silu, s_h = mark("gate_up_first_half", 2 * CH), mark("silu", 4 * CH), mark("hidden_done", 4 * CH)
        s_ht, s_hh, s_hl = (mark(n, 2 * CH) for n in ("hidden_turned", "hT_high_done", "hT_low_done"))
        s_out = mark("out_landed", 0)
        f_mm, f_arg, f_sin = mark("filter_mm", 2), mark("sine_argument", 2), mark("sine", 2)
        f_w3, f_hw, f_hs = mark("filter_taps", 4), mark("taps_windowed", 4), mark("taps_summed", 1)
        k_mm, k_ev = mark("filter_dft", 5), mark("filter_dft_copied", 5)
        c_base, c_conv, c_tr, c_nat = mark("conv_centre", 6), mark("conv_done", 6), mark("conv_turned", 3), mark("conv_natural", 3)
        g_qk, g_in, g_z, g_az = mark("gla_qk", 1), mark("gate_in", 1), mark("gate_mm", 1), mark("gate_logits", 1)
        g_ln, g_g0 = mark("gate_log", 1), mark("gate_exponents", 1)
        g_e, g_lq, g_gu = mark("level_exp", LEVELS), mark("level_qk", LEVELS), mark("level_exponents", LEVELS - 1)
        g_ls, g_la = mark("level_scores", LEVELS + 1), mark("level_scores_kept", LEVELS + 1)
        g_vr = mark("gla_vr", 2)
        g_o, g_sq, g_s8, g_r8, g_y, g_r = (mark(n, 1) for n in ("gla_out", "gla_squares", "gla_sums", "gla_rstd", "gla_y", "gla_silu"))
        q_ss, q_r, q_n, q_kt, q_kr = (mark(n, 1) for n in ("latent_squares", "latent_rstd", "latent_normed", "k_rope_products", "k_rope"))
        q_tr, q_hi, q_lo, q_krt = mark("latent_turned", 2), mark("latent_high", 2), mark("latent_low", 2), mark("k_rope_turned_copied", 1)
        a_qn, a_qt, a_qr, a_qtr, a_qre = mark("q_copied", 2), mark("q_rope_products", 1), mark("q_rope", 1), mark("q_rope_turned", 1), mark("q_rope_copied", 2)
        a_kn, a_v = mark("k_copied", 2), mark("v_copied", 2)
        a_s, a_mx, a_p, a_pt, a_pte = (mark(n, 2) for n in ("scores", "score_max", "probs", "probs_turned", "probs_turned_copied"))
        a_o, a_oe = mark("attended", 2), mark("attended_scaled", 2)
        a_sq, a_r, a_y = mark("mla_squares", 2), mark("mla_rstd", 1), mark("mla_y", 1)
        h_u, h_pr, h_y, h_inv, h_z = (mark(n, 2) for n in ("hy_dft", "hy_products", "hy_spectrum", "hy_inverse", "hy_gated"))
        h_sq, h_r, h_yy = mark("hy_squares", 2), mark("hy_rstd", 1), mark("hy_y", 1)
        s_step = {n: mark(f"step_{n}", 0) for n in ("pe", "pool", "dve")}
        chain = {n: mark(f"order_{n}", LINKS[n]) for n in LINKS}
        linked = {}

        def linker(e, name):
            linked[name] = 0

            def link(l, ins):
                linked[name] += 1
                ins.then_inc(chain[name].sem, 1)
                e.wait_ge(chain[name].sem, chain[name].at(l, linked[name]))
            return link

        def hold(e, name):
            e.sem_inc(s_step[name].sem, 1)

        def used(l, n):
            return s_used.at(l, n + RING + 1)

        block = ctx.enter_context(nc.Block())

        @block.sync
        def _(e):
            with e.Fori(0, DEPTH * SLOTS // RING) as i:
                for u in range(RING):
                    e.wait_ge(s_used.sem, i * RING + u + 1)
                    src = w_d[bass.ds(i * RING + u, 1), :, :].rearrange("s p n -> (s p) n")
                    e.dma_start(raw[pos(u)][:].rearrange("p a b -> p (a b)"), src).then_inc(landed[pos(u)].sem, 16)
            e.wait_ge(s_xn.sem, 2 * NORMS * DEPTH + 2)
            e.dma_start(out_d.rearrange("(t p) d -> p t d", p=P), xn[:]).then_inc(s_out.sem, 16)
            e.wait_ge(s_out.sem, 16)

        @block.gpsimd
        def _(e):
            link = linker(e, "pool")
            e.wait_ge(s_in.sem, N_IN * 16)

            def rstd(l, m, v, src, dst, inv, n, done):
                e.wait_ge(m.sem, m.at(l, v))
                a, b = st[:, src:src + n], st[:, dst:dst + n]
                link(l, e.tensor_tensor(b, a, cst[:, inv:inv + n], ALU.mult))
                link(l, e.tensor_tensor(b, b, cst[:, I_EPS:I_EPS + n], ALU.add))
                e.tensor_tensor(b, b, cst[:, I_POW:I_POW + n], ALU.pow).then_inc(done.sem, 1)

            def levels(l, b):
                B = 1 << b
                e.wait_ge(g_e.sem, g_e.at(l, b + 1))
                g = [G[:, n, :].rearrange("p (a w b) -> p a w b", w=2, b=B) for n in range(4)]
                n = SEQ // (2 * B)
                sb_, pf, sf, pb_ = g

                def add(to, side, of, oside, i, last=False):
                    o = of[:, :, oside, i:i + 1].to_broadcast([P, n, B])
                    return e.tensor_tensor(to[:, :, side, :], to[:, :, side, :], o, ALU.add)
                link(l, add(sf, 0, pf, 1, B - 1))
                link(l, add(pb_, 1, sb_, 0, 0))
                link(l, add(pf, 1, pf, 0, B - 1))
                add(sb_, 0, sb_, 1, 0).then_inc(g_gu.sem, 1)

            with e.Fori(0, DEPTH) as l:
                e.wait_ge(s_x.sem, s_x.at(l, 2))
                hold(e, "pool")
                e.tensor_copy(par[:], par_all[:, bass.ds(l, 1), :].rearrange("p a b -> p (a b)")).then_inc(s_par.sem, 1)
                e.dma_start(fil, fil_d[bass.ds(l, 1), :, :].rearrange("s p n -> (s p) n")).then_inc(s_fil.sem, 16)
                e.dma_start(wg[64:96, :, :].rearrange("p a b -> p (a b)"), gate_d[bass.ds(l, 1), :, :].rearrange("s p n -> (s p) n")).then_inc(s_fil.sem, 16)
                rstd(l, s_ss, 2, T_SS, T_R, I_D, 2, s_rstd)
                rstd(l, s_ss, 4, T_SS, T_R, I_D, 2, s_rstd)
                for o in range(2):
                    for p in range(T):
                        e.wait_ge(f_hw.sem, f_hw.at(l, o * 2 + p + 1))
                        a, b = HW[:, o, p, 0:256], HW[:, o, p, 256:512]
                        link(l, e.tensor_tensor(HS[:, p, o * 256:(o + 1) * 256], a, b, ALU.add))
                        link(l, e.tensor_tensor(HD[:, p, o * 256:(o + 1) * 256], a, b, ALU.subtract))
                e.tensor_tensor(HS[0:1, 0, :], HS[0:1, 0, :], fil[0:1, F_SKIP:F_SKIP + 512], ALU.add).then_inc(f_hs.sem, 1)
                rstd(l, q_ss, 1, T_S4, T_R4, I_CQ, 4, q_r)
                e.wait_ge(q_kt.sem, q_kt.at(l))
                e.tensor_tensor(xn[:, :, 640:704], KT[:, 0], KT[:, 1], ALU.add).then_inc(q_kr.sem, 1)
                e.wait_ge(a_qt.sem, a_qt.at(l))
                e.tensor_tensor(xn[:, :, 768:1024], TT[:, 0:2, :], TT[:, 2:4, :], ALU.add).then_inc(a_qr.sem, 1)
                levels(l, 0)
                e.wait_ge(h_pr.sem, h_pr.at(l, 1))
                e.tensor_tensor(Y, Y, TT, ALU.add).then_inc(h_y.sem, 1)
                levels(l, 1)
                levels(l, 2)
                e.wait_ge(h_pr.sem, h_pr.at(l, 2))
                e.tensor_tensor(Y, Y, TT, ALU.add).then_inc(h_y.sem, 1)
                levels(l, 3)
                levels(l, 4)
                levels(l, 5)
                levels(l, 6)
                rstd(l, h_sq, 2, T_SH, T_RH, I_H, 2, h_r)
                rstd(l, a_sq, 2, T_SM, T_RM, I_M, 2, a_r)
                rstd(l, g_s8, 1, T_S8, T_R8, I_G, 8, g_r8)
                rstd(l, s_ss, 6, T_SS, T_R, I_D, 2, s_rstd)
            e.wait_ge(s_ss.sem, DEPTH * 2 * NORMS + 2)
            a, b = st[:, T_SS:T_SS + 2], st[:, T_R:T_R + 2]
            last = DEPTH * LINKS["pool"]
            e.tensor_tensor(b, a, cst[:, I_D:I_D + 2], ALU.mult).then_inc(chain["pool"].sem, 1)
            e.wait_ge(chain["pool"].sem, last + 1)
            e.tensor_tensor(b, b, cst[:, I_EPS:I_EPS + 2], ALU.add).then_inc(chain["pool"].sem, 1)
            e.wait_ge(chain["pool"].sem, last + 2)
            e.tensor_tensor(b, b, cst[:, I_POW:I_POW + 2], ALU.pow).then_inc(s_rstd.sem, 1)

        @block.scalar
        def _(e):
            link = linker(e, "act")
            for dst, src in ((x[:], x_d.rearrange("(t p) d -> p t d", p=P)), (cst[:], cst_d),
                             (par_all[:].rearrange("p a b -> p (a b)"), par_d),
                             (dft[:].rearrange("p a b -> p (a b)"), dft_d[:, 0:1024]),
                             (idft[:].rearrange("p a b -> p (a b)"), dft_d[:, 1024:2048]),
                             (rope[:].rearrange("p a b c -> p (a b c)"), rope_d),
                             (scratch[:, MASK_AT:MASK_AT + (LEVELS - 1) * P], mask_d)):
                e.dma_start(dst, src).then_inc(s_in.sem, 16)

            def hi(l, n, occ=None):
                p, k = (pos(n), n // RING + 1) if occ is None else occ
                e.wait_ge(landed[p].sem, l * landed[p].per + k * 16)
                e.wait_ge(s_used.sem, l * SLOTS + n + 1)
                e.activation(WH[p][:], raw[p][:], ACT.Copy).then_inc(s_hi.sem, 1)

            def squares(l, j):
                for t in range(T):
                    e.wait_ge(s_x.sem, s_x.at(l, 2 * j + 1 + t))
                    e.activation(xn[:, t, :], x[:, t, :], ACT.Square, accum_out=st[:, T_SS + t:T_SS + t + 1]).then_inc(s_ss.sem, 1)

            def turned_high(l, j, g, bank, tiles, col):
                e.wait_ge(s_tr.sem, s_tr.at(l, 4 * j + g + 1))
                for n, k in enumerate(tiles):
                    r = e.activation(XH[:, k, :], PS[:, bank, n * SEQ:(n + 1) * SEQ], ACT.Copy, scale=par[:, col + k:col + k + 1])
                r.then_inc(s_xh.sem, 1)

            def norm(l, j, turn, col):
                squares(l, j)
                e.wait_ge(s_par.sem, s_par.at(l))
                for g in range(4):
                    turned_high(l, turn, g, g, (2 * g, 2 * g + 1), col)

            def silu(l, q, pr, slot):
                for t in range(T):
                    if t == 0:
                        e.wait_ge(s_gu.sem, s_gu.at(l, q + 1))
                    else:
                        e.wait_ge(s_used.sem, used(l, slot))
                    e.activation(sg[:, t, :], PS[:, 4 + 2 * pr + t, 0:256], ACT.Silu).then_inc(s_silu.sem, 1)

            def ht_high(l, q, pr):
                e.wait_ge(s_ht.sem, s_ht.at(l, q + 1))
                e.activation(HH[:].rearrange("p a b -> p (a b)"), PS[:, 4 + 2 * pr, :], ACT.Copy).then_inc(s_hh.sem, 1)

            def sine(l, n, dst):
                e.wait_ge(f_arg.sem, f_arg.at(l, n + 1))
                e.activation(dst[0:HYF], ARG[0:HYF], ACT.Sin).then_inc(f_sin.sem, 1)

            def ffn(l, f, base, j, turn, col):
                hi(l, base); hi(l, base + 1)
                norm(l, j, turn, col)
                hi(l, base + 2); hi(l, base + 3)

                def chunk(c, pr, slot, last=False):
                    q = f * CH + (c - 1)
                    silu(l, q, 1 - pr, slot)
                    for d in (1, 2) if last else (1, 2, 3):
                        hi(l, base + 3 * c + d, (pos(base + d), base // RING + c + d // RING + 1))
                        if d == 1:
                            ht_high(l, q, 1 - pr)
                chunk(1, 1, base + 1)
                if f == 0:
                    sine(l, 0, H1)
                with e.Fori(0, (CH - 3) // 2) as i:
                    chunk(i * 2 + 2, 0, base + (i * 2 + 1) * 3)
                    chunk(i * 2 + 3, 1, base + (i * 2 + 2) * 3)
                chunk(CH - 1, (CH - 1) % 2, base + 3 * (CH - 2), last=True)
                if f == 0:
                    sine(l, 1, H2)
                silu(l, f * CH + CH - 1, (CH - 1) % 2, base + 3 * (CH - 1))
                ht_high(l, f * CH + CH - 1, (CH - 1) % 2)

            def copy(dst, src, m=None, **kw):
                r = e.activation(dst, src, ACT.Copy, **kw)
                if m is not None:
                    r.then_inc(m.sem, 1)

            def conv_centre(tile, bank, dst):
                e.activation(C[:, dst, :], PS[:, bank, 0:SEQ], ACT.Identity, scale=par[:, C_W1 + tile:C_W1 + tile + 1],
                             bias=par[:, C_CB + tile:C_CB + tile + 1]).then_inc(c_base.sem, 1)

            def natural(l, n, which, bank):
                e.wait_ge(c_tr.sem, c_tr.at(l, n))
                copy(NV[:, which].rearrange("p a b -> p (a b)"), PS[:, bank, :], c_nat)

            def level_exp(l, b):
                B = 1 << b
                if b == 0:
                    e.wait_ge(g_g0.sem, g_g0.at(l))
                else:
                    e.wait_ge(g_gu.sem, g_gu.at(l, b))
                    e.wait_ge(g_lq.sem, g_lq.at(l, b))
                for n in range(2):
                    first = G[:, 2 * n:2 * n + 1, 0:1]
                    src = bass.AP(first.tensor, first.offset, [first.ap[0], [2 * B, SEQ // (2 * B)], [SEQ + B, 2], [1, B]])
                    dst = sg[:, n, :].rearrange("p (a w b) -> p a w b", w=2, b=B)
                    r = e.activation(dst, src, ACT.Exp)
                r.then_inc(g_e.sem, 1)

            def probs(l, s):
                e.wait_ge(a_mx.sem, a_mx.at(l, s + 1))
                if s:
                    e.wait_ge(a_pt.sem, a_pt.at(l, s))
                for h in range(H):
                    c = T_MX + 4 * s + h
                    r = e.activation(PE_[:, h, :], PS[:, 4 + h // 2, (h % 2) * SEQ:(h % 2 + 1) * SEQ], ACT.Exp,
                                     scale=MLA_SCALE, bias=st[:, c:c + 1], accum_out=st[:, T_RS + 4 * s + h:T_RS + 4 * s + h + 1])
                r.then_inc(a_p.sem, 1)

            def probs_turned(l, s):
                e.wait_ge(a_pt.sem, a_pt.at(l, s + 1))
                if s:
                    e.wait_ge(a_o.sem, a_o.at(l, s))
                copy(PT.rearrange("p a h c -> p (a h c)"), PS[:, 4:6, :], a_pte)

            with e.Fori(0, DEPTH) as l:
                ffn(l, 0, 0, 0, 0, C_G1)
                hi(l, S_G2); hi(l, S_G2 + 1)
                norm(l, 1, 1, C_GM)
                hi(l, S_G3); hi(l, S_G3 + 1)
                e.wait_ge(s_used.sem, used(l, S_G2 + 1))
                conv_centre(4, 4, 0); conv_centre(5, 5, 1)
                copy(QK[:, 0, :], PS[:, 6, 0:SEQ], scale=GDK ** -0.5)
                copy(QK[:, 1, :], PS[:, 7, 0:SEQ], g_qk)
                hi(l, S_G1)
                for n, dst in enumerate((KA[:, 0, :], KA[:, 1, :], KI[:, 0, :], KI[:, 1, :])):
                    e.wait_ge(k_mm.sem, k_mm.at(l, n + 1))
                    copy(dst, PS[:, n, :], k_ev)
                hi(l, S_G1 + 1)
                e.wait_ge(s_used.sem, used(l, S_G3 + 1))
                copy(hid[64:96, 0, :], PS[64:96, 4, 0:SEQ], g_in)
                for t in range(T):
                    e.activation(RG[:, t, :], PS[:, 5 + t, 0:256], ACT.Square, accum_out=st[:, T_S4 + 2 * t:T_S4 + 2 * t + 1])
                    r = e.activation(VG[:, t, 0:128], PS[:, 5 + t, 256:384], ACT.Square, accum_out=st[:, T_S4 + 2 * t + 1:T_S4 + 2 * t + 2])
                r.then_inc(q_ss.sem, 1)
                e.wait_ge(k_mm.sem, k_mm.at(l, 5))
                copy(KB[:], PS[:, 7, :], k_ev)
                hi(l, S_UQN)
                natural(l, 1, 2, 4)
                e.wait_ge(g_az.sem, g_az.at(l))
                link(l, e.activation(Z[:, 1], Z[:, 0], ACT.Abs))
                link(l, e.activation(Z[:, 1], Z[:, 1], ACT.Exp, scale=-1.0))
                e.activation(Z[:, 1], Z[:, 1], ACT.Ln, bias=1.0).then_inc(g_ln.sem, 1)
                e.wait_ge(q_tr.sem, q_tr.at(l, 1))
                for n in range(2):
                    r = e.activation(HH[:, n, :], PS[:, 5, n * SEQ:(n + 1) * SEQ], ACT.Copy, scale=par[:, C_QN + n:C_QN + n + 1])
                r.then_inc(q_hi.sem, 1)
                e.wait_ge(q_tr.sem, q_tr.at(l, 2))
                copy(KR[0:DR, :], PS[0:DR, 6, SEQ:2 * SEQ], q_krt)
                copy(KVH[:], PS[:, 6, 0:SEQ], q_hi, scale=par[:, C_KVN:C_KVN + 1])
                hi(l, S_UQR)
                e.wait_ge(s_used.sem, used(l, S_G1 + 1))
                e.wait_ge(c_tr.sem, c_tr.at(l, 1))
                for n in range(4):
                    conv_centre(n, n, n)
                hi(l, S_UKV)
                natural(l, 2, 0, 4)
                natural(l, 3, 1, 7)
                hi(l, S_G4)
                e.wait_ge(s_used.sem, used(l, S_UQN))
                for n in range(2):
                    copy(QN[:, 2 * n:2 * n + 2, :].rearrange("p a b -> p (a b)"), PS[:, n, :], a_qn)
                hi(l, S_G4 + 1)
                e.wait_ge(s_used.sem, used(l, S_UKV))
                for n in range(2):
                    copy(KN[:, 2 * n:2 * n + 2, :].rearrange("p a b -> p (a b)"), PS[:, 5 + n, :], a_kn)
                copy(VM[:, 0, :], PS[:, 3, :], a_v)
                copy(VM[:, 1, :], PS[:, 0, :], a_v)
                level_exp(l, 0)
                hi(l, S_WO)
                e.wait_ge(s_used.sem, used(l, S_G4 + 1))
                for t in range(T):
                    copy(VG[:, t, :], PS[:, 4 + t, 0:256])
                    copy(RG[:, t, :], PS[:, 4 + t, 256:512], g_vr)
                hi(l, S_WO + 1)
                hi(l, S_WO + 2)
                e.wait_ge(a_qtr.sem, a_qtr.at(l))
                for n in range(2):
                    copy(QR[0:DR, 2 * n:2 * n + 2, :].rearrange("p a b -> p (a b)"), PS[0:DR, 1 + n, :], a_qre)
                e.wait_ge(g_ls.sem, g_ls.at(l, 1))
                copy(AD.rearrange("p h t c -> p h (t c)"), PS[:, 0:4, 0:256], g_la)
                level_exp(l, 1)
                probs(l, 0)
                level_exp(l, 2)
                probs_turned(l, 0)
                level_exp(l, 3)
                level_exp(l, 4)
                probs(l, 1)
                level_exp(l, 5)
                probs_turned(l, 1)
                level_exp(l, 6)
                e.wait_ge(h_z.sem, h_z.at(l, 2))
                for t in range(T):
                    e.activation(TT[:, t, :], xn[:, t, 0:256], ACT.Square, accum_out=st[:, T_SH + t:T_SH + t + 1]).then_inc(h_sq.sem, 1)
                level_exp(l, 7)
                for s in range(T):
                    e.wait_ge(a_oe.sem, a_oe.at(l, s + 1))
                    e.activation(C[:, 2 * s:2 * s + 2, :].rearrange("p a b -> p (a b)"), xn[:, s, 256:768], ACT.Square,
                                 accum_out=st[:, T_SM + s:T_SM + s + 1]).then_inc(a_sq.sem, 1)
                e.wait_ge(g_ls.sem, g_ls.at(l, LEVELS + 1))
                copy(AC.rearrange("p h t c -> p h (t c)"), PS[:, 0:4, 0:256], g_la)
                e.activation(RG, RG, ACT.Silu).then_inc(g_r.sem, 1)
                for g in range(2):
                    turned_high(l, 2, g, Y_BANKS[g], Y_TILES[g], C_GO)
                e.wait_ge(g_o.sem, g_o.at(l))
                e.activation(sg[:].rearrange("p a b -> p (a b)"), PS[:, 7, :], ACT.Square).then_inc(g_sq.sem, 1)
                hi(l, S_WO + 3)
                for g in range(2, 4):
                    turned_high(l, 2, g, Y_BANKS[g], Y_TILES[g], C_GO)
                ffn(l, 1, FFN2, 2, 3, C_G2)
            for t in range(T):
                e.wait_ge(s_x.sem, DEPTH * 2 * NORMS + 1 + t)
                e.activation(xn[:, t, :], x[:, t, :], ACT.Square, accum_out=st[:, T_SS + t:T_SS + t + 1]).then_inc(s_ss.sem, 1)
            e.dma_start(C.rearrange("p a b -> p (a b)"), fin_d.rearrange("(a d) -> a d", a=1).to_broadcast([P, D])).then_inc(s_in.sem, 16)

        @block.vector
        def _(e):
            link = linker(e, "dve")

            def lo(l, n, p=None):
                p = pos(n) if p is None else p
                e.wait_ge(s_hi.sem, s_hi.at(l, n + 1))
                e.tensor_tensor(WL[p][:], raw[p][:], WH[p][:].bitcast(F32), ALU.subtract).then_inc(s_lo.sem, 1)

            def turned_low(l, j, g, bank, tiles, col):
                e.wait_ge(s_xh.sem, s_xh.at(l, 4 * j + g + 1))
                for n, k in enumerate(tiles):
                    r = e.scalar_tensor_tensor(out=XL[:, k, :], in0=PS[:, bank, n * SEQ:(n + 1) * SEQ], scalar=par[:, col + k:col + k + 1],
                                               in1=XH[:, k, :].bitcast(F32), op0=ALU.mult, op1=ALU.subtract)
                r.then_inc(s_xl.sem, 1)

            def norm(l, j, turn, col):
                e.wait_ge(s_rstd.sem, s_rstd.at(l, j + 1))
                for t in range(T):
                    e.tensor_scalar(xn[:, t, :], x[:, t, :], st[:, T_R + t:T_R + t + 1], None, ALU.mult).then_inc(s_xn.sem, 1)
                for g in range(4):
                    turned_low(l, turn, g, g, (2 * g, 2 * g + 1), col)

            def gate(l, q, pr):
                for t in range(T):
                    e.wait_ge(s_silu.sem, s_silu.at(l, 2 * q + t + 1))
                    e.tensor_tensor(hid[:, t, :], sg[:, t, :], PS[:, 4 + 2 * pr + t, 256:512], ALU.mult).then_inc(s_h.sem, 1)

            def ht_low(l, q, pr):
                e.wait_ge(s_hh.sem, s_hh.at(l, q + 1))
                e.tensor_tensor(HL[:].rearrange("p a b -> p (a b)"), PS[:, 4 + 2 * pr, :],
                                HH[:].bitcast(F32).rearrange("p a b -> p (a b)"), ALU.subtract).then_inc(s_hl.sem, 1)

            def update(l, slot, scale):
                e.wait_ge(s_used.sem, used(l, slot))
                for t in range(T):
                    for n in range(2):
                        xs = x[:, t, n * 512:(n + 1) * 512]
                        r = e.scalar_tensor_tensor(out=xs, in0=PS[:, t * 2 + n, :], scalar=scale, in1=xs, op0=ALU.mult, op1=ALU.add)
                    r.then_inc(s_x.sem, 1)

            def argument(l, n, bank, b, f):
                e.wait_ge(f_mm.sem, f_mm.at(l, n + 1))
                a, t = ARG[0:HYF], TURN[0:HYF]
                link(l, e.tensor_scalar(a, PS[0:HYF, bank, 0:SEQ], par[0:HYF, b:b + 1], par[0:HYF, f:f + 1], ALU.add, ALU.mult))
                link(l, e.tensor_scalar(t, a, 1 / (2 * math.pi), ROUND, ALU.mult, ALU.add))
                link(l, e.tensor_scalar(t, t, -ROUND, None, ALU.add))
                for c in (TWO_PI_A, TWO_PI_B, TWO_PI_C):
                    link(l, e.scalar_tensor_tensor(out=a, in0=t, scalar=-c, in1=a, op0=ALU.mult, op1=ALU.add))
                e.tensor_scalar(a, a, PI_F, -PI_F, ALU.min, ALU.max).then_inc(f_arg.sem, 1)

            def ffn(l, f, base, j, turn, col):
                lo(l, base); lo(l, base + 1)
                norm(l, j, turn, col)
                lo(l, base + 2); lo(l, base + 3)

                def chunk(c, pr, last=False):
                    q = f * CH + (c - 1)
                    gate(l, q, 1 - pr)
                    for d in (1, 2) if last else (1, 2, 3):
                        lo(l, base + 3 * c + d, pos(base + d))
                        if d == 1:
                            ht_low(l, q, 1 - pr)
                chunk(1, 1)
                if f == 0:
                    argument(l, 0, 5, C_FB1, C_FF1)
                with e.Fori(0, (CH - 3) // 2) as i:
                    chunk(i * 2 + 2, 0)
                    chunk(i * 2 + 3, 1)
                chunk(CH - 1, (CH - 1) % 2, last=True)
                if f == 0:
                    argument(l, 1, 7, C_FB2, C_FF2)
                gate(l, f * CH + CH - 1, (CH - 1) % 2)
                ht_low(l, f * CH + CH - 1, (CH - 1) % 2)
                if f == 0:
                    lo(l, S_G2); lo(l, S_G2 + 1)
                update(l, base + FFN_SLOTS - 1, 0.5)

            def taps(l, n, tile, bank, dst):
                e.wait_ge(c_base.sem, c_base.at(l, n))
                link(l, e.scalar_tensor_tensor(out=C[:, dst, 1:SEQ], in0=PS[:, bank, 0:SEQ - 1], scalar=par[:, C_W0 + tile:C_W0 + tile + 1],
                                               in1=C[:, dst, 1:SEQ], op0=ALU.mult, op1=ALU.add))
                e.scalar_tensor_tensor(out=C[:, dst, 0:SEQ - 1], in0=PS[:, bank, 1:SEQ], scalar=par[:, C_W2 + tile:C_W2 + tile + 1],
                                       in1=C[:, dst, 0:SEQ - 1], op0=ALU.mult, op1=ALU.add).then_inc(c_conv.sem, 1)

            def level_qk(l, b):
                e.wait_ge(g_e.sem, g_e.at(l, b + 1))
                if b >= 2:
                    e.wait_ge(g_ls.sem, g_ls.at(l, b))
                e.tensor_tensor(QKL[b % 2], QK, sg[:], ALU.mult).then_inc(g_lq.sem, 1)

            def level_keep(l, b):
                e.wait_ge(g_ls.sem, g_ls.at(l, b + 2))
                if b == 0:
                    e.wait_ge(g_la.sem, g_la.at(l, 1))
                hold(e, "dve")
                m = mask[:, b, :]
                m = bass.AP(m.tensor, m.offset, [m.ap[0], [0, H], [0, T], [1, P]])
                e.copy_predicated(AD, m, PS[:, 0:4, 0:256].rearrange("p h (t c) -> p h t c", t=T)).then_inc(g_la.sem, 1)

            def score_max(l, s):
                e.wait_ge(a_s.sem, a_s.at(l, s + 1))
                c = T_MX + 4 * s
                link(l, e.tensor_reduce(st[:, c:c + 4], PS[:, 4:6, :].rearrange("p b (h k) -> p (b h) k", h=2), AX.X, ALU.max))
                e.tensor_scalar(st[:, c:c + 4], st[:, c:c + 4], -MLA_SCALE, None, ALU.mult).then_inc(a_mx.sem, 1)

            def attended(l, s):
                e.wait_ge(a_o.sem, a_o.at(l, s + 1))
                a, b = T_RS + 4 * s, T_RR + 4 * s
                link(l, e.reciprocal(st[:, b:b + 4], st[:, a:a + 4]))
                r = st[:, b:b + 4]
                r = bass.AP(r.tensor, r.offset, [r.ap[0], [1, H], [0, DV]])
                e.tensor_tensor(xn[:, s, 256:768].rearrange("p (h d) -> p h d", h=H), PS[:, 4, :].rearrange("p (h d) -> p h d", h=H),
                                r, ALU.mult).then_inc(a_oe.sem, 1)

            def products(l, o):
                e.wait_ge(h_u.sem, h_u.at(l, o + 1))
                if o:
                    e.wait_ge(h_inv.sem, h_inv.at(l, o))
                c = slice(o * 256, (o + 1) * 256)
                ur = PS[:, 6, :].rearrange("p (m n) -> p m n", m=2)
                ui = PS[:, 7, :].rearrange("p (m n) -> p m n", m=2)
                e.tensor_tensor(Y[:, 0:2, :], ur, KA[:, :, c], ALU.mult)
                e.scalar_tensor_tensor(out=TT[:, 0:2, :], in0=ui, scalar=-1.0, in1=KI[:, :, c], op0=ALU.mult, op1=ALU.mult)
                e.tensor_tensor(Y[:, 2, :], ui[:, 0, :], KB[:, c], ALU.mult)
                e.tensor_tensor(Y[:, 3, :], ui[:, 1, :], KA[:, 1, c], ALU.mult)
                e.tensor_tensor(TT[:, 2:4, :], ur, KI[:, :, c], ALU.mult).then_inc(h_pr.sem, 1)

            def gated(l, o):
                e.wait_ge(h_inv.sem, h_inv.at(l, o + 1))
                dst = NV[:, 0] if o == 0 else xn[:, :, 0:256]
                e.tensor_tensor(dst, PS[:, 6, :].rearrange("p (t n) -> p t n", t=T), NV[:, 1 + o], ALU.mult).then_inc(h_z.sem, 1)

            e.wait_ge(s_in.sem, N_IN * 16)
            e.tensor_copy(mask[:].rearrange("p a b -> p (a b)"), scratch[:, MASK_AT:MASK_AT + (LEVELS - 1) * P])
            e.sem_inc(s_x.sem, 2)
            with e.Fori(0, DEPTH) as l:
                ffn(l, 0, 0, 0, 0, C_G1)
                for o in range(2):
                    for p in range(T):
                        e.wait_ge(f_w3.sem, f_w3.at(l, o * 2 + p + 1))
                        e.tensor_tensor(HW[:, o, p, :], PS[:, 4 + o * 2 + p, :], fil[:, F_WIN + p * 512:F_WIN + (p + 1) * 512], ALU.mult).then_inc(f_hw.sem, 1)
                norm(l, 1, 1, C_GM)
                lo(l, S_G3); lo(l, S_G3 + 1)
                taps(l, 1, 4, 4, 0); taps(l, 2, 5, 5, 1)
                lo(l, S_G1)
                lo(l, S_G1 + 1)
                e.wait_ge(s_used.sem, used(l, S_G3 + 1))
                e.wait_ge(q_r.sem, q_r.at(l))
                for t in range(T):
                    for n, (a, b) in enumerate(((0, 256), (256, 384))):
                        c = T_R4 + 2 * t + n
                        r = e.tensor_scalar(xn[:, t, 256 + a:256 + b], PS[:, 5 + t, a:b], st[:, c:c + 1], None, ALU.mult)
                r.then_inc(q_n.sem, 1)
                kr = PS[:, 5:7, 384:448]
                e.tensor_tensor(KT[:, 0], kr, rope[:, 0], ALU.mult)
                e.tensor_tensor(KT[:, 1, :, 0:32], kr[:, :, 32:64], rope[:, 1, :, 0:32], ALU.mult)
                e.tensor_tensor(KT[:, 1, :, 32:64], kr[:, :, 0:32], rope[:, 1, :, 32:64], ALU.mult).then_inc(q_kt.sem, 1)
                lo(l, S_UQN)
                e.wait_ge(g_z.sem, g_z.at(l))
                for d in range(2):
                    r = e.tensor_scalar(Z[:, 0, d, :], PS[:, 7, d * SEQ:(d + 1) * SEQ], par[:, C_BG + d:C_BG + d + 1], None, ALU.add)
                r.then_inc(g_az.sem, 1)
                e.memset(G[:, 2:4, :], 0.0)
                e.wait_ge(g_ln.sem, g_ln.at(l))
                link(l, e.tensor_scalar(Z[:, 0], Z[:, 0], 0.0, 1 / 16, ALU.min, ALU.mult))
                e.scalar_tensor_tensor(out=G[:, 1, :], in0=Z[:, 1, 0, :], scalar=-1 / 16, in1=Z[:, 0, 0, :], op0=ALU.mult, op1=ALU.add)
                e.scalar_tensor_tensor(out=G[:, 0, :], in0=Z[:, 1, 1, :], scalar=-1 / 16, in1=Z[:, 0, 1, :], op0=ALU.mult, op1=ALU.add).then_inc(g_g0.sem, 1)
                e.wait_ge(q_hi.sem, q_hi.at(l, 1))
                for n in range(2):
                    r = e.scalar_tensor_tensor(out=HL[:, n, :], in0=PS[:, 5, n * SEQ:(n + 1) * SEQ], scalar=par[:, C_QN + n:C_QN + n + 1],
                                               in1=HH[:, n, :].bitcast(F32), op0=ALU.mult, op1=ALU.subtract)
                r.then_inc(q_lo.sem, 1)
                e.wait_ge(q_hi.sem, q_hi.at(l, 2))
                e.scalar_tensor_tensor(out=KVL[:], in0=PS[:, 6, 0:SEQ], scalar=par[:, C_KVN:C_KVN + 1],
                                       in1=KVH[:].bitcast(F32), op0=ALU.mult, op1=ALU.subtract).then_inc(q_lo.sem, 1)
                lo(l, S_UQR)
                for n in range(4):
                    taps(l, 3 + n, n, n, n)
                lo(l, S_UKV)
                lo(l, S_G4)
                e.wait_ge(s_used.sem, used(l, S_UQR))
                q = PS[:, 2, :].rearrange("p (t h d) -> p t h d", t=T, h=H)

                def rp(n, a, b):
                    r = rope[:, n, :, a:b]
                    return bass.AP(r.tensor, r.offset, [r.ap[0], [DR, T], [0, H], [1, b - a]])
                t1 = TT[:, 0:2, :].rearrange("p t (h d) -> p t h d", h=H)
                t2 = TT[:, 2:4, :].rearrange("p t (h d) -> p t h d", h=H)
                e.tensor_tensor(t1, q, rp(0, 0, 64), ALU.mult)
                e.tensor_tensor(t2[:, :, :, 0:32], q[:, :, :, 32:64], rp(1, 0, 32), ALU.mult)
                e.tensor_tensor(t2[:, :, :, 32:64], q[:, :, :, 0:32], rp(1, 32, 64), ALU.mult).then_inc(a_qt.sem, 1)
                lo(l, S_G4 + 1)
                level_qk(l, 0)
                lo(l, S_WO)
                lo(l, S_WO + 1)
                lo(l, S_WO + 2)
                e.wait_ge(a_qr.sem, a_qr.at(l))
                products(l, 0)
                level_qk(l, 1)
                score_max(l, 0)
                gated(l, 0)
                level_keep(l, 0)
                level_qk(l, 2)
                level_keep(l, 1)
                level_qk(l, 3)
                attended(l, 0)
                products(l, 1)
                level_keep(l, 2)
                level_qk(l, 4)
                score_max(l, 1)
                level_keep(l, 3)
                level_qk(l, 5)
                gated(l, 1)
                level_keep(l, 4)
                level_qk(l, 6)
                level_keep(l, 5)
                level_qk(l, 7)
                attended(l, 1)
                level_keep(l, 6)
                e.wait_ge(h_r.sem, h_r.at(l))
                for t in range(T):
                    v = xn[:, t, 0:256]
                    r = e.tensor_scalar(v, v, st[:, T_RH + t:T_RH + t + 1], None, ALU.mult)
                r.then_inc(h_yy.sem, 1)
                e.wait_ge(a_r.sem, a_r.at(l))
                for t in range(T):
                    v = xn[:, t, 256:768]
                    r = e.tensor_scalar(v, v, st[:, T_RM + t:T_RM + t + 1], None, ALU.mult)
                r.then_inc(a_y.sem, 1)
                for g in range(2):
                    turned_low(l, 2, g, Y_BANKS[g], Y_TILES[g], C_GO)
                e.wait_ge(g_sq.sem, g_sq.at(l))
                e.tensor_reduce(st[:, T_S8:T_S8 + 8], sg[:].rearrange("p t (h d) -> p (t h) d", d=GDV), AX.X, ALU.add).then_inc(g_s8.sem, 1)
                e.wait_ge(g_r8.sem, g_r8.at(l))
                r8 = st[:, T_R8:T_R8 + 8]
                r8 = bass.AP(r8.tensor, r8.offset, [r8.ap[0], [1, 8], [0, GDV]])
                og = hid[:].rearrange("p t (h d) -> p (t h) d", d=GDV)
                link(l, e.tensor_tensor(og, PS[:, 7, :].rearrange("p (n d) -> p n d", d=GDV), r8, ALU.mult))
                e.wait_ge(g_r.sem, g_r.at(l))
                e.tensor_tensor(xn[:, :, 768:1024], hid[:], RG, ALU.mult).then_inc(g_y.sem, 1)
                lo(l, S_WO + 3)
                for g in range(2, 4):
                    turned_low(l, 2, g, Y_BANKS[g], Y_TILES[g], C_GO)
                update(l, S_WO + 3, 1.0)
                ffn(l, 1, FFN2, 2, 3, C_G2)
            e.wait_ge(s_in.sem, (N_IN + 1) * 16)
            e.wait_ge(s_rstd.sem, DEPTH * NORMS + 1)
            for t in range(T):
                e.scalar_tensor_tensor(out=xn[:, t, :], in0=x[:, t, :], scalar=st[:, T_R + t:T_R + t + 1], in1=C.rearrange("p a b -> p (a b)"),
                                       op0=ALU.mult, op1=ALU.mult).then_inc(s_xn.sem, 1)

        @block.tensor
        def _(e):
            e.sem_inc(s_used.sem, RING)
            e.wait_ge(s_in.sem, N_IN * 16)

            def passes(out, ah, al, bh, bl, start, stop):
                e.matmul(out, ah, bh, start=start, stop=False)
                e.matmul(out, ah, bl, start=False, stop=False)
                return e.matmul(out, al, bh, start=False, stop=stop)

            def turn_group(l, j, g, bank, tiles):
                for n, k in enumerate(tiles):
                    for t in range(T):
                        r = e.transpose(PS[:, bank, n * SEQ + t * P:n * SEQ + (t + 1) * P], xn[:, t, k * P:(k + 1) * P], ident)
                r.then_inc(s_tr.sem, 1)

            def norm(l, j, turn):
                e.wait_ge(s_xn.sem, s_xn.at(l, 2 * j + 2))
                for g in range(4):
                    turn_group(l, turn, g, g, (2 * g, 2 * g + 1))

            def x_tile(l, turn, k, first):
                if first and k % 2 == 0:
                    e.wait_ge(s_xl.sem, s_xl.at(l, 4 * turn + k // 2 + 1))

            def rows(l, turn, n, half, width, banks, inc=None):
                p = pos(n)
                e.wait_ge(s_lo.sem, s_lo.at(l, n + 1))
                for t in range(T):
                    for kk in range(4):
                        k = half * 4 + kk
                        x_tile(l, turn, k, t == 0)
                        r = passes(PS[:, banks[t], 0:width], XH[:, k, t * P:(t + 1) * P], XL[:, k, t * P:(t + 1) * P],
                                   WH[p][:, kk, 0:width], WL[p][:, kk, 0:width], k == 0, k == KD - 1)
                    if inc is not None and t == 0:
                        r.then_inc(inc.sem, 1)
                return r

            def columns(l, turn, n, half, tiles):
                p = pos(n)
                e.wait_ge(s_lo.sem, s_lo.at(l, n + 1))
                for kk in range(4):
                    k = half * 4 + kk
                    x_tile(l, turn, k, True)
                    for c, b in tiles:
                        r = passes(PS[:, b, 0:SEQ], WH[p][:, kk, c:c + P], WL[p][:, kk, c:c + P], XH[:, k, :], XL[:, k, :], k == 0, k == KD - 1)
                return r

            def turn_hidden(l, q, pr):
                e.wait_ge(s_h.sem, s_h.at(l, 2 * q + 2))
                for f in range(2):
                    for t in range(T):
                        r = e.transpose(PS[:, 4 + 2 * pr, f * SEQ + t * P:f * SEQ + (t + 1) * P], hid[:, t, f * P:(f + 1) * P], ident)
                r.then_inc(s_ht.sem, 1)

            def down(l, n, p, q, first, last):
                e.wait_ge(s_lo.sem, s_lo.at(l, n + 1))
                e.wait_ge(s_hl.sem, s_hl.at(l, q + 1))
                for t in range(T):
                    for f in range(2):
                        for m in range(2):
                            r = passes(PS[:, t * 2 + m, :], HH[:, f, t * P:(t + 1) * P], HL[:, f, t * P:(t + 1) * P],
                                       WH[p][:, f * 2 + m, :], WL[p][:, f * 2 + m, :], first and f == 0, last and f == 1)
                r.then_inc(s_used.sem, 1)

            def gate_up(l, turn, n, p, half, pr, first):
                e.wait_ge(s_lo.sem, s_lo.at(l, n + 1))
                for t in range(T):
                    for kk in range(4):
                        k = half * 4 + kk
                        if first:
                            x_tile(l, turn, k, t == 0)
                        r = passes(PS[:, 4 + 2 * pr + t, :], XH[:, k, t * P:(t + 1) * P], XL[:, k, t * P:(t + 1) * P],
                                   WH[p][:, kk, :], WL[p][:, kk, :], k == 0, k == KD - 1)
                    if half == 1 and t == 0:
                        r.then_inc(s_gu.sem, 1)
                r.then_inc(s_used.sem, 1)

            def filter_mm(l, n, w, src, rows_, bank):
                if n == 0:
                    e.wait_ge(s_fil.sem, s_fil.at(l, 32))
                else:
                    e.wait_ge(f_sin.sem, f_sin.at(l, n))
                hold(e, "pe")
                e.matmul(PS[0:HYF, bank, 0:SEQ], fil[0:rows_, w:w + HYF], src[0:rows_], start=True, stop=True).then_inc(f_mm.sem, 1)

            def ffn(l, f, base, j, turn):
                norm(l, j, turn)
                gate_up(l, turn, base, pos(base), 0, 0, True)
                gate_up(l, turn, base + 1, pos(base + 1), 1, 0, True)

                def chunk(c, pr, first=False):
                    q = f * CH + (c - 1)
                    if not first:
                        e.wait_ge(s_hl.sem, s_hl.at(l, q))
                    gate_up(l, turn, base + 3 * c - 1, pos(base + 2), 0, pr, False)
                    turn_hidden(l, q, 1 - pr)
                    if f == 0 and first:
                        filter_mm(l, 0, F_W1, fil[:, F_Z:F_Z + SEQ], HYE, 5)
                    gate_up(l, turn, base + 3 * c, pos(base), 1, pr, False)
                    down(l, base + 3 * c + 1, pos(base + 1), q, first, False)
                chunk(1, 1, True)
                if f == 0:
                    e.wait_ge(f_arg.sem, f_arg.at(l, 1))
                    hold(e, "pe")
                with e.Fori(0, (CH - 3) // 2) as i:
                    chunk(i * 2 + 2, 0)
                    chunk(i * 2 + 3, 1)
                chunk(CH - 1, (CH - 1) % 2)
                if f == 0:
                    filter_mm(l, 1, F_W2, H1, HYF, 7)
                turn_hidden(l, f * CH + CH - 1, (CH - 1) % 2)
                down(l, base + FFN_SLOTS - 1, pos(base + FFN_SLOTS - 1), f * CH + CH - 1, False, True)

            def level_scores(l, b):
                if b >= 0:
                    e.wait_ge(g_lq.sem, g_lq.at(l, b + 1))
                    e.wait_ge(g_la.sem, g_la.at(l, b + 1))
                qk = QK if b < 0 else QKL[b % 2]
                for t in range(T):
                    o = t if b < LEVELS - 1 else 1 - t
                    for h in range(H):
                        r = e.matmul(PS[:, h, t * P:(t + 1) * P], qk[32 * h:32 * h + 32, 1, t * P:(t + 1) * P],
                                     qk[32 * h:32 * h + 32, 0, o * P:(o + 1) * P], start=True, stop=True)
                r.then_inc(g_ls.sem, 1)

            def hy_dft(l, o):
                for part in range(2):
                    for m in range(2):
                        for p in range(T):
                            r = e.matmul(PS[:, 6 + part, m * 256:(m + 1) * 256], dft[:, p, part * 256 + m * P:part * 256 + (m + 1) * P],
                                         NV[:, 0, p, :], start=(p == 0), stop=(p == T - 1))
                r.then_inc(h_u.sem, 1)

            def hy_inverse(l, o):
                e.wait_ge(h_y.sem, h_y.at(l, o + 1))
                for t in range(T):
                    for m in range(4):
                        r = e.matmul(PS[:, 6, t * 256:(t + 1) * 256], idft[:, m, t * P:(t + 1) * P], Y[:, m, :], start=(m == 0), stop=(m == 3))
                r.then_inc(h_inv.sem, 1)

            def scores(l, s):
                for h in range(H):
                    out = PS[:, 4 + h // 2, (h % 2) * SEQ:(h % 2 + 1) * SEQ]
                    e.matmul(out, QN[:, h, s * P:(s + 1) * P], KN[:, h, :], start=True, stop=False)
                    r = e.matmul(out, QR[0:DR, h, s * P:(s + 1) * P], KR[0:DR, :], start=False, stop=True)
                r.then_inc(a_s.sem, 1)

            def turn_probs(l, s):
                e.wait_ge(a_p.sem, a_p.at(l, s + 1))
                for k in range(T):
                    for h in range(H):
                        r = e.transpose(PS[:, 4 + k, h * P:(h + 1) * P], PE_[:, h, k * P:(k + 1) * P], ident)
                r.then_inc(a_pt.sem, 1)

            def attend(l, s):
                e.wait_ge(a_pte.sem, a_pte.at(l, s + 1))
                for h in range(H):
                    for k in range(T):
                        r = e.matmul(PS[:, 4, h * P:(h + 1) * P], PT[:, k, h, :], VM[:, k, h * P:(h + 1) * P], start=(k == 0), stop=(k == T - 1))
                r.then_inc(a_o.sem, 1)

            def turn_conv(l, dst, bank):
                for t in range(T):
                    for j in range(2):
                        r = e.transpose(PS[:, bank, t * 256 + j * P:t * 256 + (j + 1) * P], C[:, dst + j, t * P:(t + 1) * P], ident)
                r.then_inc(c_tr.sem, 1)

            with e.Fori(0, DEPTH) as l:
                ffn(l, 0, 0, 0, 0)
                e.wait_ge(f_sin.sem, f_sin.at(l, 2))
                for o in range(2):
                    for p in range(T):
                        e.matmul(PS[:, 4 + 2 * o + p, :], H2[0:HYF, p * P:(p + 1) * P], fil[0:HYF, F_W3 + o * 512:F_W3 + (o + 1) * 512],
                                 start=True, stop=True).then_inc(f_w3.sem, 1)
                norm(l, 1, 1)
                e.wait_ge(f_hw.sem, f_hw.at(l, 4))
                g2 = [(0, 4), (128, 5), (256, 6), (384, 7)]
                for i in range(2):
                    columns(l, 1, S_G2 + i, i, g2).then_inc(s_used.sem, 1)
                e.wait_ge(f_hs.sem, f_hs.at(l))
                for m in range(2):
                    for p in range(T):
                        r = e.matmul(PS[:, m, :], dft[:, p, m * P:(m + 1) * P], HS[:, p, :], start=(p == 0), stop=(p == T - 1))
                    r.then_inc(k_mm.sem, 1)
                for m in range(2):
                    for p in range(T):
                        r = e.matmul(PS[:, 2 + m, :], fil[:, F_DFT + p * 384 + m * P:F_DFT + p * 384 + (m + 1) * P], HD[:, p, :], start=(p == 0), stop=(p == T - 1))
                    r.then_inc(k_mm.sem, 1)
                e.wait_ge(c_conv.sem, c_conv.at(l, 2))
                e.wait_ge(g_qk.sem, g_qk.at(l))
                for i in range(2):
                    rows(l, 1, S_G3 + i, i, 448, (5, 6))
                    columns(l, 1, S_G3 + i, i, [(384, 4)]).then_inc(s_used.sem, 1)
                for p in range(T):
                    r = e.matmul(PS[:, 7, :], fil[:, F_DFT + p * 384 + 256:F_DFT + p * 384 + 384], HS[:, p, :], start=(p == 0), stop=(p == T - 1))
                r.then_inc(k_mm.sem, 1)
                e.wait_ge(g_in.sem, g_in.at(l))
                turn_conv(l, 0, 4)
                e.wait_ge(k_ev.sem, k_ev.at(l, 5))
                for d in range(2):
                    r = e.matmul(PS[:, 7, d * SEQ:(d + 1) * SEQ], wg[64:96, d, :], hid[64:96, 0, :], start=True, stop=True)
                r.then_inc(g_z.sem, 1)
                for i in range(2):
                    columns(l, 1, S_G1 + i, i, [(128 * n, n) for n in range(4)]).then_inc(s_used.sem, 1)
                e.wait_ge(q_n.sem, q_n.at(l))
                e.wait_ge(q_kr.sem, q_kr.at(l))
                for n in range(2):
                    for t in range(T):
                        r = e.transpose(PS[:, 5, n * SEQ + t * P:n * SEQ + (t + 1) * P], xn[:, t, 256 + n * P:256 + (n + 1) * P], ident)
                r.then_inc(q_tr.sem, 1)
                for t in range(T):
                    e.transpose(PS[:, 6, t * P:(t + 1) * P], xn[:, t, 512:640], ident)
                    r = e.transpose(PS[0:DR, 6, SEQ + t * P:SEQ + (t + 1) * P], xn[:, t, 640:704], ident)
                r.then_inc(q_tr.sem, 1)
                e.wait_ge(c_nat.sem, c_nat.at(l, 1))
                e.wait_ge(c_conv.sem, c_conv.at(l, 4))
                turn_conv(l, 0, 4)
                e.wait_ge(g_az.sem, g_az.at(l))
                e.wait_ge(c_conv.sem, c_conv.at(l, 6))
                turn_conv(l, 2, 7)
                e.wait_ge(s_lo.sem, s_lo.at(l, S_UQN + 1))
                e.wait_ge(q_lo.sem, q_lo.at(l, 2))
                p = pos(S_UQN)
                for h in range(H):
                    for k in range(2):
                        r = passes(PS[:, h // 2, (h % 2) * SEQ:(h % 2 + 1) * SEQ], WH[p][:, k, h * P:(h + 1) * P], WL[p][:, k, h * P:(h + 1) * P],
                                   HH[:, k, :], HL[:, k, :], k == 0, k == 1)
                r.then_inc(s_used.sem, 1)
                e.wait_ge(s_lo.sem, s_lo.at(l, S_UQR + 1))
                p = pos(S_UQR)
                for t in range(T):
                    for k in range(2):
                        r = passes(PS[:, 2, t * 256:(t + 1) * 256], HH[:, k, t * P:(t + 1) * P], HL[:, k, t * P:(t + 1) * P],
                                   WH[p][:, k, 0:256], WL[p][:, k, 0:256], k == 0, k == 1)
                r.then_inc(s_used.sem, 1)
                e.wait_ge(s_lo.sem, s_lo.at(l, S_UKV + 1))
                p = pos(S_UKV)
                for h in range(H):
                    passes(PS[:, 5 + h // 2, (h % 2) * SEQ:(h % 2 + 1) * SEQ], WH[p][:, 0, h * P:(h + 1) * P], WL[p][:, 0, h * P:(h + 1) * P],
                           KVH[:], KVL[:], True, True)
                for t, b in ((0, 3), (1, 0)):
                    if t:
                        e.wait_ge(a_qn.sem, a_qn.at(l, 1))
                    r = passes(PS[:, b, :], KVH[:, t * P:(t + 1) * P], KVL[:, t * P:(t + 1) * P], WH[p][:, 1, :], WL[p][:, 1, :], True, True)
                r.then_inc(s_used.sem, 1)
                e.wait_ge(c_nat.sem, c_nat.at(l, 2))
                e.wait_ge(a_kn.sem, a_kn.at(l, 1))
                for i in range(2):
                    rows(l, 1, S_G4 + i, i, 512, (4, 5)).then_inc(s_used.sem, 1)
                e.wait_ge(a_kn.sem, a_kn.at(l, 2))
                e.wait_ge(c_nat.sem, c_nat.at(l, 3))
                hy_dft(l, 0)
                e.wait_ge(a_qr.sem, a_qr.at(l))
                e.wait_ge(a_qn.sem, a_qn.at(l, 2))
                hold(e, "pe")
                for h in range(H):
                    for t in range(T):
                        r = e.transpose(PS[0:DR, 1 + h // 2, (h % 2) * SEQ + t * P:(h % 2) * SEQ + (t + 1) * P],
                                        xn[:, t, 768 + h * DR:768 + (h + 1) * DR], ident)
                r.then_inc(a_qtr.sem, 1)
                e.wait_ge(a_qre.sem, a_qre.at(l, 2))
                e.wait_ge(a_v.sem, a_v.at(l, 2))
                level_scores(l, -1)
                e.wait_ge(g_vr.sem, g_vr.at(l, 2))
                scores(l, 0)
                hy_inverse(l, 0)
                level_scores(l, 0)
                turn_probs(l, 0)
                level_scores(l, 1)
                attend(l, 0)
                e.wait_ge(h_z.sem, h_z.at(l, 1))
                hy_dft(l, 1)
                level_scores(l, 2)
                e.wait_ge(a_oe.sem, a_oe.at(l, 1))
                scores(l, 1)
                level_scores(l, 3)
                hy_inverse(l, 1)
                level_scores(l, 4)
                turn_probs(l, 1)
                level_scores(l, 5)
                attend(l, 1)
                level_scores(l, 6)
                level_scores(l, 7)
                e.wait_ge(g_la.sem, g_la.at(l, LEVELS + 1))
                for s in range(T):
                    for h in range(H):
                        for t in range(T):
                            a = AD[:, h, s, :] if t == s else AC[:, h, t, :]
                            r = e.matmul(PS[:, 7, s * 256 + h * GDV:s * 256 + (h + 1) * GDV], a, VG[:, t, h * GDV:(h + 1) * GDV],
                                         start=(t == 0), stop=(t == T - 1))
                r.then_inc(g_o.sem, 1)
                e.wait_ge(a_y.sem, a_y.at(l))
                for g in range(2):
                    turn_group(l, 2, g, Y_BANKS[g], Y_TILES[g])
                e.wait_ge(h_yy.sem, h_yy.at(l))
                turn_group(l, 2, 2, Y_BANKS[2], Y_TILES[2])
                for g in range(4):
                    if g == 2:
                        e.wait_ge(g_y.sem, g_y.at(l))
                        turn_group(l, 2, 3, Y_BANKS[3], Y_TILES[3])
                    n = S_WO + g
                    p = pos(n)
                    e.wait_ge(s_lo.sem, s_lo.at(l, n + 1))
                    e.wait_ge(s_xl.sem, s_xl.at(l, 8 + g + 1))
                    for t in range(T):
                        for i, k in enumerate(Y_TILES[g]):
                            for m in range(2):
                                r = passes(PS[:, t * 2 + m, :], XH[:, k, t * P:(t + 1) * P], XL[:, k, t * P:(t + 1) * P],
                                           WH[p][:, 2 * i + m, :], WL[p][:, 2 * i + m, :], g == 0 and i == 0, g == 3 and i == 1)
                    r.then_inc(s_used.sem, 1)
                ffn(l, 1, FFN2, 2, 3)
        assert linked == LINKS, linked


N_IN = 7


def ffn_slots(gate, up, down):
    out, last = [], None
    for c in range(CH):
        at = slice(c * 256, (c + 1) * 256)
        for half in range(2):
            r = slice(half * 512, (half + 1) * 512)
            a = np.stack([gate[r, at].reshape(4, P, 256), up[r, at].reshape(4, P, 256)], 2)
            out.append(a.transpose(1, 0, 2, 3).reshape(P, SLOT))
        if last is not None:
            out.append(last)
        last = down[at].reshape(2, P, D).transpose(1, 0, 2).reshape(P, SLOT)
    return out + [last]


def mix_slots(w_in, w_uq, w_ukv, w_out):
    def two(cols):
        w = np.zeros((D, 512), np.float32)
        at = 0
        for a, b in cols:
            w[:, at:at + b - a] = w_in[:, a:b]
            at += b - a
        w = w.reshape(2, 4, P, 512).transpose(0, 2, 1, 3)
        return [w[0].reshape(P, SLOT), w[1].reshape(P, SLOT)]

    def one(parts):
        w = np.zeros((P, 4, 512), np.float32)
        for n, a in enumerate(parts):
            w[:, n, :a.shape[1]] = a
        return [w.reshape(P, SLOT)]
    out = two([(512, 768), (1216, 1472)])
    out += two([(768, 1216), (1728, 1760)])
    out += two([(0, 512)])
    uq = w_uq.reshape(2, P, H, DN + DR)
    out += one([uq[k, :, :, :DN].reshape(P, H * DN) for k in range(2)])
    out += one([uq[k, :, :, DN:].reshape(P, H * DR) for k in range(2)])
    ukv = w_ukv.reshape(P, H, DN + DV)
    out += one([ukv[:, :, :DN].reshape(P, 512), ukv[:, :, DN:].reshape(P, 512)])
    out += two([(1472, 1728), (1760, 2016)])
    for ks in Y_TILES:
        out.append(np.stack([w_out[k * P:(k + 1) * P] for k in ks], 1).reshape(P, SLOT))
    return out


def shape_constants():
    f32 = np.float32
    f = np.arange(256)
    ang = 2 * np.pi / 512 * ((f[:, None] * f[None, :]) % 512)
    cos, sin = np.cos(ang), np.sin(ang)
    nyq = 1.0 - 2.0 * (f % 2)
    sin_n, cos_n = -sin, cos[:, :P].copy()
    sin_n[:, 0], cos_n[:, 0] = nyq, nyq
    dft = np.concatenate([cos, sin_n], 1).reshape(T, P, 512).transpose(1, 0, 2).reshape(P, 1024)
    w = np.where(f == 0, 1.0, 2.0)[:, None] / 512
    inv_im = -w * sin
    inv_im[0] = nyq / 512
    inv = np.concatenate([w * cos, inv_im]).reshape(4, P, SEQ).transpose(1, 0, 2).reshape(P, 1024)
    fil_dft = np.concatenate([-sin, cos_n], 1).reshape(T, P, 384).transpose(1, 0, 2).reshape(P, 768)

    p = np.arange(SEQ, dtype=f32)
    t = p / f32(SEQ - 1)
    bands = np.linspace(1e-4, 15, 16, dtype=f32)
    a = (f32(2 * math.pi) * p / f32(SEQ))[:, None] * bands[None, :]
    z = np.concatenate([t[:, None], np.cos(a), -np.sin(a)], -1)
    lo_, hi_ = math.log(1e-2) / 1.5, math.log(1e-2) / 0.3
    win = np.exp(-t[:, None] * np.abs(np.linspace(lo_, hi_, HYW, dtype=f32))[None, :])
    win_b = win.copy()
    win_b[0] = 0
    win = np.concatenate([win, win_b], 1).reshape(T, P, 512).transpose(1, 0, 2).reshape(P, 1024)

    inv_f = f32(10000.0) ** (-np.arange(32, dtype=f32) * f32(2.0) / f32(DR))
    a = p[:, None] * inv_f[None, :].astype(f32)
    rope = np.stack([np.concatenate([np.cos(a)] * 2, 1), np.concatenate([-np.sin(a), np.sin(a)], 1)])
    rope = rope.reshape(2, T, P, DR).transpose(2, 0, 1, 3).reshape(P, 2 * T * DR)

    i = np.arange(P)
    mask = np.stack([(i[:, None] >> (b + 1) == i[None, :] >> (b + 1)) & (i[:, None] >> b != i[None, :] >> b)
                     for b in range(LEVELS - 1)], 1).reshape(P, -1)

    cst = np.zeros((P, NCST), f32)
    cst[:, :P] = np.eye(P)
    cst[:, I_D:I_CQ] = 1 / D
    cst[:, I_CQ:I_M] = [1 / 256, 1 / 128, 1 / 256, 1 / 128]
    cst[:, I_M:I_H] = 1 / 512
    cst[:, I_H:I_G] = 1 / 256
    cst[:, I_G:I_EPS] = 1 / 64
    cst[:, I_EPS:I_POW] = EPS
    cst[:, I_POW:] = -0.5
    dft = np.concatenate([dft, inv], 1)
    return {n: a.astype(f32) for n, a in dict(cst=cst, dft=dft, rope=rope, win=win, z=z.T, fil_dft=fil_dft, mask=mask).items()}


def kernel(**inputs):
    import concourse.bacc as _bacc
    from concourse import mybir as _mybir
    from concourse.bass_utils import run_bass_kernel_spmd as _run

    a = {k: np.asarray(v) for k, v in inputs.items()}
    k = shape_constants()
    f32 = np.float32
    slots, par = [], np.zeros((P, DEPTH, NPAR), f32)
    fil, gates = np.zeros((DEPTH, P, NFIL), f32), np.zeros((DEPTH, 32, 2 * P), f32)
    for l in range(DEPTH):
        slots += ffn_slots(a["ffn1_w_gate"][l], a["ffn1_w_up"][l], a["ffn1_w_down"][l])
        slots += mix_slots(a["w_in"][l], a["mla_w_uq"][l], a["mla_w_ukv"][l], a["w_out"][l])
        slots += ffn_slots(a["ffn2_w_gate"][l], a["ffn2_w_up"][l], a["ffn2_w_down"][l])

        def tiles(v):
            return v.reshape(-1, P).T
        q = par[:, l]
        q[:, C_G1:C_GM] = tiles(a["ffn1_norm"][l])
        q[:, C_GM:C_G2] = tiles(a["mix_norm"][l])
        q[:, C_G2:C_QN] = tiles(a["ffn2_norm"][l])
        q[:, C_QN:C_KVN] = tiles(a["mla_q_norm"][l])
        q[:, C_KVN:C_GO] = tiles(a["mla_kv_norm"][l])
        q[:, C_GO:C_W0] = tiles(np.concatenate([a["hy_out_norm"][l], a["mla_out_norm"][l]] + [a["gla_head_norm"][l]] * 4))
        for n, c in enumerate((C_W0, C_W1, C_W2)):
            q[:, c:c + 6] = tiles(a["hy_conv_w"][l, n])
        q[:, C_CB:C_BG] = tiles(a["hy_conv_b"][l])
        q[:, C_BG] = a["gla_b_gate_fwd"][l]
        q[:, C_BG + 1] = a["gla_b_gate_bwd"][l]
        for c, n in ((C_FB1, "b1"), (C_FF1, "freq1"), (C_FB2, "b2"), (C_FF2, "freq2")):
            q[:HYF, c] = a["hy_filt_" + n][l]
        g = fil[l]
        g[:, F_WIN:F_Z] = k["win"]
        g[:HYE, F_Z:F_W1] = k["z"]
        g[:HYE, F_W1:F_W2] = a["hy_filt_w1"][l]
        g[:HYF, F_W2:F_W3] = a["hy_filt_w2"][l]
        g[:HYF, F_W3:F_DFT] = a["hy_filt_w3"][l]
        g[:, F_DFT:F_SKIP] = k["fil_dft"]
        g[0, F_SKIP:] = a["hy_skip"][l].reshape(-1)
        gates[l, 0:16, 0:P] = a["gla_w_gate_fwd"][l]
        gates[l, 16:32, P:] = a["gla_w_gate_bwd"][l]
    arrays = {"x": a["x"][0], "w": np.stack(slots), "par": par.reshape(P, -1), "cst": k["cst"], "fil": fil, "gates": gates,
              "dft": k["dft"], "rope": k["rope"], "mask": k["mask"], "fin": a["final_norm"]}
    arrays = {f"in_{n}_dram": np.ascontiguousarray(v) for n, v in arrays.items()}
    nc = _bacc.Bacc("TRN2", target_bir_lowering=False, num_devices=1)
    args = [nc.dram_tensor(n, v.shape, _mybir.dt.from_np(v.dtype), kind="ExternalInput").ap() for n, v in arrays.items()]
    args.append(nc.dram_tensor("out_0_dram", (SEQ, D), F32, kind="ExternalOutput").ap())
    build(nc, *args)
    r = _run(nc, [arrays], core_ids=[0])
    return r.results[0]["out_0_dram"].reshape(1, SEQ, D)
```

```python
from contextlib import ExitStack
import math

import numpy as np
import concourse.bass as bass
from concourse import mybir

F32 = mybir.dt.float32
F32R = mybir.dt.float32r
U8 = mybir.dt.uint8
ACT = mybir.ActivationFunctionType
ALU = mybir.AluOpType
AX = mybir.AxisListType

P = 128
SEQ, D, FF, DEPTH = 256, 1024, 2816, 2
T = SEQ // P
KD = D // P
CH = FF // 256
RING = 3
SLOT = 4 * 512
FFN_SLOTS = 3 * CH
MIX = FFN_SLOTS
MIX_SLOTS = 15
FFN2 = MIX + MIX_SLOTS
SLOTS = FFN2 + FFN_SLOTS
S_G3, S_G2, S_G1, S_G4, S_UQN, S_UQR, S_UKV, S_WO = (MIX + n for n in (0, 2, 4, 6, 8, 9, 10, 11))
assert SLOTS % RING == 0 and CH % 2 == 1

HYW, HYE, HYF = 256, 33, 64
H, DN, DR, DV = 4, 128, 64, 128
GDK, GDV = 32, 64
LEVELS = 8
EPS = 1e-6
MLA_SCALE = float(DN + DR) ** -0.5

(C_G1, C_GM, C_G2, C_QN, C_KVN, C_GO, C_W0, C_W1, C_W2, C_CB, C_BG, C_FB1, C_FF1, C_FB2, C_FF2,
 NPAR) = np.cumsum([0, 8, 8, 8, 2, 1, 8, 6, 6, 6, 6, 2, 1, 1, 1, 1]).tolist()
I_D, I_CQ, I_M, I_H, I_G, I_EPS, I_POW, NCST = (128 + np.cumsum([0, 2, 4, 2, 2, 8, 8, 8])).tolist()
F_WIN, F_Z, F_W1, F_W2, F_W3, F_DFT, F_SKIP, NFIL = np.cumsum([0, 1024, 256, 64, 64, 1024, 768, 512]).tolist()
T_SS, T_R, T_S4, T_R4, T_SM, T_RM, T_SH, T_RH, T_S8, T_R8, T_MX, T_RS, T_RR, NST = np.cumsum(
    [0, 4, 2, 4, 4, 2, 2, 2, 2, 8, 8, 8, 8, 8]).tolist()
TWO_PI_A, TWO_PI_B = 6.28125, 2029.0 / 2 ** 20
TWO_PI_C = 2 * math.pi - TWO_PI_A - TWO_PI_B
ROUND = 1.5 * 2 ** 23
PI_F = 3.1415925
Y_TILES = [(2, 3), (4, 5), (0, 1), (6, 7)]
Y_BANKS = [4, 5, 6, 4]
NORMS = 3
TURNS = 4
LINKS = {"dve": 24, "pool": 43, "act": 2}


class Mark:

    def __init__(self, sem, per):
        self.sem, self.per = sem, per

    def at(self, l, v=1):
        return l * self.per + v


def pos(n):
    return (n + 1) % RING


def build(nc, x_d, w_d, par_d, cst_d, fil_d, gate_d, dft_d, rope_d, mask_d, fin_d, out_d):
    with ExitStack() as ctx:
        def sb(name, shape, dt=F32):
            return ctx.enter_context(nc.sbuf_tensor(name, shape, dt))

        def mark(name, per):
            return Mark(ctx.enter_context(nc.semaphore(name)), per)

        raw = [sb(f"w_raw{i}", [P, 4, 512]) for i in range(RING)]
        WH = [sb(f"w_high{i}", [P, 4, 512], F32R) for i in range(RING)]
        WL = [sb(f"w_low{i}", [P, 4, 512], F32R) for i in range(RING)]
        x = sb("x", [P, T, D])
        xn = sb("x_normed", [P, T, D])
        XH = sb("xT_high", [P, KD, SEQ], F32R)
        XL = sb("xT_low", [P, KD, SEQ], F32R)
        sg = sb("silu_gate", [P, 2, SEQ])
        hid = sb("hidden", [P, 2, SEQ])
        HHB = [sb(f"hT_high{i}", [P, 2, SEQ], F32R) for i in range(2)]
        HLB = [sb(f"hT_low{i}", [P, 2, SEQ], F32R) for i in range(2)]
        HH, HL = HHB[0], HLB[0]
        diag = sb("diag_rstd", [P, T, P])
        KVH = sb("kvT_high", [P, SEQ], F32R)
        KVL = sb("kvT_low", [P, SEQ], F32R)
        par_next = sb("par_next", [P, DEPTH, NPAR])
        par = sb("par", [P, NPAR])
        cst = sb("constants", [P, NCST])
        ident = cst[:, 0:P]
        st = sb("statistics", [P, NST])
        dft = sb("dft", [P, T, 512])
        idft = sb("inverse_dft", [P, 4, SEQ])
        rope = sb("rope", [P, 2, T, DR])
        mask = sb("level_masks", [P, LEVELS - 1, P], U8)
        wg = sb("gate_weights", [P, 2, P])
        KA = sb("filter_re", [P, 2, 512])
        KI = sb("filter_im", [P, 2, 512])
        KB = sb("filter_nyquist", [P, 512])
        scratch = sb("mixer_scratch", [P, 16896])
        cols = [0]

        def view(*dims, at=None):
            n = int(np.prod(dims))
            a = cols[0] if at is None else at
            if at is None:
                cols[0] += n
            v = scratch[:, a:a + n]
            if len(dims) == 2:
                v = v.rearrange("p (a b) -> p a b", b=dims[1])
            if len(dims) == 3:
                v = v.rearrange("p (a b c) -> p a b c", b=dims[1], c=dims[2])
            return v

        QN, QR, KN = view(H, SEQ), view(H, SEQ), view(H, SEQ)
        VM = view(T, H * DV)
        PE_ = view(H, SEQ)
        PT = view(2, H, P)
        AD = view(H, T, P)
        AC = view(H, T, P)
        Y = view(4, SEQ)
        TT = view(4, SEQ)
        filter_cols = cols[0]
        KR = view(SEQ)
        QK = view(2, SEQ)
        G = view(4, SEQ)
        Z = scratch[:, cols[0]:cols[0] + 4 * SEQ].rearrange("p (a b c) -> p a b c", a=2, b=2)
        QKL = [view(2, SEQ), view(2, SEQ)]
        VG, RG = view(T, 256), view(T, 256)
        C = view(4, SEQ)
        NV = view(3, T, 256)
        KT = view(2, T, DR)
        assert cols[0] <= 16896, cols[0]
        fil = scratch[:, 0:NFIL]
        at = NFIL
        H1, H2 = view(SEQ, at=at), view(SEQ, at=at + SEQ)
        ARG, TURN = view(SEQ, at=at + 2 * SEQ), view(SEQ, at=at + 3 * SEQ)
        HW = view(2, T, 512, at=at + 4 * SEQ)
        HS = view(T, 512, at=at + 4 * SEQ + 2048)
        HD = view(T, 512, at=at + 4 * SEQ + 3072)
        assert at + 4 * SEQ + 4096 <= filter_cols

        PS = ctx.enter_context(nc.psum_tensor("psum", [P, 8, 512], F32))

        s_in0, s_in1, s_cst, s_in = (mark(n, 0) for n in ("x_first_half", "x_second_half", "params_landed", "constants_landed"))
        landed = [mark(f"slot_landed{i}", SLOTS // RING * 16) for i in range(RING)]
        s_hi, s_lo, s_used = mark("slot_high", SLOTS), mark("slot_low", SLOTS), mark("slot_used", SLOTS)
        s_par, s_mask = mark("params_copied", 1), mark("masks_made", 0)
        s_fil1, s_fil = mark("filter_mlp_landed", 16), mark("filter_pack_landed", 64)
        s_x = mark("x_updated", 4 * NORMS)
        s_ss, s_rstd, s_dg = mark("squares_summed", 4 * NORMS), mark("rstd", NORMS), mark("rstd_diagonal", 2 * NORMS)
        s_d0 = mark("first_tokens_summed", 2)
        s_tr, s_xh, s_xl = (mark(n, 4 * TURNS) for n in ("turned", "turned_high", "turned_low"))
        s_silu, s_h, s_hh, s_hl = (mark(n, 4 * CH) for n in ("silu", "hidden_done", "hT_high_done", "hT_low_done"))
        s_y, s_out = mark("final_normed", 0), mark("out_landed", 0)
        f_mm, f_arg, f_sin = mark("filter_mm", 2), mark("sine_argument", 2), mark("sine", 2)
        f_w3, f_hw, f_hs = mark("filter_taps", 4), mark("taps_windowed", 4), mark("taps_summed", 1)
        k_mm, k_ev = mark("filter_dft", 5), mark("filter_dft_copied", 5)
        c_base, c_conv, c_tr, c_nat = mark("conv_centre", 6), mark("conv_done", 6), mark("conv_turned", 3), mark("conv_natural", 3)
        g_qk, g_in, g_z, g_az = mark("gla_qk", 1), mark("gate_in", 1), mark("gate_mm", 1), mark("gate_logits", 1)
        g_ln, g_g0 = mark("gate_log", 1), mark("gate_exponents", 1)
        g_e, g_lq, g_gu = mark("level_exp", LEVELS), mark("level_qk", LEVELS), mark("level_exponents", LEVELS - 1)
        g_ls, g_la = mark("level_scores", LEVELS + 1), mark("level_scores_kept", LEVELS + 1)
        g_vr = mark("gla_vr", 2)
        g_o, g_sq, g_s8, g_r8, g_y, g_r = (mark(n, 1) for n in ("gla_out", "gla_squares", "gla_sums", "gla_rstd", "gla_y", "gla_silu"))
        q_ss, q_r, q_n, q_kt, q_kr = (mark(n, 1) for n in ("latent_squares", "latent_rstd", "latent_normed", "k_rope_products", "k_rope"))
        q_tr, q_hi, q_lo, q_krt = mark("latent_turned", 2), mark("latent_high", 2), mark("latent_low", 2), mark("k_rope_turned_copied", 1)
        a_qn, a_qt, a_qr, a_qtr, a_qre = mark("q_copied", 2), mark("q_rope_products", 1), mark("q_rope", 1), mark("q_rope_turned", 1), mark("q_rope_copied", 2)
        a_kn, a_v = mark("k_copied", 2), mark("v_copied", 2)
        a_s, a_mx, a_p, a_pt, a_pte = (mark(n, 2) for n in ("scores", "score_max", "probs", "probs_turned", "probs_turned_copied"))
        a_o, a_oe = mark("attended", 2), mark("attended_scaled", 2)
        a_sq, a_r, a_y = mark("mla_squares", 2), mark("mla_rstd", 1), mark("mla_y", 1)
        h_u, h_pr, h_y, h_inv, h_z = (mark(n, 2) for n in ("hy_dft", "hy_products", "hy_spectrum", "hy_inverse", "hy_gated"))
        h_sq, h_r, h_yy = mark("hy_squares", 2), mark("hy_rstd", 1), mark("hy_y", 1)
        s_step = {n: mark(f"step_{n}", 0) for n in ("pe", "pool", "dve")}
        chain = {n: mark(f"order_{n}", LINKS[n]) for n in LINKS}
        linked = {}

        def linker(e, name):
            linked[name] = 0

            def link(l, ins):
                linked[name] += 1
                ins.then_inc(chain[name].sem, 1)
                e.wait_ge(chain[name].sem, chain[name].at(l, linked[name]))
            return link

        def hold(e, name):
            e.sem_inc(s_step[name].sem, 1)

        def used(l, n):
            return s_used.at(l, n + RING + 1)

        block = ctx.enter_context(nc.Block())

        @block.sync
        def _(e):
            def fetch(n, p):
                src = w_d[bass.ds(n, 1), :, :].rearrange("s p n -> (s p) n")
                e.dma_start(raw[p][:].rearrange("p a b -> p (a b)"), src).then_inc(landed[p].sem, 16)

            def stream(first, last):
                with e.Fori(first, last) as i:
                    for u in range(RING):
                        e.wait_ge(s_lo.sem, (i - 1) * RING + u + 1)
                        fetch(i * RING + u, pos(u))

            fetch(0, pos(0))
            e.wait_ge(s_in0.sem, 16)
            e.wait_ge(s_in1.sem, 16)
            fetch(1, pos(1))
            fetch(2, pos(2))
            stream(1, FFN_SLOTS // RING // 2)
            for dst, src in ((dft[:].rearrange("p a b -> p (a b)"), dft_d[:, 0:1024]),
                             (idft[:].rearrange("p a b -> p (a b)"), dft_d[:, 1024:2048]),
                             (rope[:].rearrange("p a b c -> p (a b c)"), rope_d)):
                e.dma_start(dst, src).then_inc(s_in.sem, 16)
            stream(FFN_SLOTS // RING // 2, DEPTH * SLOTS // RING)
            for t in range(T):
                e.wait_ge(s_y.sem, t + 1)
                e.dma_start(out_d[t * P:(t + 1) * P, :], xn[:, t, :]).then_inc(s_out.sem, 16)
            e.wait_ge(s_out.sem, T * 16)

        @block.gpsimd
        def _(e):
            link = linker(e, "pool")
            e.dma_start(mask[:].rearrange("p a b -> p (a b)"), mask_d).then_inc(s_mask.sem, 16)
            e.wait_ge(s_cst.sem, 48)

            def rstd(l, m, v, src, dst, inv, n, done):
                e.wait_ge(m.sem, m.at(l, v))
                a, b = st[:, src:src + n], st[:, dst:dst + n]
                link(l, e.tensor_tensor(b, a, cst[:, inv:inv + n], ALU.mult))
                link(l, e.tensor_tensor(b, b, cst[:, I_EPS:I_EPS + n], ALU.add))
                e.tensor_tensor(b, b, cst[:, I_POW:I_POW + n], ALU.pow).then_inc(done.sem, 1)

            def x_rstd(l, j):
                r = st[:, T_R:T_R + 2]
                e.wait_ge(s_ss.sem, s_ss.at(l, 4 * j + 3))
                link(l, e.tensor_tensor(r, st[:, T_SS:T_SS + 2], cst[:, I_D:I_D + 2], ALU.add))
                e.wait_ge(s_ss.sem, s_ss.at(l, 4 * j + 4))
                link(l, e.tensor_tensor(r, r, st[:, T_SS + 2:T_SS + 4], ALU.add))
                e.tensor_tensor(r, r, cst[:, I_POW:I_POW + 2], ALU.pow).then_inc(s_rstd.sem, 1)

            def levels(l, b):
                B = 1 << b
                e.wait_ge(g_e.sem, g_e.at(l, b + 1))
                g = [G[:, n, :].rearrange("p (a w b) -> p a w b", w=2, b=B) for n in range(4)]
                n = SEQ // (2 * B)
                sb_, pf, sf, pb_ = g

                def add(to, side, of, oside, i, last=False):
                    o = of[:, :, oside, i:i + 1].to_broadcast([P, n, B])
                    return e.tensor_tensor(to[:, :, side, :], to[:, :, side, :], o, ALU.add)
                link(l, add(sf, 0, pf, 1, B - 1))
                link(l, add(pb_, 1, sb_, 0, 0))
                link(l, add(pf, 1, pf, 0, B - 1))
                add(sb_, 0, sb_, 1, 0).then_inc(g_gu.sem, 1)

            with e.Fori(0, DEPTH) as l:
                x_rstd(l, 0)
                e.wait_ge(s_x.sem, s_x.at(l, 4))
                e.wait_ge(s_used.sem, used(l, 0))
                for rows_, a, b in ((HYF, F_Z, F_DFT), (P, F_WIN, F_Z), (P, F_DFT, F_SKIP), (1, F_SKIP, NFIL)):
                    src = fil_d[bass.ds(l, 1), 0:rows_, a:b].rearrange("s p n -> (s p) n")
                    e.dma_start(fil[0:rows_, a:b], src).then_inc((s_fil1 if a == F_Z else s_fil).sem, 16)
                e.dma_start(wg[64:96, :, :].rearrange("p a b -> p (a b)"), gate_d[bass.ds(l, 1), :, :].rearrange("s p n -> (s p) n")).then_inc(s_fil.sem, 16)
                x_rstd(l, 1)
                for o in range(2):
                    for p in range(T):
                        e.wait_ge(f_hw.sem, f_hw.at(l, o * 2 + p + 1))
                        a, b = HW[:, o, p, 0:256], HW[:, o, p, 256:512]
                        link(l, e.tensor_tensor(HS[:, p, o * 256:(o + 1) * 256], a, b, ALU.add))
                        link(l, e.tensor_tensor(HD[:, p, o * 256:(o + 1) * 256], a, b, ALU.subtract))
                e.tensor_tensor(HS[0:1, 0, :], HS[0:1, 0, :], fil[0:1, F_SKIP:F_SKIP + 512], ALU.add).then_inc(f_hs.sem, 1)
                rstd(l, q_ss, 1, T_S4, T_R4, I_CQ, 4, q_r)
                e.wait_ge(q_kt.sem, q_kt.at(l))
                e.tensor_tensor(xn[:, :, 640:704], KT[:, 0], KT[:, 1], ALU.add).then_inc(q_kr.sem, 1)
                e.wait_ge(h_pr.sem, h_pr.at(l, 1))
                e.tensor_tensor(Y, Y, TT, ALU.add).then_inc(h_y.sem, 1)
                e.wait_ge(a_qt.sem, a_qt.at(l))
                e.tensor_tensor(xn[:, :, 768:1024], TT[:, 0:2, :], TT[:, 2:4, :], ALU.add).then_inc(a_qr.sem, 1)
                levels(l, 0)
                e.wait_ge(h_pr.sem, h_pr.at(l, 2))
                e.tensor_tensor(Y, Y, TT, ALU.add).then_inc(h_y.sem, 1)
                levels(l, 1)
                levels(l, 2)
                levels(l, 3)
                levels(l, 4)
                levels(l, 5)
                levels(l, 6)
                rstd(l, h_sq, 2, T_SH, T_RH, I_H, 2, h_r)
                rstd(l, a_sq, 2, T_SM, T_RM, I_M, 2, a_r)
                rstd(l, g_s8, 1, T_S8, T_R8, I_G, 8, g_r8)
                x_rstd(l, 2)
                e.wait_ge(s_x.sem, s_x.at(l, 4 * NORMS + 4))
                hold(e, "pool")
                e.tensor_copy(par[:], par_next[:, bass.ds(l, 1), :].rearrange("p a b -> p (a b)")).then_inc(s_par.sem, 1)
            r = st[:, T_R:T_R + 2]
            last = DEPTH * LINKS["pool"]
            e.wait_ge(s_ss.sem, s_ss.at(DEPTH, 4))
            e.tensor_tensor(r, st[:, T_SS:T_SS + 2], cst[:, I_D:I_D + 2], ALU.add).then_inc(chain["pool"].sem, 1)
            e.wait_ge(chain["pool"].sem, last + 1)
            e.tensor_tensor(r, r, st[:, T_SS + 2:T_SS + 4], ALU.add).then_inc(chain["pool"].sem, 1)
            e.wait_ge(chain["pool"].sem, last + 2)
            e.tensor_tensor(r, r, cst[:, I_POW:I_POW + 2], ALU.pow).then_inc(s_rstd.sem, 1)

        @block.scalar
        def _(e):
            link = linker(e, "act")
            for t, m in ((0, s_in0), (1, s_in1)):
                e.dma_start(x[:, t, :], x_d[t * P:(t + 1) * P, :]).then_inc(m.sem, 16)
            e.dma_start(cst[:], cst_d).then_inc(s_cst.sem, 16)
            e.dma_start(par[:], par_d[:, 0:NPAR]).then_inc(s_cst.sem, 16)
            e.dma_start(par_next[:].rearrange("p a b -> p (a b)"), par_d[:, NPAR:]).then_inc(s_cst.sem, 16)
            e.wait_ge(s_cst.sem, 48)
            e.sem_inc(s_par.sem, 1)

            def hi(l, n, occ=None):
                p, k = (pos(n), n // RING + 1) if occ is None else occ
                e.wait_ge(landed[p].sem, l * landed[p].per + k * 16)
                e.wait_ge(s_used.sem, l * SLOTS + n + 1)
                e.activation(WH[p][:], raw[p][:], ACT.Copy).then_inc(s_hi.sem, 1)

            def squares(l, j):
                for t in range(T):
                    for n in range(2):
                        q, c = 2 * t + n, T_SS + 2 * n + t
                        e.wait_ge(s_x.sem, s_x.at(l, 4 * j + 1 + q))
                        e.activation(xn[:, t, n * 512:(n + 1) * 512], x[:, t, n * 512:(n + 1) * 512], ACT.Square,
                                     accum_out=st[:, c:c + 1]).then_inc(s_ss.sem, 1)

            def turned_high(l, j, g, bank, tiles, col):
                e.wait_ge(s_tr.sem, s_tr.at(l, 4 * j + g + 1))
                for n, k in enumerate(tiles):
                    r = e.activation(XH[:, k, :], PS[:, bank, n * SEQ:(n + 1) * SEQ], ACT.Copy, scale=par[:, col + k:col + k + 1])
                r.then_inc(s_xh.sem, 1)

            def norm(l, j, turn, col, slot):
                hi(l, slot)
                squares(l, j)
                hi(l, slot + 1)
                e.wait_ge(s_par.sem, s_par.at(l))
                for g in range(4):
                    turned_high(l, turn, g, g, (2 * g, 2 * g + 1), col)

            def silu(l, q, f, pr, slot):
                e.wait_ge(s_used.sem, used(l, slot))
                e.activation(sg[:, f, :], PS[:, 4 + 2 * pr + f, 0:SEQ], ACT.Silu).then_inc(s_silu.sem, 1)

            def ht_high(l, q, f, pr):
                e.wait_ge(s_h.sem, s_h.at(l, 2 * q + f + 1))
                e.activation(HHB[pr][:, f, :], hid[:, f, :], ACT.Copy).then_inc(s_hh.sem, 1)

            def sine(l, n, dst):
                e.wait_ge(f_arg.sem, f_arg.at(l, n + 1))
                e.activation(dst[0:HYF], ARG[0:HYF], ACT.Sin).then_inc(f_sin.sem, 1)

            def ffn(l, f, base, j, turn, col):
                norm(l, j, turn, col, base)
                hi(l, base + 2); hi(l, base + 3)

                def chunk(c, pr):
                    q = f * CH + (c - 1)
                    for h in range(2):
                        silu(l, q, h, 1 - pr, base + h if c is first else base + 3 * c - 4 + h)
                        if c is not first:
                            hi(l, base + 3 * c - 1 + h, (pos(base + 2 + h), base // RING + c - 1 + (2 + h) // RING + 1))
                        ht_high(l, q, h, 1 - pr)
                    hi(l, base + 3 * c + 1, (pos(base + 1), base // RING + c + 1))
                first = 1
                chunk(first, 1)
                if f == 0:
                    sine(l, 0, H1)
                with e.Fori(0, (CH - 3) // 2) as i:
                    chunk(i * 2 + 2, 0)
                    chunk(i * 2 + 3, 1)
                chunk(CH - 1, (CH - 1) % 2)
                q, pr = f * CH + CH - 1, (CH - 1) % 2
                silu(l, q, 0, pr, base + FFN_SLOTS - 4)
                hi(l, base + FFN_SLOTS - 1)
                ht_high(l, q, 0, pr)
                silu(l, q, 1, pr, base + FFN_SLOTS - 3)
                ht_high(l, q, 1, pr)
                if f == 0:
                    sine(l, 1, H2)

            def copy(dst, src, m=None, **kw):
                r = e.activation(dst, src, ACT.Copy, **kw)
                if m is not None:
                    r.then_inc(m.sem, 1)

            def conv_centre(tile, bank, dst):
                e.activation(C[:, dst, :], PS[:, bank, 0:SEQ], ACT.Identity, scale=par[:, C_W1 + tile:C_W1 + tile + 1],
                             bias=par[:, C_CB + tile:C_CB + tile + 1]).then_inc(c_base.sem, 1)

            def natural(l, n, which, bank):
                e.wait_ge(c_tr.sem, c_tr.at(l, n))
                copy(NV[:, which].rearrange("p a b -> p (a b)"), PS[:, bank, :], c_nat)

            def level_exp(l, b):
                B = 1 << b
                if b == 0:
                    e.wait_ge(g_g0.sem, g_g0.at(l))
                else:
                    e.wait_ge(g_gu.sem, g_gu.at(l, b))
                    e.wait_ge(g_lq.sem, g_lq.at(l, b))
                for n in range(2):
                    first = G[:, 2 * n:2 * n + 1, 0:1]
                    src = bass.AP(first.tensor, first.offset, [first.ap[0], [2 * B, SEQ // (2 * B)], [SEQ + B, 2], [1, B]])
                    dst = sg[:, n, :].rearrange("p (a w b) -> p a w b", w=2, b=B)
                    r = e.activation(dst, src, ACT.Exp)
                r.then_inc(g_e.sem, 1)

            def probs(l, s):
                e.wait_ge(a_mx.sem, a_mx.at(l, s + 1))
                if s:
                    e.wait_ge(a_pt.sem, a_pt.at(l, s))
                for h in range(H):
                    c = T_MX + 4 * s + h
                    r = e.activation(PE_[:, h, :], PS[:, 4 + h // 2, (h % 2) * SEQ:(h % 2 + 1) * SEQ], ACT.Exp,
                                     scale=MLA_SCALE, bias=st[:, c:c + 1], accum_out=st[:, T_RS + 4 * s + h:T_RS + 4 * s + h + 1])
                r.then_inc(a_p.sem, 1)

            def probs_turned(l, s):
                e.wait_ge(a_pt.sem, a_pt.at(l, s + 1))
                if s:
                    e.wait_ge(a_o.sem, a_o.at(l, s))
                copy(PT.rearrange("p a h c -> p (a h c)"), PS[:, 4:6, :], a_pte)

            with e.Fori(0, DEPTH) as l:
                ffn(l, 0, 0, 0, 0, C_G1)
                norm(l, 1, 1, C_GM, S_G3)
                hi(l, S_G2); hi(l, S_G2 + 1)
                e.wait_ge(s_used.sem, used(l, S_G3 + 1))
                copy(hid[64:96, 0, :], PS[64:96, 4, 0:SEQ], g_in)
                for t in range(T):
                    e.activation(RG[:, t, :], PS[:, 5 + t, 0:256], ACT.Square, accum_out=st[:, T_S4 + 2 * t:T_S4 + 2 * t + 1])
                    r = e.activation(VG[:, t, 0:128], PS[:, 5 + t, 256:384], ACT.Square, accum_out=st[:, T_S4 + 2 * t + 1:T_S4 + 2 * t + 2])
                r.then_inc(q_ss.sem, 1)
                hi(l, S_G1); hi(l, S_G1 + 1)
                e.wait_ge(s_used.sem, used(l, S_G2 + 1))
                conv_centre(4, 0, 0); conv_centre(5, 1, 1)
                copy(QK[:, 0, :], PS[:, 2, 0:SEQ], scale=GDK ** -0.5)
                copy(QK[:, 1, :], PS[:, 3, 0:SEQ], g_qk)
                e.wait_ge(q_tr.sem, q_tr.at(l, 1))
                for n in range(2):
                    r = e.activation(HH[:, n, :], PS[:, 5, n * SEQ:(n + 1) * SEQ], ACT.Copy, scale=par[:, C_QN + n:C_QN + n + 1])
                r.then_inc(q_hi.sem, 1)
                e.wait_ge(q_tr.sem, q_tr.at(l, 2))
                copy(KR[0:DR, :], PS[0:DR, 6, SEQ:2 * SEQ], q_krt)
                copy(KVH[:], PS[:, 6, 0:SEQ], q_hi, scale=par[:, C_KVN:C_KVN + 1])
                for n, (dst, b) in enumerate(((KB[:], 4), (KA[:, 0, :], 2), (KA[:, 1, :], 3), (KI[:, 0, :], 0), (KI[:, 1, :], 1))):
                    e.wait_ge(k_mm.sem, k_mm.at(l, n + 1))
                    copy(dst, PS[:, b, :], k_ev)
                natural(l, 1, 2, 7)
                hi(l, S_G4)
                e.wait_ge(g_az.sem, g_az.at(l))
                link(l, e.activation(Z[:, 1], Z[:, 0], ACT.Abs))
                link(l, e.activation(Z[:, 1], Z[:, 1], ACT.Exp, scale=-1.0))
                e.activation(Z[:, 1], Z[:, 1], ACT.Ln, bias=1.0).then_inc(g_ln.sem, 1)
                hi(l, S_G4 + 1)
                e.wait_ge(s_used.sem, used(l, S_G1 + 1))
                e.wait_ge(c_tr.sem, c_tr.at(l, 1))
                for n in range(4):
                    conv_centre(n, n, n)
                hi(l, S_UQN)
                natural(l, 2, 0, 7)
                natural(l, 3, 1, 4)
                hi(l, S_UQR)
                level_exp(l, 0)
                e.wait_ge(s_used.sem, used(l, S_G4 + 1))
                for t in range(T):
                    copy(VG[:, t, :], PS[:, 5 + t, 0:256])
                    copy(RG[:, t, :], PS[:, 5 + t, 256:512], g_vr)
                hi(l, S_UKV)
                e.wait_ge(s_used.sem, used(l, S_UQN))
                for n in range(2):
                    copy(QN[:, 2 * n:2 * n + 2, :].rearrange("p a b -> p (a b)"), PS[:, 2 + n, :], a_qn)
                hi(l, S_WO)
                e.wait_ge(s_used.sem, used(l, S_UKV))
                copy(KN[:, 0:2, :].rearrange("p a b -> p (a b)"), PS[:, 4, :], a_kn)
                copy(KN[:, 2:4, :].rearrange("p a b -> p (a b)"), PS[:, 1, :], a_kn)
                copy(VM[:, 0, :], PS[:, 5, :], a_v)
                copy(VM[:, 1, :], PS[:, 6, :], a_v)
                e.wait_ge(a_qtr.sem, a_qtr.at(l))
                for n in range(2):
                    copy(QR[0:DR, 2 * n:2 * n + 2, :].rearrange("p a b -> p (a b)"), PS[0:DR, 2 + n, :], a_qre)
                hi(l, S_WO + 1)
                e.wait_ge(g_ls.sem, g_ls.at(l, 1))
                copy(AD.rearrange("p h t c -> p h (t c)"), PS[:, 0:4, 0:256], g_la)
                level_exp(l, 1)
                probs(l, 0)
                hi(l, S_WO + 2)
                level_exp(l, 2)
                probs_turned(l, 0)
                level_exp(l, 3)
                level_exp(l, 4)
                probs(l, 1)
                level_exp(l, 5)
                probs_turned(l, 1)
                level_exp(l, 6)
                e.wait_ge(h_z.sem, h_z.at(l, 2))
                for t in range(T):
                    e.activation(TT[:, t, :], xn[:, t, 0:256], ACT.Square, accum_out=st[:, T_SH + t:T_SH + t + 1]).then_inc(h_sq.sem, 1)
                level_exp(l, 7)
                for s in range(T):
                    e.wait_ge(a_oe.sem, a_oe.at(l, s + 1))
                    e.activation(C[:, 2 * s:2 * s + 2, :].rearrange("p a b -> p (a b)"), xn[:, s, 256:768], ACT.Square,
                                 accum_out=st[:, T_SM + s:T_SM + s + 1]).then_inc(a_sq.sem, 1)
                e.wait_ge(g_ls.sem, g_ls.at(l, LEVELS + 1))
                copy(AC.rearrange("p h t c -> p h (t c)"), PS[:, 0:4, 0:256], g_la)
                e.activation(RG, RG, ACT.Silu).then_inc(g_r.sem, 1)
                for g in range(2):
                    turned_high(l, 2, g, Y_BANKS[g], Y_TILES[g], C_GO)
                e.wait_ge(g_o.sem, g_o.at(l))
                e.activation(sg[:].rearrange("p a b -> p (a b)"), PS[:, 7, :], ACT.Square).then_inc(g_sq.sem, 1)
                hi(l, S_WO + 3)
                for g in range(2, 4):
                    turned_high(l, 2, g, Y_BANKS[g], Y_TILES[g], C_GO)
                ffn(l, 1, FFN2, 2, 3, C_G2)
            e.dma_start(C.rearrange("p a b -> p (a b)"), fin_d.rearrange("(a d) -> a d", a=1).to_broadcast([P, D])).then_inc(s_in.sem, 16)
            squares(DEPTH, 0)

        @block.vector
        def _(e):
            link = linker(e, "dve")

            def lo(l, n, p=None):
                p = pos(n) if p is None else p
                e.wait_ge(s_hi.sem, s_hi.at(l, n + 1))
                e.tensor_tensor(WL[p][:], raw[p][:], WH[p][:].bitcast(F32), ALU.subtract).then_inc(s_lo.sem, 1)

            def turned_low(l, j, g, bank, tiles, col):
                e.wait_ge(s_xh.sem, s_xh.at(l, 4 * j + g + 1))
                for n, k in enumerate(tiles):
                    r = e.scalar_tensor_tensor(out=XL[:, k, :], in0=PS[:, bank, n * SEQ:(n + 1) * SEQ], scalar=par[:, col + k:col + k + 1],
                                               in1=XH[:, k, :].bitcast(F32), op0=ALU.mult, op1=ALU.subtract)
                r.then_inc(s_xl.sem, 1)

            def diagonal(l, j):
                e.wait_ge(s_rstd.sem, s_rstd.at(l, j + 1))
                for t in range(T):
                    e.tensor_scalar(diag[:, t, :], ident, st[:, T_R + t:T_R + t + 1], float(D) ** 0.5, ALU.mult, ALU.mult).then_inc(s_dg.sem, 1)

            def norm(l, j, turn, col):
                diagonal(l, j)
                for g in range(4):
                    turned_low(l, turn, g, g, (2 * g, 2 * g + 1), col)

            def gate(l, q, f, pr):
                e.wait_ge(s_silu.sem, s_silu.at(l, 2 * q + f + 1))
                e.tensor_tensor(hid[:, f, :], sg[:, f, :], PS[:, 4 + 2 * pr + f, SEQ:2 * SEQ], ALU.mult).then_inc(s_h.sem, 1)

            def ht_low(l, q, f, pr):
                e.wait_ge(s_hh.sem, s_hh.at(l, 2 * q + f + 1))
                e.tensor_tensor(HLB[pr][:, f, :], hid[:, f, :], HHB[pr][:, f, :].bitcast(F32), ALU.subtract).then_inc(s_hl.sem, 1)

            def update(l, slot, scale, f=None):
                for t in range(T):
                    if t == 0 and f is not None:
                        e.wait_ge(s_d0.sem, s_d0.at(l, f + 1))
                    else:
                        e.wait_ge(s_used.sem, used(l, slot))
                    for n in range(2):
                        xs = x[:, t, n * 512:(n + 1) * 512]
                        e.scalar_tensor_tensor(out=xs, in0=PS[:, t * 2 + n, :], scalar=scale, in1=xs, op0=ALU.mult, op1=ALU.add).then_inc(s_x.sem, 1)

            def argument(l, n, bank, b, f):
                e.wait_ge(f_mm.sem, f_mm.at(l, n + 1))
                a, t = ARG[0:HYF], TURN[0:HYF]
                link(l, e.tensor_scalar(a, PS[0:HYF, bank, 0:SEQ], par[0:HYF, b:b + 1], par[0:HYF, f:f + 1], ALU.add, ALU.mult))
                link(l, e.tensor_scalar(t, a, 1 / (2 * math.pi), ROUND, ALU.mult, ALU.add))
                link(l, e.tensor_scalar(t, t, -ROUND, None, ALU.add))
                for c in (TWO_PI_A, TWO_PI_B, TWO_PI_C):
                    link(l, e.scalar_tensor_tensor(out=a, in0=t, scalar=-c, in1=a, op0=ALU.mult, op1=ALU.add))
                e.tensor_scalar(a, a, PI_F, -PI_F, ALU.min, ALU.max).then_inc(f_arg.sem, 1)

            def ffn(l, f, base, j, turn, col):
                lo(l, base)
                norm(l, j, turn, col)
                lo(l, base + 1)
                lo(l, base + 2); lo(l, base + 3)

                def chunk(c, pr):
                    q = f * CH + (c - 1)
                    for h in range(2):
                        gate(l, q, h, 1 - pr)
                        if c is not first:
                            lo(l, base + 3 * c - 1 + h, pos(base + 2 + h))
                        ht_low(l, q, h, 1 - pr)
                    lo(l, base + 3 * c + 1, pos(base + 1))
                first = 1
                chunk(first, 1)
                if f == 0:
                    argument(l, 0, 5, C_FB1, C_FF1)
                with e.Fori(0, (CH - 3) // 2) as i:
                    chunk(i * 2 + 2, 0)
                    chunk(i * 2 + 3, 1)
                chunk(CH - 1, (CH - 1) % 2)
                q, pr = f * CH + CH - 1, (CH - 1) % 2
                gate(l, q, 0, pr)
                lo(l, base + FFN_SLOTS - 1)
                ht_low(l, q, 0, pr)
                gate(l, q, 1, pr)
                ht_low(l, q, 1, pr)
                if f == 0:
                    argument(l, 1, 7, C_FB2, C_FF2)
                    lo(l, S_G3)
                update(l, base + FFN_SLOTS - 1, 0.5, f)

            def taps(l, n, tile, bank, dst):
                e.wait_ge(c_base.sem, c_base.at(l, n))
                link(l, e.scalar_tensor_tensor(out=C[:, dst, 1:SEQ], in0=PS[:, bank, 0:SEQ - 1], scalar=par[:, C_W0 + tile:C_W0 + tile + 1],
                                               in1=C[:, dst, 1:SEQ], op0=ALU.mult, op1=ALU.add))
                e.scalar_tensor_tensor(out=C[:, dst, 0:SEQ - 1], in0=PS[:, bank, 1:SEQ], scalar=par[:, C_W2 + tile:C_W2 + tile + 1],
                                       in1=C[:, dst, 0:SEQ - 1], op0=ALU.mult, op1=ALU.add).then_inc(c_conv.sem, 1)

            def level_qk(l, b):
                e.wait_ge(g_e.sem, g_e.at(l, b + 1))
                if b >= 2:
                    e.wait_ge(g_ls.sem, g_ls.at(l, b))
                e.tensor_tensor(QKL[b % 2], QK, sg[:], ALU.mult).then_inc(g_lq.sem, 1)

            def level_keep(l, b):
                e.wait_ge(g_ls.sem, g_ls.at(l, b + 2))
                if b == 0:
                    e.wait_ge(g_la.sem, g_la.at(l, 1))
                hold(e, "dve")
                m = mask[:, b, :]
                m = bass.AP(m.tensor, m.offset, [m.ap[0], [0, H], [0, T], [1, P]])
                e.copy_predicated(AD, m, PS[:, 0:4, 0:256].rearrange("p h (t c) -> p h t c", t=T)).then_inc(g_la.sem, 1)

            def score_max(l, s):
                e.wait_ge(a_s.sem, a_s.at(l, s + 1))
                c = T_MX + 4 * s
                link(l, e.tensor_reduce(st[:, c:c + 4], PS[:, 4:6, :].rearrange("p b (h k) -> p (b h) k", h=2), AX.X, ALU.max))
                e.tensor_scalar(st[:, c:c + 4], st[:, c:c + 4], -MLA_SCALE, None, ALU.mult).then_inc(a_mx.sem, 1)

            def attended(l, s):
                e.wait_ge(a_o.sem, a_o.at(l, s + 1))
                a, b = T_RS + 4 * s, T_RR + 4 * s
                link(l, e.reciprocal(st[:, b:b + 4], st[:, a:a + 4]))
                r = st[:, b:b + 4]
                r = bass.AP(r.tensor, r.offset, [r.ap[0], [1, H], [0, DV]])
                e.tensor_tensor(xn[:, s, 256:768].rearrange("p (h d) -> p h d", h=H), PS[:, 4, :].rearrange("p (h d) -> p h d", h=H),
                                r, ALU.mult).then_inc(a_oe.sem, 1)

            def products(l, o, b):
                e.wait_ge(h_u.sem, h_u.at(l, o + 1))
                if o:
                    e.wait_ge(h_inv.sem, h_inv.at(l, o))
                c = slice(o * 256, (o + 1) * 256)
                ur = PS[:, b, :].rearrange("p (m n) -> p m n", m=2)
                ui = PS[:, b + 1, :].rearrange("p (m n) -> p m n", m=2)
                e.tensor_tensor(Y[:, 0:2, :], ur, KA[:, :, c], ALU.mult)
                e.scalar_tensor_tensor(out=TT[:, 0:2, :], in0=ui, scalar=-1.0, in1=KI[:, :, c], op0=ALU.mult, op1=ALU.mult)
                e.tensor_tensor(Y[:, 2, :], ui[:, 0, :], KB[:, c], ALU.mult)
                e.tensor_tensor(Y[:, 3, :], ui[:, 1, :], KA[:, 1, c], ALU.mult)
                e.tensor_tensor(TT[:, 2:4, :], ur, KI[:, :, c], ALU.mult).then_inc(h_pr.sem, 1)

            def gated(l, o, b):
                e.wait_ge(h_inv.sem, h_inv.at(l, o + 1))
                dst = NV[:, 0] if o == 0 else xn[:, :, 0:256]
                e.tensor_tensor(dst, PS[:, b, :].rearrange("p (t n) -> p t n", t=T), NV[:, 1 + o], ALU.mult).then_inc(h_z.sem, 1)

            e.wait_ge(s_in0.sem, 16)
            e.sem_inc(s_x.sem, 2)
            e.wait_ge(s_in1.sem, 16)
            e.sem_inc(s_x.sem, 2)
            e.wait_ge(s_cst.sem, 48)
            with e.Fori(0, DEPTH) as l:
                ffn(l, 0, 0, 0, 0, C_G1)
                e.wait_ge(s_in.sem, 16 * N_IN)
                e.wait_ge(s_mask.sem, 16)
                e.wait_ge(s_fil.sem, s_fil.at(l, 64))
                for o in range(2):
                    for p in range(T):
                        e.wait_ge(f_w3.sem, f_w3.at(l, o * 2 + p + 1))
                        e.tensor_tensor(HW[:, o, p, :], PS[:, 4 + o * 2 + p, :], fil[:, F_WIN + p * 512:F_WIN + (p + 1) * 512], ALU.mult).then_inc(f_hw.sem, 1)
                diagonal(l, 1)
                for g in range(4):
                    turned_low(l, 1, g, g, (2 * g, 2 * g + 1), C_GM)
                lo(l, S_G3 + 1)
                lo(l, S_G2); lo(l, S_G2 + 1)
                e.wait_ge(s_used.sem, used(l, S_G3 + 1))
                e.wait_ge(q_r.sem, q_r.at(l))
                for t in range(T):
                    for n, (a, b) in enumerate(((0, 256), (256, 384))):
                        c = T_R4 + 2 * t + n
                        r = e.tensor_scalar(xn[:, t, 256 + a:256 + b], PS[:, 5 + t, a:b], st[:, c:c + 1], None, ALU.mult)
                r.then_inc(q_n.sem, 1)
                kr = PS[:, 5:7, 384:448]
                e.tensor_tensor(KT[:, 0], kr, rope[:, 0], ALU.mult)
                e.tensor_tensor(KT[:, 1, :, 0:32], kr[:, :, 32:64], rope[:, 1, :, 0:32], ALU.mult)
                e.tensor_tensor(KT[:, 1, :, 32:64], kr[:, :, 0:32], rope[:, 1, :, 32:64], ALU.mult).then_inc(q_kt.sem, 1)
                lo(l, S_G1)
                taps(l, 1, 4, 0, 0); taps(l, 2, 5, 1, 1)
                e.wait_ge(g_z.sem, g_z.at(l))
                for d in range(2):
                    r = e.tensor_scalar(Z[:, 0, d, :], PS[:, 7, d * SEQ:(d + 1) * SEQ], par[:, C_BG + d:C_BG + d + 1], None, ALU.add)
                r.then_inc(g_az.sem, 1)
                e.wait_ge(q_hi.sem, q_hi.at(l, 1))
                for n in range(2):
                    r = e.scalar_tensor_tensor(out=HL[:, n, :], in0=PS[:, 5, n * SEQ:(n + 1) * SEQ], scalar=par[:, C_QN + n:C_QN + n + 1],
                                               in1=HH[:, n, :].bitcast(F32), op0=ALU.mult, op1=ALU.subtract)
                r.then_inc(q_lo.sem, 1)
                e.wait_ge(q_hi.sem, q_hi.at(l, 2))
                e.scalar_tensor_tensor(out=KVL[:], in0=PS[:, 6, 0:SEQ], scalar=par[:, C_KVN:C_KVN + 1],
                                       in1=KVH[:].bitcast(F32), op0=ALU.mult, op1=ALU.subtract).then_inc(q_lo.sem, 1)
                lo(l, S_G1 + 1)
                lo(l, S_G4)
                e.memset(G[:, 2:4, :], 0.0)
                e.wait_ge(g_ln.sem, g_ln.at(l))
                link(l, e.tensor_scalar(Z[:, 0], Z[:, 0], 0.0, 1 / 16, ALU.min, ALU.mult))
                e.scalar_tensor_tensor(out=G[:, 1, :], in0=Z[:, 1, 0, :], scalar=-1 / 16, in1=Z[:, 0, 0, :], op0=ALU.mult, op1=ALU.add)
                e.scalar_tensor_tensor(out=G[:, 0, :], in0=Z[:, 1, 1, :], scalar=-1 / 16, in1=Z[:, 0, 1, :], op0=ALU.mult, op1=ALU.add).then_inc(g_g0.sem, 1)
                lo(l, S_G4 + 1)
                for n in range(4):
                    taps(l, 3 + n, n, n, n)
                lo(l, S_UQN)
                lo(l, S_UQR)
                products(l, 0, 0)
                lo(l, S_UKV)
                e.wait_ge(s_used.sem, used(l, S_UQR))
                e.wait_ge(h_y.sem, h_y.at(l, 1))
                q = PS[:, 7, :].rearrange("p (t h d) -> p t h d", t=T, h=H)

                def rp(n, a, b):
                    r = rope[:, n, :, a:b]
                    return bass.AP(r.tensor, r.offset, [r.ap[0], [DR, T], [0, H], [1, b - a]])
                t1 = TT[:, 0:2, :].rearrange("p t (h d) -> p t h d", h=H)
                t2 = TT[:, 2:4, :].rearrange("p t (h d) -> p t h d", h=H)
                e.tensor_tensor(t1, q, rp(0, 0, 64), ALU.mult)
                e.tensor_tensor(t2[:, :, :, 0:32], q[:, :, :, 32:64], rp(1, 0, 32), ALU.mult)
                e.tensor_tensor(t2[:, :, :, 32:64], q[:, :, :, 0:32], rp(1, 32, 64), ALU.mult).then_inc(a_qt.sem, 1)
                gated(l, 0, 0)
                level_qk(l, 0)
                lo(l, S_WO)
                e.wait_ge(a_qr.sem, a_qr.at(l))
                products(l, 1, 6)
                level_qk(l, 1)
                lo(l, S_WO + 1)
                score_max(l, 0)
                level_keep(l, 0)
                level_qk(l, 2)
                level_keep(l, 1)
                level_qk(l, 3)
                lo(l, S_WO + 2)
                attended(l, 0)
                level_keep(l, 2)
                level_qk(l, 4)
                score_max(l, 1)
                level_keep(l, 3)
                level_qk(l, 5)
                gated(l, 1, 6)
                level_keep(l, 4)
                level_qk(l, 6)
                level_keep(l, 5)
                level_qk(l, 7)
                attended(l, 1)
                level_keep(l, 6)
                e.wait_ge(h_r.sem, h_r.at(l))
                for t in range(T):
                    v = xn[:, t, 0:256]
                    r = e.tensor_scalar(v, v, st[:, T_RH + t:T_RH + t + 1], None, ALU.mult)
                r.then_inc(h_yy.sem, 1)
                e.wait_ge(a_r.sem, a_r.at(l))
                for t in range(T):
                    v = xn[:, t, 256:768]
                    r = e.tensor_scalar(v, v, st[:, T_RM + t:T_RM + t + 1], None, ALU.mult)
                r.then_inc(a_y.sem, 1)
                for g in range(2):
                    turned_low(l, 2, g, Y_BANKS[g], Y_TILES[g], C_GO)
                e.wait_ge(g_sq.sem, g_sq.at(l))
                e.tensor_reduce(st[:, T_S8:T_S8 + 8], sg[:].rearrange("p t (h d) -> p (t h) d", d=GDV), AX.X, ALU.add).then_inc(g_s8.sem, 1)
                e.wait_ge(g_r8.sem, g_r8.at(l))
                r8 = st[:, T_R8:T_R8 + 8]
                r8 = bass.AP(r8.tensor, r8.offset, [r8.ap[0], [1, 8], [0, GDV]])
                og = hid[:].rearrange("p t (h d) -> p (t h) d", d=GDV)
                link(l, e.tensor_tensor(og, PS[:, 7, :].rearrange("p (n d) -> p n d", d=GDV), r8, ALU.mult))
                e.wait_ge(g_r.sem, g_r.at(l))
                e.tensor_tensor(xn[:, :, 768:1024], hid[:], RG, ALU.mult).then_inc(g_y.sem, 1)
                lo(l, S_WO + 3)
                for g in range(2, 4):
                    turned_low(l, 2, g, Y_BANKS[g], Y_TILES[g], C_GO)
                update(l, S_WO + 3, 1.0)
                ffn(l, 1, FFN2, 2, 3, C_G2)
            e.wait_ge(s_in.sem, 16 * (N_IN + 1))
            e.wait_ge(s_rstd.sem, s_rstd.at(DEPTH))
            last = DEPTH * LINKS["dve"]
            r = st[:, T_R:T_R + 2]
            e.tensor_scalar(r, r, float(D) ** 0.5, None, ALU.mult).then_inc(chain["dve"].sem, 1)
            e.wait_ge(chain["dve"].sem, last + 1)
            for t in range(T):
                e.scalar_tensor_tensor(out=xn[:, t, :], in0=x[:, t, :], scalar=st[:, T_R + t:T_R + t + 1], in1=C.rearrange("p a b -> p (a b)"),
                                       op0=ALU.mult, op1=ALU.mult).then_inc(s_y.sem, 1)

        @block.tensor
        def _(e):
            e.sem_inc(s_used.sem, RING)

            def passes(out, ah, al, bh, bl, start, stop):
                e.matmul(out, ah, bh, start=start, stop=False)
                e.matmul(out, ah, bl, start=False, stop=False)
                return e.matmul(out, al, bh, start=False, stop=stop)

            def turn_group(l, j, g, bank, tiles):
                for n, k in enumerate(tiles):
                    for t in range(T):
                        r = e.transpose(PS[:, bank, n * SEQ + t * P:n * SEQ + (t + 1) * P], xn[:, t, k * P:(k + 1) * P], ident)
                r.then_inc(s_tr.sem, 1)

            def norm(l, j, turn):
                for g in range(4):
                    for n in range(2):
                        k = 2 * g + n
                        for t in range(T):
                            if g == 0 and n == 0:
                                e.wait_ge(s_dg.sem, s_dg.at(l, 2 * j + t + 1))
                            r = e.matmul(PS[:, g, n * SEQ + t * P:n * SEQ + (t + 1) * P], x[:, t, k * P:(k + 1) * P], diag[:, t, :],
                                         start=True, stop=True)
                    r.then_inc(s_tr.sem, 1)

            def x_tile(l, turn, k, first):
                if first and k % 2 == 0:
                    e.wait_ge(s_xl.sem, s_xl.at(l, 4 * turn + k // 2 + 1))

            def rows(l, turn, n, half, width, banks, inc=None):
                p = pos(n)
                e.wait_ge(s_lo.sem, s_lo.at(l, n + 1))
                for t in range(T):
                    for kk in range(4):
                        k = half * 4 + kk
                        x_tile(l, turn, k, t == 0)
                        r = passes(PS[:, banks[t], 0:width], XH[:, k, t * P:(t + 1) * P], XL[:, k, t * P:(t + 1) * P],
                                   WH[p][:, kk, 0:width], WL[p][:, kk, 0:width], k == 0, k == KD - 1)
                    if inc is not None and t == 0:
                        r.then_inc(inc.sem, 1)
                return r

            def columns(l, turn, n, half, tiles):
                p = pos(n)
                e.wait_ge(s_lo.sem, s_lo.at(l, n + 1))
                for kk in range(4):
                    k = half * 4 + kk
                    x_tile(l, turn, k, True)
                    for c, b in tiles:
                        r = passes(PS[:, b, 0:SEQ], WH[p][:, kk, c:c + P], WL[p][:, kk, c:c + P], XH[:, k, :], XL[:, k, :], k == 0, k == KD - 1)
                return r

            def down(l, n, p, q, pr, first, last, f):
                e.wait_ge(s_lo.sem, s_lo.at(l, n + 1))
                for h in range(2):
                    e.wait_ge(s_hl.sem, s_hl.at(l, 2 * q + h + 1))
                    for t in range(T):
                        for m in range(2):
                            r = passes(PS[:, t * 2 + m, :], HHB[pr][:, h, t * P:(t + 1) * P], HLB[pr][:, h, t * P:(t + 1) * P],
                                       WH[p][:, h * 2 + m, :], WL[p][:, h * 2 + m, :], first and h == 0, last and h == 1)
                        if last and h == 1 and t == 0:
                            r.then_inc(s_d0.sem, 1)
                r.then_inc(s_used.sem, 1)

            def gate_up(l, turn, n, p, half, pr, first):
                e.wait_ge(s_lo.sem, s_lo.at(l, n + 1))
                for g in range(2):
                    for k in range(KD):
                        if first:
                            x_tile(l, turn, k, g == 0)
                        a = slice((k % 2) * 256 + g * P, (k % 2) * 256 + (g + 1) * P)
                        r = passes(PS[:, 4 + 2 * pr + half, g * SEQ:(g + 1) * SEQ], WH[p][:, k // 2, a], WL[p][:, k // 2, a],
                                   XH[:, k, :], XL[:, k, :], k == 0, k == KD - 1)
                r.then_inc(s_used.sem, 1)

            def filter_mm(l, n, w, src, rows_, bank):
                if n == 0:
                    e.wait_ge(s_fil1.sem, s_fil1.at(l, 16))
                else:
                    e.wait_ge(f_sin.sem, f_sin.at(l, n))
                hold(e, "pe")
                e.matmul(PS[0:HYF, bank, 0:SEQ], fil[0:rows_, w:w + HYF], src[0:rows_], start=True, stop=True).then_inc(f_mm.sem, 1)

            def ffn(l, f, base, j, turn):
                norm(l, j, turn)
                gate_up(l, turn, base, pos(base), 0, 0, True)
                gate_up(l, turn, base + 1, pos(base + 1), 1, 0, True)

                def chunk(c, pr, first=False):
                    q = f * CH + (c - 1)
                    gate_up(l, turn, base + 3 * c - 1, pos(base + 2), 0, pr, False)
                    gate_up(l, turn, base + 3 * c, pos(base), 1, pr, False)
                    if f == 0 and first:
                        e.wait_ge(s_hl.sem, s_hl.at(l, 2))
                        filter_mm(l, 0, F_W1, fil[:, F_Z:F_Z + SEQ], HYE, 5)
                    if f == 0 and c is last:
                        filter_mm(l, 1, F_W2, H1, HYF, 7)
                    down(l, base + 3 * c + 1, pos(base + 1), q, 1 - pr, first, False, f)
                last = CH - 1
                chunk(1, 1, True)
                if f == 0:
                    e.wait_ge(f_arg.sem, f_arg.at(l, 1))
                    hold(e, "pe")
                with e.Fori(0, (CH - 3) // 2) as i:
                    chunk(i * 2 + 2, 0)
                    chunk(i * 2 + 3, 1)
                chunk(last, last % 2)
                down(l, base + FFN_SLOTS - 1, pos(base + FFN_SLOTS - 1), f * CH + last, last % 2, False, True, f)

            def level_scores(l, b):
                if b >= 0:
                    e.wait_ge(g_lq.sem, g_lq.at(l, b + 1))
                    e.wait_ge(g_la.sem, g_la.at(l, b + 1))
                qk = QK if b < 0 else QKL[b % 2]
                for t in range(T):
                    o = t if b < LEVELS - 1 else 1 - t
                    for h in range(H):
                        r = e.matmul(PS[:, h, t * P:(t + 1) * P], qk[32 * h:32 * h + 32, 1, t * P:(t + 1) * P],
                                     qk[32 * h:32 * h + 32, 0, o * P:(o + 1) * P], start=True, stop=True)
                r.then_inc(g_ls.sem, 1)

            def hy_dft(l, o, b):
                for part in range(2):
                    for m in range(2):
                        for p in range(T):
                            r = e.matmul(PS[:, b + part, m * 256:(m + 1) * 256], dft[:, p, part * 256 + m * P:part * 256 + (m + 1) * P],
                                         NV[:, 0, p, :], start=(p == 0), stop=(p == T - 1))
                r.then_inc(h_u.sem, 1)

            def hy_inverse(l, o, b):
                e.wait_ge(h_y.sem, h_y.at(l, o + 1))
                for t in range(T):
                    for m in range(4):
                        r = e.matmul(PS[:, b, t * 256:(t + 1) * 256], idft[:, m, t * P:(t + 1) * P], Y[:, m, :], start=(m == 0), stop=(m == 3))
                r.then_inc(h_inv.sem, 1)

            def scores(l, s):
                for h in range(H):
                    out = PS[:, 4 + h // 2, (h % 2) * SEQ:(h % 2 + 1) * SEQ]
                    e.matmul(out, QN[:, h, s * P:(s + 1) * P], KN[:, h, :], start=True, stop=False)
                    r = e.matmul(out, QR[0:DR, h, s * P:(s + 1) * P], KR[0:DR, :], start=False, stop=True)
                r.then_inc(a_s.sem, 1)

            def turn_probs(l, s):
                e.wait_ge(a_p.sem, a_p.at(l, s + 1))
                for k in range(T):
                    for h in range(H):
                        r = e.transpose(PS[:, 4 + k, h * P:(h + 1) * P], PE_[:, h, k * P:(k + 1) * P], ident)
                r.then_inc(a_pt.sem, 1)

            def attend(l, s):
                e.wait_ge(a_pte.sem, a_pte.at(l, s + 1))
                for h in range(H):
                    for k in range(T):
                        r = e.matmul(PS[:, 4, h * P:(h + 1) * P], PT[:, k, h, :], VM[:, k, h * P:(h + 1) * P], start=(k == 0), stop=(k == T - 1))
                r.then_inc(a_o.sem, 1)

            def turn_conv(l, dst, bank):
                for t in range(T):
                    for j in range(2):
                        r = e.transpose(PS[:, bank, t * 256 + j * P:t * 256 + (j + 1) * P], C[:, dst + j, t * P:(t + 1) * P], ident)
                r.then_inc(c_tr.sem, 1)

            with e.Fori(0, DEPTH) as l:
                ffn(l, 0, 0, 0, 0)
                e.wait_ge(s_in.sem, 16 * N_IN)
                e.wait_ge(f_sin.sem, f_sin.at(l, 2))
                for o in range(2):
                    for p in range(T):
                        e.matmul(PS[:, 4 + 2 * o + p, :], H2[0:HYF, p * P:(p + 1) * P], fil[0:HYF, F_W3 + o * 512:F_W3 + (o + 1) * 512],
                                 start=True, stop=True).then_inc(f_w3.sem, 1)
                norm(l, 1, 1)
                e.wait_ge(f_hw.sem, f_hw.at(l, 4))
                for i in range(2):
                    rows(l, 1, S_G3 + i, i, 448, (5, 6))
                    columns(l, 1, S_G3 + i, i, [(384, 4)]).then_inc(s_used.sem, 1)
                for i in range(2):
                    columns(l, 1, S_G2 + i, i, [(128 * n, n) for n in range(4)]).then_inc(s_used.sem, 1)
                e.wait_ge(s_fil.sem, s_fil.at(l, 64))
                e.wait_ge(g_in.sem, g_in.at(l))
                for d in range(2):
                    r = e.matmul(PS[:, 7, d * SEQ:(d + 1) * SEQ], wg[64:96, d, :], hid[64:96, 0, :], start=True, stop=True)
                r.then_inc(g_z.sem, 1)
                e.wait_ge(q_n.sem, q_n.at(l))
                e.wait_ge(q_kr.sem, q_kr.at(l))
                for n in range(2):
                    for t in range(T):
                        r = e.transpose(PS[:, 5, n * SEQ + t * P:n * SEQ + (t + 1) * P], xn[:, t, 256 + n * P:256 + (n + 1) * P], ident)
                r.then_inc(q_tr.sem, 1)
                for t in range(T):
                    e.transpose(PS[:, 6, t * P:(t + 1) * P], xn[:, t, 512:640], ident)
                    r = e.transpose(PS[0:DR, 6, SEQ + t * P:SEQ + (t + 1) * P], xn[:, t, 640:704], ident)
                r.then_inc(q_tr.sem, 1)
                e.wait_ge(f_hs.sem, f_hs.at(l))
                for b, what in ((4, 256), (2, None), (3, None), (0, 0), (1, P)):
                    if b == 2:
                        e.wait_ge(g_qk.sem, g_qk.at(l))
                    if b == 0:
                        e.wait_ge(c_conv.sem, c_conv.at(l, 2))
                    for p in range(T):
                        if what is None:
                            w, h = dft[:, p, (b - 2) * P:(b - 1) * P], HS
                        else:
                            w, h = fil[:, F_DFT + p * 384 + what:F_DFT + p * 384 + what + P], HS if b == 4 else HD
                        r = e.matmul(PS[:, b, :], w, h[:, p, :], start=(p == 0), stop=(p == T - 1))
                    r.then_inc(k_mm.sem, 1)
                e.wait_ge(g_az.sem, g_az.at(l))
                turn_conv(l, 0, 7)
                e.wait_ge(k_ev.sem, k_ev.at(l, 5))
                for i in range(2):
                    columns(l, 1, S_G1 + i, i, [(128 * n, n) for n in range(4)]).then_inc(s_used.sem, 1)
                e.wait_ge(q_lo.sem, q_lo.at(l, 2))
                e.wait_ge(q_krt.sem, q_krt.at(l))
                rows(l, 1, S_G4, 0, 512, (5, 6)).then_inc(s_used.sem, 1)
                e.wait_ge(c_nat.sem, c_nat.at(l, 1))
                e.wait_ge(c_conv.sem, c_conv.at(l, 4))
                turn_conv(l, 0, 7)
                e.wait_ge(c_conv.sem, c_conv.at(l, 6))
                turn_conv(l, 2, 4)
                rows(l, 1, S_G4 + 1, 1, 512, (5, 6)).then_inc(s_used.sem, 1)
                e.wait_ge(c_nat.sem, c_nat.at(l, 2))
                hy_dft(l, 0, 0)
                e.wait_ge(s_lo.sem, s_lo.at(l, S_UQN + 1))
                p = pos(S_UQN)
                for h in range(H):
                    for k in range(2):
                        r = passes(PS[:, 2 + h // 2, (h % 2) * SEQ:(h % 2 + 1) * SEQ], WH[p][:, k, h * P:(h + 1) * P], WL[p][:, k, h * P:(h + 1) * P],
                                   HH[:, k, :], HL[:, k, :], k == 0, k == 1)
                r.then_inc(s_used.sem, 1)
                e.wait_ge(s_lo.sem, s_lo.at(l, S_UQR + 1))
                p = pos(S_UQR)
                for t in range(T):
                    for k in range(2):
                        r = passes(PS[:, 7, t * 256:(t + 1) * 256], HH[:, k, t * P:(t + 1) * P], HL[:, k, t * P:(t + 1) * P],
                                   WH[p][:, k, 0:256], WL[p][:, k, 0:256], k == 0, k == 1)
                r.then_inc(s_used.sem, 1)
                e.wait_ge(s_lo.sem, s_lo.at(l, S_UKV + 1))
                e.wait_ge(c_nat.sem, c_nat.at(l, 3))
                e.wait_ge(h_pr.sem, h_pr.at(l, 1))
                p = pos(S_UKV)
                for h in range(H):
                    passes(PS[:, (4, 1)[h // 2], (h % 2) * SEQ:(h % 2 + 1) * SEQ], WH[p][:, 0, h * P:(h + 1) * P], WL[p][:, 0, h * P:(h + 1) * P],
                           KVH[:], KVL[:], True, True)
                for t in range(T):
                    e.wait_ge(g_vr.sem, g_vr.at(l, t + 1))
                    r = passes(PS[:, 5 + t, :], KVH[:, t * P:(t + 1) * P], KVL[:, t * P:(t + 1) * P], WH[p][:, 1, :], WL[p][:, 1, :], True, True)
                r.then_inc(s_used.sem, 1)
                hy_inverse(l, 0, 0)
                e.wait_ge(a_qr.sem, a_qr.at(l))
                e.wait_ge(a_qn.sem, a_qn.at(l, 2))
                hold(e, "pe")
                for h in range(H):
                    for t in range(T):
                        r = e.transpose(PS[0:DR, 2 + h // 2, (h % 2) * SEQ + t * P:(h % 2) * SEQ + (t + 1) * P],
                                        xn[:, t, 768 + h * DR:768 + (h + 1) * DR], ident)
                r.then_inc(a_qtr.sem, 1)
                e.wait_ge(a_v.sem, a_v.at(l, 2))
                e.wait_ge(h_z.sem, h_z.at(l, 1))
                hy_dft(l, 1, 6)
                e.wait_ge(a_qre.sem, a_qre.at(l, 2))
                level_scores(l, -1)
                scores(l, 0)
                level_scores(l, 0)
                turn_probs(l, 0)
                hy_inverse(l, 1, 6)
                level_scores(l, 1)
                attend(l, 0)
                level_scores(l, 2)
                e.wait_ge(a_oe.sem, a_oe.at(l, 1))
                scores(l, 1)
                level_scores(l, 3)
                level_scores(l, 4)
                turn_probs(l, 1)
                level_scores(l, 5)
                attend(l, 1)
                level_scores(l, 6)
                level_scores(l, 7)
                e.wait_ge(g_la.sem, g_la.at(l, LEVELS + 1))
                for s in range(T):
                    for h in range(H):
                        for t in range(T):
                            a = AD[:, h, s, :] if t == s else AC[:, h, t, :]
                            r = e.matmul(PS[:, 7, s * 256 + h * GDV:s * 256 + (h + 1) * GDV], a, VG[:, t, h * GDV:(h + 1) * GDV],
                                         start=(t == 0), stop=(t == T - 1))
                r.then_inc(g_o.sem, 1)
                e.wait_ge(a_y.sem, a_y.at(l))
                for g in range(2):
                    turn_group(l, 2, g, Y_BANKS[g], Y_TILES[g])
                e.wait_ge(h_yy.sem, h_yy.at(l))
                turn_group(l, 2, 2, Y_BANKS[2], Y_TILES[2])
                for g in range(4):
                    if g == 2:
                        e.wait_ge(g_y.sem, g_y.at(l))
                        turn_group(l, 2, 3, Y_BANKS[3], Y_TILES[3])
                    n = S_WO + g
                    p = pos(n)
                    e.wait_ge(s_lo.sem, s_lo.at(l, n + 1))
                    e.wait_ge(s_xl.sem, s_xl.at(l, 8 + g + 1))
                    for t in range(T):
                        for i, k in enumerate(Y_TILES[g]):
                            for m in range(2):
                                r = passes(PS[:, t * 2 + m, :], XH[:, k, t * P:(t + 1) * P], XL[:, k, t * P:(t + 1) * P],
                                           WH[p][:, 2 * i + m, :], WL[p][:, 2 * i + m, :], g == 0 and i == 0, g == 3 and i == 1)
                    r.then_inc(s_used.sem, 1)
                ffn(l, 1, FFN2, 2, 3)
        assert linked == LINKS, linked


N_IN = 3


def ffn_slots(gate, up, down):
    out, last = [], None
    for c in range(CH):
        at = slice(c * 256, (c + 1) * 256)
        for half in range(2):
            r = slice(at.start + half * P, at.start + (half + 1) * P)
            a = np.stack([gate[:, r].reshape(KD, P, P), up[:, r].reshape(KD, P, P)], 2)
            out.append(a.transpose(1, 0, 2, 3).reshape(P, SLOT))
        if last is not None:
            out.append(last)
        last = down[at].reshape(2, P, D).transpose(1, 0, 2).reshape(P, SLOT)
    return out + [last]


def mix_slots(w_in, w_uq, w_ukv, w_out):
    def two(cols):
        w = np.zeros((D, 512), np.float32)
        at = 0
        for a, b in cols:
            w[:, at:at + b - a] = w_in[:, a:b]
            at += b - a
        w = w.reshape(2, 4, P, 512).transpose(0, 2, 1, 3)
        return [w[0].reshape(P, SLOT), w[1].reshape(P, SLOT)]

    def one(parts):
        w = np.zeros((P, 4, 512), np.float32)
        for n, a in enumerate(parts):
            w[:, n, :a.shape[1]] = a
        return [w.reshape(P, SLOT)]
    out = two([(768, 1216), (1728, 1760)])
    out += two([(512, 768), (1216, 1472)])
    out += two([(0, 512)])
    out += two([(1472, 1728), (1760, 2016)])
    uq = w_uq.reshape(2, P, H, DN + DR)
    out += one([uq[k, :, :, :DN].reshape(P, H * DN) for k in range(2)])
    out += one([uq[k, :, :, DN:].reshape(P, H * DR) for k in range(2)])
    ukv = w_ukv.reshape(P, H, DN + DV)
    out += one([ukv[:, :, :DN].reshape(P, 512), ukv[:, :, DN:].reshape(P, 512)])
    for ks in Y_TILES:
        out.append(np.stack([w_out[k * P:(k + 1) * P] for k in ks], 1).reshape(P, SLOT))
    return out


def shape_constants():
    f32 = np.float32
    f = np.arange(256)
    ang = 2 * np.pi / 512 * ((f[:, None] * f[None, :]) % 512)
    cos, sin = np.cos(ang), np.sin(ang)
    nyq = 1.0 - 2.0 * (f % 2)
    sin_n, cos_n = -sin, cos[:, :P].copy()
    sin_n[:, 0], cos_n[:, 0] = nyq, nyq
    dft = np.concatenate([cos, sin_n], 1).reshape(T, P, 512).transpose(1, 0, 2).reshape(P, 1024)
    w = np.where(f == 0, 1.0, 2.0)[:, None] / 512
    inv_im = -w * sin
    inv_im[0] = nyq / 512
    inv = np.concatenate([w * cos, inv_im]).reshape(4, P, SEQ).transpose(1, 0, 2).reshape(P, 1024)
    fil_dft = np.concatenate([-sin, cos_n], 1).reshape(T, P, 384).transpose(1, 0, 2).reshape(P, 768)

    p = np.arange(SEQ, dtype=f32)
    t = p / f32(SEQ - 1)
    bands = np.linspace(1e-4, 15, 16, dtype=f32)
    a = (f32(2 * math.pi) * p / f32(SEQ))[:, None] * bands[None, :]
    z = np.concatenate([t[:, None], np.cos(a), -np.sin(a)], -1)
    lo_, hi_ = math.log(1e-2) / 1.5, math.log(1e-2) / 0.3
    win = np.exp(-t[:, None] * np.abs(np.linspace(lo_, hi_, HYW, dtype=f32))[None, :])
    win_b = win.copy()
    win_b[0] = 0
    win = np.concatenate([win, win_b], 1).reshape(T, P, 512).transpose(1, 0, 2).reshape(P, 1024)

    inv_f = f32(10000.0) ** (-np.arange(32, dtype=f32) * f32(2.0) / f32(DR))
    a = p[:, None] * inv_f[None, :].astype(f32)
    rope = np.stack([np.concatenate([np.cos(a)] * 2, 1), np.concatenate([-np.sin(a), np.sin(a)], 1)])
    rope = rope.reshape(2, T, P, DR).transpose(2, 0, 1, 3).reshape(P, 2 * T * DR)

    i = np.arange(P)
    mask = np.stack([(i[:, None] >> (b + 1) == i[None, :] >> (b + 1)) & (i[:, None] >> b != i[None, :] >> b)
                     for b in range(LEVELS - 1)], 1).reshape(P, -1)

    cst = np.zeros((P, NCST), f32)
    cst[:, :P] = np.eye(P)
    cst[:, I_D:I_CQ] = D * EPS
    cst[:, I_CQ:I_M] = [1 / 256, 1 / 128, 1 / 256, 1 / 128]
    cst[:, I_M:I_H] = 1 / 512
    cst[:, I_H:I_G] = 1 / 256
    cst[:, I_G:I_EPS] = 1 / 64
    cst[:, I_EPS:I_POW] = EPS
    cst[:, I_POW:] = -0.5
    dft = np.concatenate([dft, inv], 1)
    return {n: a.astype(f32) for n, a in dict(cst=cst, dft=dft, rope=rope, win=win, z=z.T, fil_dft=fil_dft, mask=mask).items()}


def kernel(**inputs):
    import concourse.bacc as _bacc
    from concourse import mybir as _mybir
    from concourse.bass_utils import run_bass_kernel_spmd as _run

    a = {k: np.asarray(v) for k, v in inputs.items()}
    k = shape_constants()
    f32 = np.float32
    slots, par = [], np.zeros((P, DEPTH + 1, NPAR), f32)
    fil, gates = np.zeros((DEPTH, P, NFIL), f32), np.zeros((DEPTH, 32, 2 * P), f32)
    for l in range(DEPTH):
        slots += ffn_slots(a["ffn1_w_gate"][l], a["ffn1_w_up"][l], a["ffn1_w_down"][l])
        slots += mix_slots(a["w_in"][l], a["mla_w_uq"][l], a["mla_w_ukv"][l], a["w_out"][l])
        slots += ffn_slots(a["ffn2_w_gate"][l], a["ffn2_w_up"][l], a["ffn2_w_down"][l])

        def tiles(v):
            return v.reshape(-1, P).T
        q = par[:, l]
        q[:, C_G1:C_GM] = tiles(a["ffn1_norm"][l])
        q[:, C_GM:C_G2] = tiles(a["mix_norm"][l])
        q[:, C_G2:C_QN] = tiles(a["ffn2_norm"][l])
        q[:, C_QN:C_KVN] = tiles(a["mla_q_norm"][l])
        q[:, C_KVN:C_GO] = tiles(a["mla_kv_norm"][l])
        q[:, C_GO:C_W0] = tiles(np.concatenate([a["hy_out_norm"][l], a["mla_out_norm"][l]] + [a["gla_head_norm"][l]] * 4))
        for n, c in enumerate((C_W0, C_W1, C_W2)):
            q[:, c:c + 6] = tiles(a["hy_conv_w"][l, n])
        q[:, C_CB:C_BG] = tiles(a["hy_conv_b"][l])
        q[:, C_BG] = a["gla_b_gate_fwd"][l]
        q[:, C_BG + 1] = a["gla_b_gate_bwd"][l]
        for c, n in ((C_FB1, "b1"), (C_FF1, "freq1"), (C_FB2, "b2"), (C_FF2, "freq2")):
            q[:HYF, c] = a["hy_filt_" + n][l]
        g = fil[l]
        g[:, F_WIN:F_Z] = k["win"]
        g[:HYE, F_Z:F_W1] = k["z"]
        g[:HYE, F_W1:F_W2] = a["hy_filt_w1"][l]
        g[:HYF, F_W2:F_W3] = a["hy_filt_w2"][l]
        g[:HYF, F_W3:F_DFT] = a["hy_filt_w3"][l]
        g[:, F_DFT:F_SKIP] = k["fil_dft"]
        g[0, F_SKIP:] = a["hy_skip"][l].reshape(-1)
        gates[l, 0:16, 0:P] = a["gla_w_gate_fwd"][l]
        gates[l, 16:32, P:] = a["gla_w_gate_bwd"][l]
    arrays = {"x": a["x"][0], "w": np.stack(slots), "par": par.reshape(P, -1), "cst": k["cst"], "fil": fil, "gates": gates,
              "dft": k["dft"], "rope": k["rope"], "mask": k["mask"], "fin": a["final_norm"]}
    arrays = {f"in_{n}_dram": np.ascontiguousarray(v) for n, v in arrays.items()}
    nc = _bacc.Bacc("TRN2", target_bir_lowering=False, num_devices=1)
    args = [nc.dram_tensor(n, v.shape, _mybir.dt.from_np(v.dtype), kind="ExternalInput").ap() for n, v in arrays.items()]
    args.append(nc.dram_tensor("out_0_dram", (SEQ, D), F32, kind="ExternalOutput").ap())
    build(nc, *args)
    r = _run(nc, [arrays], core_ids=[0])
    return r.results[0]["out_0_dram"].reshape(1, SEQ, D)
```

```python
from contextlib import ExitStack
import math

import numpy as np
import concourse.bass as bass
from concourse import mybir

F32 = mybir.dt.float32
F32R = mybir.dt.float32r
U8 = mybir.dt.uint8
ACT = mybir.ActivationFunctionType
ALU = mybir.AluOpType
AX = mybir.AxisListType

P = 128
SEQ, D, FF, DEPTH = 256, 1024, 2816, 2
T = SEQ // P
KD = D // P
CH = FF // 256
RING = 3
SLOT = 4 * 512
FFN_SLOTS = 3 * CH
MIX = FFN_SLOTS
MIX_SLOTS = 15
FFN2 = MIX + MIX_SLOTS
SLOTS = FFN2 + FFN_SLOTS
S_G3, S_G2, S_G1, S_G4, S_UQN, S_UQR, S_UKV, S_WO = (MIX + n for n in (0, 2, 4, 6, 8, 9, 10, 11))
assert SLOTS % RING == 0 and CH % 2 == 1

HYW, HYE, HYF = 256, 33, 64
H, DN, DR, DV = 4, 128, 64, 128
GDK, GDV = 32, 64
LEVELS = 8
EPS = 1e-6
MLA_SCALE = float(DN + DR) ** -0.5

(C_G1, C_GM, C_G2, C_QN, C_KVN, C_GO, C_W0, C_W1, C_W2, C_CB, C_BG, C_FB1, C_FF1, C_FB2, C_FF2,
 NPAR) = np.cumsum([0, 8, 8, 8, 2, 1, 8, 6, 6, 6, 6, 2, 1, 1, 1, 1]).tolist()
I_D, I_CQ, I_M, I_H, I_G, I_EPS, I_POW, NCST = (128 + np.cumsum([0, 2, 4, 2, 2, 8, 8, 8])).tolist()
F_WIN, F_Z, F_W1, F_W2, F_W3, F_DFT, F_SKIP, NFIL = np.cumsum([0, 1024, 256, 64, 64, 1024, 768, 512]).tolist()
T_SS, T_R, T_S4, T_R4, T_SM, T_RM, T_SH, T_RH, T_S8, T_R8, T_MX, T_RS, T_RR, NST = np.cumsum(
    [0, 4, 2, 4, 4, 2, 2, 2, 2, 8, 8, 8, 8, 8]).tolist()
TWO_PI_A, TWO_PI_B = 6.28125, 2029.0 / 2 ** 20
TWO_PI_C = 2 * math.pi - TWO_PI_A - TWO_PI_B
ROUND = 1.5 * 2 ** 23
PI_F = 3.1415925
Y_TILES = [(0, 1), (2, 3), (4, 5), (6, 7)]
Y_BANKS = [5, 4, 5, 4]
TAP_BANKS = [5, 6, 4, 7]
NORMS = 3
TURNS = 4
LINKS = {"dve": 24, "pool": 49, "act": 2, "pool_start": 4}


class Mark:

    def __init__(self, sem, per):
        self.sem, self.per = sem, per

    def at(self, l, v=1):
        return l * self.per + v


def pos(n):
    return (n + 1) % RING


def build(nc, x_d, w_d, par_d, cst_d, fil_d, gate_d, dft_d, rope_d, mask_d, fin_d, out_d):
    with ExitStack() as ctx:
        def sb(name, shape, dt=F32):
            return ctx.enter_context(nc.sbuf_tensor(name, shape, dt))

        def mark(name, per):
            return Mark(ctx.enter_context(nc.semaphore(name)), per)

        raw = [sb(f"w_raw{i}", [P, 4, 512]) for i in range(RING)]
        WH = [sb(f"w_high{i}", [P, 4, 512], F32R) for i in range(RING)]
        WL = [sb(f"w_low{i}", [P, 4, 512], F32R) for i in range(RING)]
        x = sb("x", [P, T, D])
        xn = sb("x_normed", [P, T, D])
        XH = sb("xT_high", [P, KD, SEQ], F32R)
        XL = sb("xT_low", [P, KD, SEQ], F32R)
        sg = sb("silu_gate", [P, 2, SEQ])
        hid = sb("hidden", [P, 2, SEQ])
        HHB = [sb(f"hT_high{i}", [P, 2, SEQ], F32R) for i in range(2)]
        HLB = [sb(f"hT_low{i}", [P, 2, SEQ], F32R) for i in range(2)]
        HH, HL = HHB[0], HLB[0]
        diag = sb("diag_rstd", [P, T, P])
        KVH = sb("kvT_high", [P, SEQ], F32R)
        KVL = sb("kvT_low", [P, SEQ], F32R)
        par_next = sb("par_next", [P, DEPTH, NPAR])
        par = sb("par", [P, NPAR])
        cst = sb("constants", [P, NCST])
        ident = cst[:, 0:P]
        st = sb("statistics", [P, NST])
        dft = sb("dft", [P, T, 512])
        idft = sb("inverse_dft", [P, 4, SEQ])
        rope = sb("rope", [P, 2, T, DR])
        mask = sb("level_masks", [P, LEVELS - 1, P], U8)
        wg = sb("gate_weights", [P, 2, P])
        KA = sb("filter_re", [P, 2, 512])
        KI = sb("filter_im", [P, 2, 512])
        KB = sb("filter_nyquist", [P, 512])
        scratch = sb("mixer_scratch", [P, 16896])
        cols = [0]

        def view(*dims, at=None):
            n = int(np.prod(dims))
            a = cols[0] if at is None else at
            if at is None:
                cols[0] += n
            v = scratch[:, a:a + n]
            if len(dims) == 2:
                v = v.rearrange("p (a b) -> p a b", b=dims[1])
            if len(dims) == 3:
                v = v.rearrange("p (a b c) -> p a b c", b=dims[1], c=dims[2])
            return v

        QN, QR, KN = view(H, SEQ), view(H, SEQ), view(H, SEQ)
        VM = view(T, H * DV)
        PE_ = view(H, SEQ)
        PT = view(2, H, P)
        AD = view(H, T, P)
        AC = view(H, T, P)
        Y = view(4, SEQ)
        TT = view(4, SEQ)
        filter_cols = cols[0]
        KR = view(SEQ)
        QK = view(2, SEQ)
        G = view(4, SEQ)
        Z = scratch[:, cols[0]:cols[0] + 4 * SEQ].rearrange("p (a b c) -> p a b c", a=2, b=2)
        QKL = [view(2, SEQ), view(2, SEQ)]
        VG, RG = view(T, 256), view(T, 256)
        C = view(4, SEQ)
        NV = view(3, T, 256)
        KT = view(2, T, DR)
        assert cols[0] <= 16896, cols[0]
        fil = scratch[:, 0:NFIL]
        at = NFIL
        H1, H2 = view(SEQ, at=at), view(SEQ, at=at + SEQ)
        ARG, TURN = view(SEQ, at=at + 2 * SEQ), view(SEQ, at=at + 3 * SEQ)
        HW = view(2, T, 512, at=at + 4 * SEQ)
        HS = view(T, 512, at=at + 4 * SEQ + 2048)
        HD = view(T, 512, at=at + 4 * SEQ + 3072)
        assert at + 4 * SEQ + 4096 <= filter_cols

        PS = ctx.enter_context(nc.psum_tensor("psum", [P, 8, 512], F32))

        s_in0, s_in1, s_cst, s_par0, s_par1, s_in = (mark(n, 0) for n in (
            "x_first_half", "x_second_half", "identity_landed", "params_landed", "next_params_landed", "constants_landed"))
        landed = [mark(f"slot_landed{i}", SLOTS // RING * 16) for i in range(RING)]
        s_hi, s_lo, s_used = mark("slot_high", SLOTS), mark("slot_low", SLOTS), mark("slot_used", SLOTS)
        s_par, s_mask = mark("params_copied", 1), mark("masks_made", 0)
        s_fil1, s_fil = mark("filter_mlp_landed", 16), mark("filter_pack_landed", 64)
        s_x = mark("x_updated", 4 * NORMS)
        s_ss, s_rstd, s_dg = mark("squares_summed", 4 * NORMS), mark("rstd", 2 * NORMS), mark("rstd_diagonal", 2 * NORMS)
        s_sum = mark("bank_summed", 3 * NORMS)
        s_tr, s_xh, s_xl = (mark(n, 4 * TURNS) for n in ("turned", "turned_high", "turned_low"))
        s_silu, s_h, s_hh, s_hl = (mark(n, 4 * CH) for n in ("silu", "hidden_done", "hT_high_done", "hT_low_done"))
        s_gain, s_y, s_out = mark("final_gain", 0), mark("final_normed", 0), mark("out_landed", 0)
        f_mm, f_arg, f_sin = mark("filter_mm", 2), mark("sine_argument", 2), mark("sine", 2)
        f_w3, f_hw, f_hs = mark("filter_taps", 4), mark("taps_windowed", 4), mark("taps_summed", 1)
        k_mm, k_ev = mark("filter_dft", 5), mark("filter_dft_copied", 5)
        c_base, c_conv, c_tr, c_nat = mark("conv_centre", 6), mark("conv_done", 6), mark("conv_turned", 3), mark("conv_natural", 3)
        g_qk, g_in, g_z, g_az = mark("gla_qk", 1), mark("gate_in", 1), mark("gate_mm", 1), mark("gate_logits", 1)
        g_ln, g_g0 = mark("gate_log", 1), mark("gate_exponents", 1)
        g_e, g_lq, g_gu = mark("level_exp", LEVELS), mark("level_qk", LEVELS), mark("level_exponents", LEVELS - 1)
        g_ls, g_la = mark("level_scores", LEVELS + 1), mark("level_scores_kept", LEVELS + 1)
        g_vr = mark("gla_vr", 2)
        g_o, g_sq, g_s8, g_r8, g_y, g_r = (mark(n, 1) for n in ("gla_out", "gla_squares", "gla_sums", "gla_rstd", "gla_y", "gla_silu"))
        q_ss, q_r, q_n, q_kt, q_kr = (mark(n, 1) for n in ("latent_squares", "latent_rstd", "latent_normed", "k_rope_products", "k_rope"))
        q_tr, q_hi, q_lo, q_krt = mark("latent_turned", 2), mark("latent_high", 2), mark("latent_low", 2), mark("k_rope_turned_copied", 1)
        a_qn, a_qt, a_qr, a_qtr, a_qre = mark("q_copied", 2), mark("q_rope_products", 1), mark("q_rope", 1), mark("q_rope_turned", 1), mark("q_rope_copied", 2)
        a_kn, a_v = mark("k_copied", 2), mark("v_copied", 2)
        a_s, a_mx, a_p, a_pt, a_pte = (mark(n, 2) for n in ("scores", "score_max", "probs", "probs_turned", "probs_turned_copied"))
        a_o, a_oe = mark("attended", 2), mark("attended_scaled", 2)
        a_sq, a_r, a_y = mark("mla_squares", 2), mark("mla_rstd", 1), mark("mla_y", 1)
        h_u, h_pr, h_y, h_inv, h_z = (mark(n, 2) for n in ("hy_dft", "hy_products", "hy_spectrum", "hy_inverse", "hy_gated"))
        h_sq, h_r, h_yy = mark("hy_squares", 2), mark("hy_rstd", 1), mark("hy_y", 1)
        s_step = {n: mark(f"step_{n}", 0) for n in ("pe", "pool", "dve")}
        chain = {n: mark(f"order_{n}", LINKS[n]) for n in LINKS}
        linked = {}

        def linker(e, name):
            linked[name] = 0

            def link(l, ins):
                linked[name] += 1
                ins.then_inc(chain[name].sem, 1)
                e.wait_ge(chain[name].sem, chain[name].at(l, linked[name]))
            return link

        def hold(e, name):
            e.sem_inc(s_step[name].sem, 1)

        def used(l, n):
            return s_used.at(l, n + RING + 1)

        block = ctx.enter_context(nc.Block())

        @block.sync
        def _(e):
            def fetch(n, p):
                src = w_d[bass.ds(n, 1), :, :].rearrange("s p n -> (s p) n")
                e.dma_start(raw[p][:].rearrange("p a b -> p (a b)"), src).then_inc(landed[p].sem, 16)

            def stream(first, last):
                with e.Fori(first, last) as i:
                    for u in range(RING):
                        e.wait_ge(s_lo.sem, (i - 1) * RING + u + 1)
                        fetch(i * RING + u, pos(u))

            for t, m in ((0, s_in0), (1, s_in1)):
                e.dma_start(x[:, t, :], x_d[t * P:(t + 1) * P, :]).then_inc(m.sem, 16)
            for n in range(RING):
                fetch(n, pos(n))
            stream(1, FFN_SLOTS // RING // 2)
            for dst, src in ((dft[:].rearrange("p a b -> p (a b)"), dft_d[:, 0:1024]),
                             (idft[:].rearrange("p a b -> p (a b)"), dft_d[:, 1024:2048]),
                             (rope[:].rearrange("p a b c -> p (a b c)"), rope_d)):
                e.dma_start(dst, src).then_inc(s_in.sem, 16)
            stream(FFN_SLOTS // RING // 2, DEPTH * SLOTS // RING)
            e.wait_ge(s_lo.sem, DEPTH * SLOTS - RING + 1)
            e.dma_start(raw[pos(0)][:].rearrange("p a b -> p (a b)"), w_d[0]).then_inc(landed[pos(0)].sem, 16)
            e.wait_ge(s_x.sem, s_x.at(DEPTH - 1, 12))
            e.dma_start(C.rearrange("p a b -> p (a b)"), fin_d.rearrange("(a d) -> a d", a=1).to_broadcast([P, D])).then_inc(s_in.sem, 16)
            for t in range(T):
                for n in range(2):
                    e.wait_ge(s_y.sem, 2 * t + n + 1)
                    c = slice(n * 512, (n + 1) * 512)
                    e.dma_start(out_d[t * P:(t + 1) * P, c], xn[:, t, c]).then_inc(s_out.sem, 16)
            e.wait_ge(s_out.sem, 2 * T * 16)

        @block.gpsimd
        def _(e):
            link = linker(e, "pool")
            e.dma_start(mask[:].rearrange("p a b -> p (a b)"), mask_d).then_inc(s_mask.sem, 16)
            e.wait_ge(s_cst.sem, 16)

            def rstd(l, m, v, src, dst, inv, n, done):
                e.wait_ge(m.sem, m.at(l, v))
                a, b = st[:, src:src + n], st[:, dst:dst + n]
                link(l, e.tensor_tensor(b, a, cst[:, inv:inv + n], ALU.mult))
                link(l, e.tensor_tensor(b, b, cst[:, I_EPS:I_EPS + n], ALU.add))
                e.tensor_tensor(b, b, cst[:, I_POW:I_POW + n], ALU.pow).then_inc(done.sem, 1)

            def x_rstd(l, j, link=link):
                for t in range(T):
                    r = st[:, T_R + t:T_R + t + 1]
                    e.wait_ge(s_ss.sem, s_ss.at(l, 4 * j + 2 * t + 1))
                    link(l, e.tensor_tensor(r, st[:, T_SS + 2 * t:T_SS + 2 * t + 1], cst[:, I_D:I_D + 1], ALU.add))
                    e.wait_ge(s_ss.sem, s_ss.at(l, 4 * j + 2 * t + 2))
                    link(l, e.tensor_tensor(r, r, st[:, T_SS + 2 * t + 1:T_SS + 2 * t + 2], ALU.add))
                    e.tensor_tensor(r, r, cst[:, I_POW:I_POW + 1], ALU.pow).then_inc(s_rstd.sem, 1)

            def levels(l, b):
                B = 1 << b
                e.wait_ge(g_e.sem, g_e.at(l, b + 1))
                g = [G[:, n, :].rearrange("p (a w b) -> p a w b", w=2, b=B) for n in range(4)]
                n = SEQ // (2 * B)
                sb_, pf, sf, pb_ = g

                def add(to, side, of, oside, i, last=False):
                    o = of[:, :, oside, i:i + 1].to_broadcast([P, n, B])
                    return e.tensor_tensor(to[:, :, side, :], to[:, :, side, :], o, ALU.add)
                link(l, add(sf, 0, pf, 1, B - 1))
                link(l, add(pb_, 1, sb_, 0, 0))
                link(l, add(pf, 1, pf, 0, B - 1))
                add(sb_, 0, sb_, 1, 0).then_inc(g_gu.sem, 1)

            x_rstd(0, 0, linker(e, "pool_start"))
            with e.Fori(0, DEPTH) as l:
                e.wait_ge(s_x.sem, s_x.at(l, 4))
                for rows_, a, b in ((HYF, F_Z, F_DFT), (P, F_WIN, F_Z), (P, F_DFT, F_SKIP), (1, F_SKIP, NFIL)):
                    src = fil_d[bass.ds(l, 1), 0:rows_, a:b].rearrange("s p n -> (s p) n")
                    e.dma_start(fil[0:rows_, a:b], src).then_inc((s_fil1 if a == F_Z else s_fil).sem, 16)
                e.dma_start(wg[64:96, :, :].rearrange("p a b -> p (a b)"), gate_d[bass.ds(l, 1), :, :].rearrange("s p n -> (s p) n")).then_inc(s_fil.sem, 16)
                x_rstd(l, 1)
                for o in range(2):
                    for p in range(T):
                        e.wait_ge(f_hw.sem, f_hw.at(l, o * 2 + p + 1))
                        a, b = HW[:, o, p, 0:256], HW[:, o, p, 256:512]
                        link(l, e.tensor_tensor(HS[:, p, o * 256:(o + 1) * 256], a, b, ALU.add))
                        link(l, e.tensor_tensor(HD[:, p, o * 256:(o + 1) * 256], a, b, ALU.subtract))
                e.tensor_tensor(HS[0:1, 0, :], HS[0:1, 0, :], fil[0:1, F_SKIP:F_SKIP + 512], ALU.add).then_inc(f_hs.sem, 1)
                rstd(l, q_ss, 1, T_S4, T_R4, I_CQ, 4, q_r)
                e.wait_ge(q_kt.sem, q_kt.at(l))
                e.tensor_tensor(xn[:, :, 640:704], KT[:, 0], KT[:, 1], ALU.add).then_inc(q_kr.sem, 1)
                e.wait_ge(h_pr.sem, h_pr.at(l, 1))
                e.tensor_tensor(Y, Y, TT, ALU.add).then_inc(h_y.sem, 1)
                e.wait_ge(a_qt.sem, a_qt.at(l))
                e.tensor_tensor(xn[:, :, 768:1024], TT[:, 0:2, :], TT[:, 2:4, :], ALU.add).then_inc(a_qr.sem, 1)
                levels(l, 0)
                e.wait_ge(h_pr.sem, h_pr.at(l, 2))
                e.tensor_tensor(Y, Y, TT, ALU.add).then_inc(h_y.sem, 1)
                levels(l, 1)
                levels(l, 2)
                rstd(l, h_sq, 2, T_SH, T_RH, I_H, 2, h_r)
                for b in range(3, LEVELS - 1):
                    levels(l, b)
                rstd(l, a_sq, 2, T_SM, T_RM, I_M, 2, a_r)
                rstd(l, g_s8, 1, T_S8, T_R8, I_G, 8, g_r8)
                x_rstd(l, 2)
                x_rstd(l, NORMS)
                e.wait_ge(s_par1.sem, 16)
                e.wait_ge(s_x.sem, s_x.at(l, 4 * NORMS + 4))
                hold(e, "pool")
                e.tensor_copy(par[:], par_next[:, bass.ds(l, 1), :].rearrange("p a b -> p (a b)")).then_inc(s_par.sem, 1)
        @block.scalar
        def _(e):
            link = linker(e, "act")
            e.dma_start(cst[:], cst_d).then_inc(s_cst.sem, 16)
            e.dma_start(par[:], par_d[:, 0:NPAR]).then_inc(s_par0.sem, 16)
            e.dma_start(par_next[:].rearrange("p a b -> p (a b)"), par_d[:, NPAR:]).then_inc(s_par1.sem, 16)

            def hi(l, n, occ=None):
                p, k = (pos(n), n // RING + 1) if occ is None else occ
                e.wait_ge(landed[p].sem, l * landed[p].per + k * 16)
                e.wait_ge(s_used.sem, l * SLOTS + n + 1)
                e.activation(WH[p][:], raw[p][:], ACT.Copy).then_inc(s_hi.sem, 1)

            def squares(l, j):
                for t in range(T):
                    for n in range(2):
                        q, c = 2 * t + n, T_SS + 2 * t + n
                        e.wait_ge(s_x.sem, s_x.at(l, 4 * j + 1 + q))
                        e.activation(xn[:, t, n * 512:(n + 1) * 512], x[:, t, n * 512:(n + 1) * 512], ACT.Square,
                                     accum_out=st[:, c:c + 1]).then_inc(s_ss.sem, 1)

            def turned_high(l, j, g, bank, tiles, col):
                e.wait_ge(s_tr.sem, s_tr.at(l, 4 * j + g + 1))
                for n, k in enumerate(tiles):
                    r = e.activation(XH[:, k, :], PS[:, bank, n * SEQ:(n + 1) * SEQ], ACT.Copy, scale=par[:, col + k:col + k + 1])
                r.then_inc(s_xh.sem, 1)

            def norm(l, j, turn, col, slot):
                if j:
                    hi(l, slot)
                    squares(l, j)
                e.wait_ge(s_par.sem, s_par.at(l))
                for g in range(4):
                    turned_high(l, turn, g, g, (2 * g, 2 * g + 1), col)
                hi(l, slot + 1)

            def silu(l, q, f, pr, slot):
                e.wait_ge(s_used.sem, used(l, slot))
                e.activation(sg[:, f, :], PS[:, 4 + 2 * pr + f, 0:SEQ], ACT.Silu).then_inc(s_silu.sem, 1)

            def ht_high(l, q, f, pr):
                e.wait_ge(s_h.sem, s_h.at(l, 2 * q + f + 1))
                e.activation(HHB[pr][:, f, :], hid[:, f, :], ACT.Copy).then_inc(s_hh.sem, 1)

            def sine(l, n, dst):
                e.wait_ge(f_arg.sem, f_arg.at(l, n + 1))
                e.activation(dst[0:HYF], ARG[0:HYF], ACT.Sin).then_inc(f_sin.sem, 1)

            def ffn(l, f, base, j, turn, col):
                norm(l, j, turn, col, base)
                hi(l, base + 2); hi(l, base + 3)

                def chunk(c, pr):
                    q = f * CH + (c - 1)
                    for h in range(2):
                        silu(l, q, h, 1 - pr, base + h if c is first else base + 3 * c - 4 + h)
                        if c is not first:
                            hi(l, base + 3 * c - 1 + h, (pos(base + 2 + h), base // RING + c - 1 + (2 + h) // RING + 1))
                        ht_high(l, q, h, 1 - pr)
                    hi(l, base + 3 * c + 1, (pos(base + 1), base // RING + c + 1))
                first = 1
                chunk(first, 1)
                if f == 0:
                    sine(l, 0, H1)
                with e.Fori(0, (CH - 3) // 2) as i:
                    chunk(i * 2 + 2, 0)
                    chunk(i * 2 + 3, 1)
                chunk(CH - 1, (CH - 1) % 2)
                q, pr = f * CH + CH - 1, (CH - 1) % 2
                silu(l, q, 0, pr, base + FFN_SLOTS - 4)
                hi(l, base + FFN_SLOTS - 1)
                ht_high(l, q, 0, pr)
                silu(l, q, 1, pr, base + FFN_SLOTS - 3)
                ht_high(l, q, 1, pr)
                if f == 0:
                    sine(l, 1, H2)

            def copy(dst, src, m=None, **kw):
                r = e.activation(dst, src, ACT.Copy, **kw)
                if m is not None:
                    r.then_inc(m.sem, 1)

            def conv_centre(tile, bank, dst):
                e.activation(C[:, dst, :], PS[:, bank, 0:SEQ], ACT.Identity, scale=par[:, C_W1 + tile:C_W1 + tile + 1],
                             bias=par[:, C_CB + tile:C_CB + tile + 1]).then_inc(c_base.sem, 1)

            def natural(l, n, which, bank):
                e.wait_ge(c_tr.sem, c_tr.at(l, n))
                copy(NV[:, which].rearrange("p a b -> p (a b)"), PS[:, bank, :], c_nat)

            def level_exp(l, b):
                B = 1 << b
                if b == 0:
                    e.wait_ge(g_g0.sem, g_g0.at(l))
                else:
                    e.wait_ge(g_gu.sem, g_gu.at(l, b))
                    e.wait_ge(g_lq.sem, g_lq.at(l, b))
                for n in range(2):
                    first = G[:, 2 * n:2 * n + 1, 0:1]
                    src = bass.AP(first.tensor, first.offset, [first.ap[0], [2 * B, SEQ // (2 * B)], [SEQ + B, 2], [1, B]])
                    dst = sg[:, n, :].rearrange("p (a w b) -> p a w b", w=2, b=B)
                    r = e.activation(dst, src, ACT.Exp)
                r.then_inc(g_e.sem, 1)

            def probs(l, s):
                e.wait_ge(a_mx.sem, a_mx.at(l, s + 1))
                if s:
                    e.wait_ge(a_pt.sem, a_pt.at(l, s))
                for h in range(H):
                    c = T_MX + 4 * s + h
                    r = e.activation(PE_[:, h, :], PS[:, 4 + 2 * s + h // 2, (h % 2) * SEQ:(h % 2 + 1) * SEQ], ACT.Exp,
                                     scale=MLA_SCALE, bias=st[:, c:c + 1], accum_out=st[:, T_RS + 4 * s + h:T_RS + 4 * s + h + 1])
                r.then_inc(a_p.sem, 1)

            def probs_turned(l, s):
                e.wait_ge(a_pt.sem, a_pt.at(l, s + 1))
                if s:
                    e.wait_ge(a_o.sem, a_o.at(l, s))
                copy(PT.rearrange("p a h c -> p (a h c)"), PS[:, 4 + 2 * s:6 + 2 * s, :], a_pte)

            squares(0, 0)
            hi(0, 0)
            e.wait_ge(s_par0.sem, 16)
            e.sem_inc(s_par.sem, 1)
            with e.Fori(0, DEPTH) as l:
                ffn(l, 0, 0, 0, 0, C_G1)
                norm(l, 1, 1, C_GM, S_G3)
                hi(l, S_G2); hi(l, S_G2 + 1)
                e.wait_ge(s_used.sem, used(l, S_G3 + 1))
                for t in range(T):
                    e.activation(RG[:, t, :], PS[:, 5 + t, 0:256], ACT.Square, accum_out=st[:, T_S4 + 2 * t:T_S4 + 2 * t + 1])
                    r = e.activation(VG[:, t, 0:128], PS[:, 5 + t, 256:384], ACT.Square, accum_out=st[:, T_S4 + 2 * t + 1:T_S4 + 2 * t + 2])
                r.then_inc(q_ss.sem, 1)
                hi(l, S_G1); hi(l, S_G1 + 1)
                e.wait_ge(s_used.sem, used(l, S_G2 + 1))
                conv_centre(4, 0, 0); conv_centre(5, 1, 1)
                copy(QK[:, 0, :], PS[:, 2, 0:SEQ], scale=GDK ** -0.5)
                copy(QK[:, 1, :], PS[:, 3, 0:SEQ], g_qk)
                e.wait_ge(q_tr.sem, q_tr.at(l, 1))
                for n in range(2):
                    r = e.activation(HH[:, n, :], PS[:, 5, n * SEQ:(n + 1) * SEQ], ACT.Copy, scale=par[:, C_QN + n:C_QN + n + 1])
                r.then_inc(q_hi.sem, 1)
                e.wait_ge(q_tr.sem, q_tr.at(l, 2))
                copy(hid[64:96, 0, :], PS[64:96, 6, SEQ:2 * SEQ], g_in)
                copy(KR[0:DR, :], PS[0:DR, 6, SEQ:2 * SEQ], q_krt)
                copy(KVH[:], PS[:, 6, 0:SEQ], q_hi, scale=par[:, C_KVN:C_KVN + 1])
                for n, (dst, b) in enumerate(((KB[:], 4), (KA[:, 0, :], 2), (KA[:, 1, :], 3), (KI[:, 0, :], 0), (KI[:, 1, :], 1))):
                    e.wait_ge(k_mm.sem, k_mm.at(l, n + 1))
                    copy(dst, PS[:, b, :], k_ev)
                natural(l, 1, 2, 7)
                hi(l, S_G4)
                e.wait_ge(g_az.sem, g_az.at(l))
                link(l, e.activation(Z[:, 1], Z[:, 0], ACT.Abs))
                link(l, e.activation(Z[:, 1], Z[:, 1], ACT.Exp, scale=-1.0))
                e.activation(Z[:, 1], Z[:, 1], ACT.Ln, bias=1.0).then_inc(g_ln.sem, 1)
                hi(l, S_G4 + 1)
                e.wait_ge(s_used.sem, used(l, S_G1 + 1))
                e.wait_ge(c_tr.sem, c_tr.at(l, 1))
                for n in range(4):
                    conv_centre(n, n, n)
                hi(l, S_UQN)
                natural(l, 2, 0, 7)
                natural(l, 3, 1, 4)
                hi(l, S_UQR)
                level_exp(l, 0)
                e.wait_ge(s_used.sem, used(l, S_G4 + 1))
                for t in range(T):
                    copy(VG[:, t, :], PS[:, 5 + t, 0:256])
                    copy(RG[:, t, :], PS[:, 5 + t, 256:512], g_vr)
                hi(l, S_UKV)
                e.wait_ge(s_used.sem, used(l, S_UQN))
                for n in range(2):
                    copy(QN[:, 2 * n:2 * n + 2, :].rearrange("p a b -> p (a b)"), PS[:, 2 + n, :], a_qn)
                hi(l, S_WO)
                e.wait_ge(s_used.sem, used(l, S_UKV))
                copy(KN[:, 0:2, :].rearrange("p a b -> p (a b)"), PS[:, 4, :], a_kn)
                copy(KN[:, 2:4, :].rearrange("p a b -> p (a b)"), PS[:, 1, :], a_kn)
                copy(VM[:, 0, :], PS[:, 5, :], a_v)
                copy(VM[:, 1, :], PS[:, 6, :], a_v)
                e.wait_ge(a_qtr.sem, a_qtr.at(l))
                for n in range(2):
                    copy(QR[0:DR, 2 * n:2 * n + 2, :].rearrange("p a b -> p (a b)"), PS[0:DR, 2 + n, :], a_qre)
                hi(l, S_WO + 1)
                e.wait_ge(g_ls.sem, g_ls.at(l, 1))
                copy(AD.rearrange("p h t c -> p h (t c)"), PS[:, 0:4, 0:256], g_la)
                probs(l, 0)
                level_exp(l, 1)
                hi(l, S_WO + 2)
                level_exp(l, 2)
                e.wait_ge(h_z.sem, h_z.at(l, 2))
                for t in range(T):
                    e.activation(TT[:, t, :], xn[:, t, 0:256], ACT.Square, accum_out=st[:, T_SH + t:T_SH + t + 1]).then_inc(h_sq.sem, 1)
                probs_turned(l, 0)
                level_exp(l, 3)
                level_exp(l, 4)
                turned_high(l, 2, 0, Y_BANKS[0], Y_TILES[0], C_GO)
                level_exp(l, 5)
                probs(l, 1)
                level_exp(l, 6)
                probs_turned(l, 1)
                level_exp(l, 7)
                for s in range(T):
                    e.wait_ge(a_oe.sem, a_oe.at(l, s + 1))
                    e.activation(C[:, 2 * s:2 * s + 2, :].rearrange("p a b -> p (a b)"), xn[:, s, 256:768], ACT.Square,
                                 accum_out=st[:, T_SM + s:T_SM + s + 1]).then_inc(a_sq.sem, 1)
                e.wait_ge(g_ls.sem, g_ls.at(l, LEVELS + 1))
                copy(AC.rearrange("p h t c -> p h (t c)"), PS[:, 4:8, 0:256], g_la)
                for g in range(1, 3):
                    turned_high(l, 2, g, Y_BANKS[g], Y_TILES[g], C_GO)
                e.wait_ge(g_o.sem, g_o.at(l))
                e.activation(sg[:].rearrange("p a b -> p (a b)"), PS[:, 7, :], ACT.Square).then_inc(g_sq.sem, 1)
                e.activation(RG, RG, ACT.Silu).then_inc(g_r.sem, 1)
                hi(l, S_WO + 3)
                turned_high(l, 2, 3, Y_BANKS[3], Y_TILES[3], C_GO)
                ffn(l, 1, FFN2, 2, 3, C_G2)
                hi(l, SLOTS)
                squares(l, NORMS)

        @block.vector
        def _(e):
            link = linker(e, "dve")

            def lo(l, n, p=None):
                p = pos(n) if p is None else p
                e.wait_ge(s_hi.sem, s_hi.at(l, n + 1))
                e.tensor_tensor(WL[p][:], raw[p][:], WH[p][:].bitcast(F32), ALU.subtract).then_inc(s_lo.sem, 1)

            def turned_low(l, j, g, bank, tiles, col):
                e.wait_ge(s_xh.sem, s_xh.at(l, 4 * j + g + 1))
                for n, k in enumerate(tiles):
                    r = e.scalar_tensor_tensor(out=XL[:, k, :], in0=PS[:, bank, n * SEQ:(n + 1) * SEQ], scalar=par[:, col + k:col + k + 1],
                                               in1=XH[:, k, :].bitcast(F32), op0=ALU.mult, op1=ALU.subtract)
                r.then_inc(s_xl.sem, 1)

            def diagonal(l, j, t):
                e.wait_ge(s_rstd.sem, s_rstd.at(l, 2 * j + t + 1))
                e.tensor_scalar(diag[:, t, :], ident, st[:, T_R + t:T_R + t + 1], float(D) ** 0.5, ALU.mult, ALU.mult).then_inc(s_dg.sem, 1)

            def norm_low(l, turn, col):
                for g in range(4):
                    turned_low(l, turn, g, g, (2 * g, 2 * g + 1), col)

            def gate(l, q, f, pr):
                e.wait_ge(s_silu.sem, s_silu.at(l, 2 * q + f + 1))
                e.tensor_tensor(hid[:, f, :], sg[:, f, :], PS[:, 4 + 2 * pr + f, SEQ:2 * SEQ], ALU.mult).then_inc(s_h.sem, 1)

            def ht_low(l, q, f, pr):
                e.wait_ge(s_hh.sem, s_hh.at(l, 2 * q + f + 1))
                e.tensor_tensor(HLB[pr][:, f, :], hid[:, f, :], HHB[pr][:, f, :].bitcast(F32), ALU.subtract).then_inc(s_hl.sem, 1)

            def update(l, slot, scale, j):
                for t in range(T):
                    for n in range(2):
                        if t * n:
                            if j != 0:
                                diagonal(l, j + 1, 0)
                            e.wait_ge(s_used.sem, used(l, slot))
                        else:
                            e.wait_ge(s_sum.sem, s_sum.at(l, 3 * j + 2 * t + n + 1))
                        xs = x[:, t, n * 512:(n + 1) * 512]
                        e.scalar_tensor_tensor(out=xs, in0=PS[:, t * 2 + n, :], scalar=scale, in1=xs, op0=ALU.mult, op1=ALU.add).then_inc(s_x.sem, 1)
                if j != 0:
                    diagonal(l, j + 1, 1)

            def argument(l, n, bank, b, f):
                e.wait_ge(f_mm.sem, f_mm.at(l, n + 1))
                a, t = ARG[0:HYF], TURN[0:HYF]
                link(l, e.tensor_scalar(a, PS[0:HYF, bank, 0:SEQ], par[0:HYF, b:b + 1], par[0:HYF, f:f + 1], ALU.add, ALU.mult))
                link(l, e.tensor_scalar(t, a, 1 / (2 * math.pi), ROUND, ALU.mult, ALU.add))
                link(l, e.tensor_scalar(t, t, -ROUND, None, ALU.add))
                for c in (TWO_PI_A, TWO_PI_B, TWO_PI_C):
                    link(l, e.scalar_tensor_tensor(out=a, in0=t, scalar=-c, in1=a, op0=ALU.mult, op1=ALU.add))
                e.tensor_scalar(a, a, PI_F, -PI_F, ALU.min, ALU.max).then_inc(f_arg.sem, 1)

            def ffn(l, f, base, j, turn, col):
                norm_low(l, turn, col)
                lo(l, base + 1)
                lo(l, base + 2); lo(l, base + 3)

                def chunk(c, pr):
                    q = f * CH + (c - 1)
                    for h in range(2):
                        gate(l, q, h, 1 - pr)
                        if c is not first:
                            lo(l, base + 3 * c - 1 + h, pos(base + 2 + h))
                        ht_low(l, q, h, 1 - pr)
                    lo(l, base + 3 * c + 1, pos(base + 1))
                first = 1
                if f == 0:
                    argument(l, 0, 7, C_FB1, C_FF1)
                chunk(first, 1)
                with e.Fori(0, (CH - 3) // 2) as i:
                    chunk(i * 2 + 2, 0)
                    chunk(i * 2 + 3, 1)
                chunk(CH - 1, (CH - 1) % 2)
                q, pr = f * CH + CH - 1, (CH - 1) % 2
                gate(l, q, 0, pr)
                lo(l, base + FFN_SLOTS - 1)
                ht_low(l, q, 0, pr)
                gate(l, q, 1, pr)
                ht_low(l, q, 1, pr)
                if f == 0:
                    argument(l, 1, 7, C_FB2, C_FF2)
                    lo(l, S_G3)
                else:
                    lo(l, SLOTS)
                update(l, base + FFN_SLOTS - 1, 0.5, 2 * f)

            def taps(l, n, tile, bank, dst):
                e.wait_ge(c_base.sem, c_base.at(l, n))
                link(l, e.scalar_tensor_tensor(out=C[:, dst, 1:SEQ], in0=PS[:, bank, 0:SEQ - 1], scalar=par[:, C_W0 + tile:C_W0 + tile + 1],
                                               in1=C[:, dst, 1:SEQ], op0=ALU.mult, op1=ALU.add))
                e.scalar_tensor_tensor(out=C[:, dst, 0:SEQ - 1], in0=PS[:, bank, 1:SEQ], scalar=par[:, C_W2 + tile:C_W2 + tile + 1],
                                       in1=C[:, dst, 0:SEQ - 1], op0=ALU.mult, op1=ALU.add).then_inc(c_conv.sem, 1)

            def level_qk(l, b):
                e.wait_ge(g_e.sem, g_e.at(l, b + 1))
                if b >= 2:
                    e.wait_ge(g_ls.sem, g_ls.at(l, b))
                e.tensor_tensor(QKL[b % 2], QK, sg[:], ALU.mult).then_inc(g_lq.sem, 1)

            def level_keep(l, b, bank=0):
                e.wait_ge(g_ls.sem, g_ls.at(l, b + 2))
                if b == 0:
                    e.wait_ge(g_la.sem, g_la.at(l, 1))
                hold(e, "dve")
                m = mask[:, b, :]
                m = bass.AP(m.tensor, m.offset, [m.ap[0], [0, H], [0, T], [1, P]])
                e.copy_predicated(AD, m, PS[:, bank:bank + 4, 0:256].rearrange("p h (t c) -> p h t c", t=T)).then_inc(g_la.sem, 1)

            def score_max(l, s):
                e.wait_ge(a_s.sem, a_s.at(l, s + 1))
                c = T_MX + 4 * s
                link(l, e.tensor_reduce(st[:, c:c + 4], PS[:, 4 + 2 * s:6 + 2 * s, :].rearrange("p b (h k) -> p (b h) k", h=2), AX.X, ALU.max))
                e.tensor_scalar(st[:, c:c + 4], st[:, c:c + 4], -MLA_SCALE, None, ALU.mult).then_inc(a_mx.sem, 1)

            def attended(l, s):
                e.wait_ge(a_o.sem, a_o.at(l, s + 1))
                a, b = T_RS + 4 * s, T_RR + 4 * s
                link(l, e.reciprocal(st[:, b:b + 4], st[:, a:a + 4]))
                r = st[:, b:b + 4]
                r = bass.AP(r.tensor, r.offset, [r.ap[0], [1, H], [0, DV]])
                e.tensor_tensor(xn[:, s, 256:768].rearrange("p (h d) -> p h d", h=H), PS[:, 4 + 2 * s, :].rearrange("p (h d) -> p h d", h=H),
                                r, ALU.mult).then_inc(a_oe.sem, 1)

            def products(l, o, b):
                e.wait_ge(h_u.sem, h_u.at(l, o + 1))
                if o:
                    e.wait_ge(h_inv.sem, h_inv.at(l, o))
                c = slice(o * 256, (o + 1) * 256)
                ur = PS[:, b, :].rearrange("p (m n) -> p m n", m=2)
                ui = PS[:, b + 1, :].rearrange("p (m n) -> p m n", m=2)
                e.tensor_tensor(Y[:, 0:2, :], ur, KA[:, :, c], ALU.mult)
                e.scalar_tensor_tensor(out=TT[:, 0:2, :], in0=ui, scalar=-1.0, in1=KI[:, :, c], op0=ALU.mult, op1=ALU.mult)
                e.tensor_tensor(Y[:, 2, :], ui[:, 0, :], KB[:, c], ALU.mult)
                e.tensor_tensor(Y[:, 3, :], ui[:, 1, :], KA[:, 1, c], ALU.mult)
                e.tensor_tensor(TT[:, 2:4, :], ur, KI[:, :, c], ALU.mult).then_inc(h_pr.sem, 1)

            def gated(l, o, b):
                e.wait_ge(h_inv.sem, h_inv.at(l, o + 1))
                dst = NV[:, 0] if o == 0 else xn[:, :, 0:256]
                e.tensor_tensor(dst, PS[:, b, :].rearrange("p (t n) -> p t n", t=T), NV[:, 1 + o], ALU.mult).then_inc(h_z.sem, 1)

            e.wait_ge(s_in0.sem, 16)
            e.sem_inc(s_x.sem, 2)
            e.wait_ge(s_in1.sem, 16)
            e.sem_inc(s_x.sem, 2)
            e.wait_ge(s_cst.sem, 16)
            for t in range(T):
                diagonal(0, 0, t)
            lo(0, 0)
            with e.Fori(0, DEPTH) as l:
                ffn(l, 0, 0, 0, 0, C_G1)
                e.wait_ge(s_in.sem, 16 * N_IN)
                e.wait_ge(s_mask.sem, 16)
                e.wait_ge(s_fil.sem, s_fil.at(l, 64))

                def window(o, p):
                    e.wait_ge(f_w3.sem, f_w3.at(l, o * 2 + p + 1))
                    e.tensor_tensor(HW[:, o, p, :], PS[:, TAP_BANKS[o * 2 + p], :], fil[:, F_WIN + p * 512:F_WIN + (p + 1) * 512],
                                    ALU.mult).then_inc(f_hw.sem, 1)
                window(0, 0)
                diagonal(l, 1, 0)
                window(0, 1)
                diagonal(l, 1, 1)
                norm_low(l, 1, C_GM)
                window(1, 0); window(1, 1)
                lo(l, S_G3 + 1)
                lo(l, S_G2); lo(l, S_G2 + 1)
                e.wait_ge(s_used.sem, used(l, S_G3 + 1))
                e.wait_ge(q_r.sem, q_r.at(l))
                e.tensor_copy(xn[:, :, 704:736], PS[:, 5:7, 448:480])
                for t in range(T):
                    for n, (a, b) in enumerate(((0, 256), (256, 384))):
                        c = T_R4 + 2 * t + n
                        r = e.tensor_scalar(xn[:, t, 256 + a:256 + b], PS[:, 5 + t, a:b], st[:, c:c + 1], None, ALU.mult)
                r.then_inc(q_n.sem, 1)
                kr = PS[:, 5:7, 384:448]
                e.tensor_tensor(KT[:, 0], kr, rope[:, 0], ALU.mult)
                e.tensor_tensor(KT[:, 1, :, 0:32], kr[:, :, 32:64], rope[:, 1, :, 0:32], ALU.mult)
                e.tensor_tensor(KT[:, 1, :, 32:64], kr[:, :, 0:32], rope[:, 1, :, 32:64], ALU.mult).then_inc(q_kt.sem, 1)
                lo(l, S_G1)
                taps(l, 1, 4, 0, 0); taps(l, 2, 5, 1, 1)
                e.wait_ge(q_hi.sem, q_hi.at(l, 1))
                for n in range(2):
                    r = e.scalar_tensor_tensor(out=HL[:, n, :], in0=PS[:, 5, n * SEQ:(n + 1) * SEQ], scalar=par[:, C_QN + n:C_QN + n + 1],
                                               in1=HH[:, n, :].bitcast(F32), op0=ALU.mult, op1=ALU.subtract)
                r.then_inc(q_lo.sem, 1)
                e.wait_ge(q_hi.sem, q_hi.at(l, 2))
                e.scalar_tensor_tensor(out=KVL[:], in0=PS[:, 6, 0:SEQ], scalar=par[:, C_KVN:C_KVN + 1],
                                       in1=KVH[:].bitcast(F32), op0=ALU.mult, op1=ALU.subtract).then_inc(q_lo.sem, 1)
                lo(l, S_G1 + 1)
                e.wait_ge(g_z.sem, g_z.at(l))
                for d in range(2):
                    r = e.tensor_scalar(Z[:, 0, d, :], PS[:, 7, d * SEQ:(d + 1) * SEQ], par[:, C_BG + d:C_BG + d + 1], None, ALU.add)
                r.then_inc(g_az.sem, 1)
                lo(l, S_G4)
                e.memset(G[:, 2:4, :], 0.0)
                e.wait_ge(g_ln.sem, g_ln.at(l))
                link(l, e.tensor_scalar(Z[:, 0], Z[:, 0], 0.0, 1 / 16, ALU.min, ALU.mult))
                e.scalar_tensor_tensor(out=G[:, 1, :], in0=Z[:, 1, 0, :], scalar=-1 / 16, in1=Z[:, 0, 0, :], op0=ALU.mult, op1=ALU.add)
                e.scalar_tensor_tensor(out=G[:, 0, :], in0=Z[:, 1, 1, :], scalar=-1 / 16, in1=Z[:, 0, 1, :], op0=ALU.mult, op1=ALU.add).then_inc(g_g0.sem, 1)
                lo(l, S_G4 + 1)
                for n in range(4):
                    taps(l, 3 + n, n, n, n)
                lo(l, S_UQN)
                lo(l, S_UQR)
                lo(l, S_UKV)
                products(l, 0, 0)
                e.wait_ge(s_used.sem, used(l, S_UQR))
                e.wait_ge(h_y.sem, h_y.at(l, 1))
                q = PS[:, 7, :].rearrange("p (t h d) -> p t h d", t=T, h=H)

                def rp(n, a, b):
                    r = rope[:, n, :, a:b]
                    return bass.AP(r.tensor, r.offset, [r.ap[0], [DR, T], [0, H], [1, b - a]])
                t1 = TT[:, 0:2, :].rearrange("p t (h d) -> p t h d", h=H)
                t2 = TT[:, 2:4, :].rearrange("p t (h d) -> p t h d", h=H)
                e.tensor_tensor(t1, q, rp(0, 0, 64), ALU.mult)
                e.tensor_tensor(t2[:, :, :, 0:32], q[:, :, :, 32:64], rp(1, 0, 32), ALU.mult)
                e.tensor_tensor(t2[:, :, :, 32:64], q[:, :, :, 0:32], rp(1, 32, 64), ALU.mult).then_inc(a_qt.sem, 1)
                gated(l, 0, 0)
                level_qk(l, 0)
                lo(l, S_WO)
                e.wait_ge(a_qr.sem, a_qr.at(l))
                products(l, 1, 6)
                score_max(l, 0)
                lo(l, S_WO + 1)
                level_qk(l, 1)
                level_keep(l, 0)
                gated(l, 1, 6)
                level_qk(l, 2)
                level_keep(l, 1)
                level_qk(l, 3)
                e.wait_ge(h_r.sem, h_r.at(l))
                for t in range(T):
                    v = xn[:, t, 0:256]
                    r = e.tensor_scalar(v, v, st[:, T_RH + t:T_RH + t + 1], None, ALU.mult)
                r.then_inc(h_yy.sem, 1)
                level_keep(l, 2)
                level_qk(l, 4)
                level_keep(l, 3)
                level_qk(l, 5)
                score_max(l, 1)
                level_keep(l, 4)
                turned_low(l, 2, 0, Y_BANKS[0], Y_TILES[0], C_GO)
                attended(l, 0)
                level_qk(l, 6)
                level_keep(l, 5)
                lo(l, S_WO + 2)
                attended(l, 1)
                level_qk(l, 7)
                level_keep(l, 6, 4)
                e.wait_ge(a_r.sem, a_r.at(l))
                for t in range(T):
                    v = xn[:, t, 256:768]
                    r = e.tensor_scalar(v, v, st[:, T_RM + t:T_RM + t + 1], None, ALU.mult)
                r.then_inc(a_y.sem, 1)
                for g in range(1, 3):
                    turned_low(l, 2, g, Y_BANKS[g], Y_TILES[g], C_GO)
                e.wait_ge(g_sq.sem, g_sq.at(l))
                e.tensor_reduce(st[:, T_S8:T_S8 + 8], sg[:].rearrange("p t (h d) -> p (t h) d", d=GDV), AX.X, ALU.add).then_inc(g_s8.sem, 1)
                e.wait_ge(g_r8.sem, g_r8.at(l))
                r8 = st[:, T_R8:T_R8 + 8]
                r8 = bass.AP(r8.tensor, r8.offset, [r8.ap[0], [1, 8], [0, GDV]])
                og = hid[:].rearrange("p t (h d) -> p (t h) d", d=GDV)
                link(l, e.tensor_tensor(og, PS[:, 7, :].rearrange("p (n d) -> p n d", d=GDV), r8, ALU.mult))
                e.wait_ge(g_r.sem, g_r.at(l))
                e.tensor_tensor(xn[:, :, 768:1024], hid[:], RG, ALU.mult).then_inc(g_y.sem, 1)
                lo(l, S_WO + 3)
                turned_low(l, 2, 3, Y_BANKS[3], Y_TILES[3], C_GO)
                lo(l, FFN2)
                update(l, S_WO + 3, 1.0, 1)
                ffn(l, 1, FFN2, 2, 3, C_G2)
            e.wait_ge(s_in.sem, 16 * (N_IN + 1))
            gain = C.rearrange("p a b -> p (a b)")
            e.tensor_scalar(gain, gain, float(D) ** 0.5, None, ALU.mult).then_inc(s_gain.sem, 1)
            e.wait_ge(s_gain.sem, 1)
            for t in range(T):
                for n in range(2):
                    c = slice(n * 512, (n + 1) * 512)
                    e.scalar_tensor_tensor(out=xn[:, t, c], in0=x[:, t, c], scalar=st[:, T_R + t:T_R + t + 1], in1=gain[:, c],
                                           op0=ALU.mult, op1=ALU.mult).then_inc(s_y.sem, 1)

        @block.tensor
        def _(e):
            e.sem_inc(s_used.sem, RING)

            def passes(out, ah, al, bh, bl, start, stop):
                e.matmul(out, ah, bh, start=start, stop=False)
                e.matmul(out, ah, bl, start=False, stop=False)
                return e.matmul(out, al, bh, start=False, stop=stop)

            def turn_group(l, j, g, bank, tiles):
                for n, k in enumerate(tiles):
                    for t in range(T):
                        r = e.transpose(PS[:, bank, n * SEQ + t * P:n * SEQ + (t + 1) * P], xn[:, t, k * P:(k + 1) * P], ident)
                r.then_inc(s_tr.sem, 1)

            def norm(l, j, turn):
                for t in range(T):
                    e.wait_ge(s_dg.sem, s_dg.at(l, 2 * j + t + 1))
                    for k in range(KD):
                        if t == 0 and k == 6:
                            e.wait_ge(s_x.sem, s_x.at(l, 4 * j + 4))
                        r = e.matmul(PS[:, k // 2, (k % 2) * SEQ + t * P:(k % 2) * SEQ + (t + 1) * P], x[:, t, k * P:(k + 1) * P], diag[:, t, :],
                                     start=True, stop=True)
                        if t == 1 and k % 2:
                            r.then_inc(s_tr.sem, 1)

            def x_tile(l, turn, k, first):
                if first and k % 2 == 0:
                    e.wait_ge(s_xl.sem, s_xl.at(l, 4 * turn + k // 2 + 1))

            def rows(l, turn, n, half, width, banks, inc=None):
                p = pos(n)
                e.wait_ge(s_lo.sem, s_lo.at(l, n + 1))
                for t in range(T):
                    for kk in range(4):
                        k = half * 4 + kk
                        x_tile(l, turn, k, t == 0)
                        r = passes(PS[:, banks[t], 0:width], XH[:, k, t * P:(t + 1) * P], XL[:, k, t * P:(t + 1) * P],
                                   WH[p][:, kk, 0:width], WL[p][:, kk, 0:width], k == 0, k == KD - 1)
                    if inc is not None and t == 0:
                        r.then_inc(inc.sem, 1)
                return r

            def columns(l, turn, n, half, tiles):
                p = pos(n)
                e.wait_ge(s_lo.sem, s_lo.at(l, n + 1))
                for kk in range(4):
                    k = half * 4 + kk
                    x_tile(l, turn, k, True)
                    for c, b in tiles:
                        r = passes(PS[:, b, 0:SEQ], WH[p][:, kk, c:c + P], WL[p][:, kk, c:c + P], XH[:, k, :], XL[:, k, :], k == 0, k == KD - 1)
                return r

            def down(l, n, p, q, pr, first, last, f):
                e.wait_ge(s_lo.sem, s_lo.at(l, n + 1))
                order = [(h, t) for t in range(T) for h in range(2)] if last else [(h, t) for h in range(2) for t in range(T)]
                for h, t in order:
                    if t == 0:
                        e.wait_ge(s_hl.sem, s_hl.at(l, 2 * q + h + 1))
                    for m in range(2):
                        r = passes(PS[:, t * 2 + m, :], HHB[pr][:, h, t * P:(t + 1) * P], HLB[pr][:, h, t * P:(t + 1) * P],
                                   WH[p][:, h * 2 + m, :], WL[p][:, h * 2 + m, :], first and h == 0, last and h == 1)
                        if last and h == 1 and t * m == 0:
                            r.then_inc(s_sum.sem, 1)
                r.then_inc(s_used.sem, 1)

            def gate_up(l, turn, n, p, half, pr, first):
                e.wait_ge(s_lo.sem, s_lo.at(l, n + 1))
                for g in range(2):
                    for k in range(KD):
                        if first:
                            x_tile(l, turn, k, g == 0)
                        a = slice((k % 2) * 256 + g * P, (k % 2) * 256 + (g + 1) * P)
                        r = passes(PS[:, 4 + 2 * pr + half, g * SEQ:(g + 1) * SEQ], WH[p][:, k // 2, a], WL[p][:, k // 2, a],
                                   XH[:, k, :], XL[:, k, :], k == 0, k == KD - 1)
                r.then_inc(s_used.sem, 1)

            def filter_mm(l, n, w, src, rows_, bank):
                if n == 0:
                    e.wait_ge(s_fil1.sem, s_fil1.at(l, 16))
                else:
                    e.wait_ge(f_sin.sem, f_sin.at(l, n))
                hold(e, "pe")
                e.matmul(PS[0:HYF, bank, 0:SEQ], fil[0:rows_, w:w + HYF], src[0:rows_], start=True, stop=True).then_inc(f_mm.sem, 1)

            def taps_mm(l, o):
                for p in range(T):
                    e.matmul(PS[:, TAP_BANKS[o * 2 + p], :], H2[0:HYF, p * P:(p + 1) * P], fil[0:HYF, F_W3 + o * 512:F_W3 + (o + 1) * 512],
                             start=True, stop=True).then_inc(f_w3.sem, 1)

            def ffn(l, f, base, j, turn):
                norm(l, j, turn)
                gate_up(l, turn, base, pos(base), 0, 0, True)
                gate_up(l, turn, base + 1, pos(base + 1), 1, 0, True)

                def chunk(c, pr, first=False):
                    q = f * CH + (c - 1)
                    gate_up(l, turn, base + 3 * c - 1, pos(base + 2), 0, pr, False)
                    if f == 0 and first:
                        e.wait_ge(f_arg.sem, f_arg.at(l, 1))
                    gate_up(l, turn, base + 3 * c, pos(base), 1, pr, False)
                    if f == 0 and c is last:
                        filter_mm(l, 1, F_W2, H1, HYF, 7)
                    down(l, base + 3 * c + 1, pos(base + 1), q, 1 - pr, first, False, f)
                last = CH - 1
                if f == 0:
                    filter_mm(l, 0, F_W1, fil[:, F_Z:F_Z + SEQ], HYE, 7)
                chunk(1, 1, True)
                with e.Fori(0, (CH - 3) // 2) as i:
                    chunk(i * 2 + 2, 0)
                    chunk(i * 2 + 3, 1)
                chunk(last, last % 2)
                down(l, base + FFN_SLOTS - 1, pos(base + FFN_SLOTS - 1), f * CH + last, last % 2, False, True, f)

            def level_scores(l, b, bank=0):
                if b >= 0:
                    e.wait_ge(g_lq.sem, g_lq.at(l, b + 1))
                    e.wait_ge(g_la.sem, g_la.at(l, b + 1))
                qk = QK if b < 0 else QKL[b % 2]
                for t in range(T):
                    o = t if b < LEVELS - 1 else 1 - t
                    for h in range(H):
                        r = e.matmul(PS[:, bank + h, t * P:(t + 1) * P], qk[32 * h:32 * h + 32, 1, t * P:(t + 1) * P],
                                     qk[32 * h:32 * h + 32, 0, o * P:(o + 1) * P], start=True, stop=True)
                r.then_inc(g_ls.sem, 1)

            def hy_dft(l, o, b):
                for part in range(2):
                    for m in range(2):
                        for p in range(T):
                            r = e.matmul(PS[:, b + part, m * 256:(m + 1) * 256], dft[:, p, part * 256 + m * P:part * 256 + (m + 1) * P],
                                         NV[:, 0, p, :], start=(p == 0), stop=(p == T - 1))
                r.then_inc(h_u.sem, 1)

            def hy_inverse(l, o, b, halves=range(T)):
                e.wait_ge(h_y.sem, h_y.at(l, o + 1))
                for t in halves:
                    for m in range(4):
                        r = e.matmul(PS[:, b, t * 256:(t + 1) * 256], idft[:, m, t * P:(t + 1) * P], Y[:, m, :], start=(m == 0), stop=(m == 3))
                return r

            def scores(l, s, heads=range(H)):
                for h in heads:
                    out = PS[:, 4 + 2 * s + h // 2, (h % 2) * SEQ:(h % 2 + 1) * SEQ]
                    e.matmul(out, QN[:, h, s * P:(s + 1) * P], KN[:, h, :], start=True, stop=False)
                    r = e.matmul(out, QR[0:DR, h, s * P:(s + 1) * P], KR[0:DR, :], start=False, stop=True)
                return r

            def turn_probs(l, s):
                e.wait_ge(a_p.sem, a_p.at(l, s + 1))
                for k in range(T):
                    for h in range(H):
                        r = e.transpose(PS[:, 4 + 2 * s + k, h * P:(h + 1) * P], PE_[:, h, k * P:(k + 1) * P], ident)
                r.then_inc(a_pt.sem, 1)

            def attend(l, s):
                e.wait_ge(a_pte.sem, a_pte.at(l, s + 1))
                for h in range(H):
                    for k in range(T):
                        r = e.matmul(PS[:, 4 + 2 * s, h * P:(h + 1) * P], PT[:, k, h, :], VM[:, k, h * P:(h + 1) * P], start=(k == 0), stop=(k == T - 1))
                r.then_inc(a_o.sem, 1)

            def turn_conv(l, dst, bank):
                for t in range(T):
                    for j in range(2):
                        r = e.transpose(PS[:, bank, t * 256 + j * P:t * 256 + (j + 1) * P], C[:, dst + j, t * P:(t + 1) * P], ident)
                r.then_inc(c_tr.sem, 1)

            def project(l, g, t, i):
                p, k = pos(S_WO + g), Y_TILES[g][i]
                for m in range(2):
                    r = passes(PS[:, t * 2 + m, :], XH[:, k, t * P:(t + 1) * P], XL[:, k, t * P:(t + 1) * P],
                               WH[p][:, 2 * i + m, :], WL[p][:, 2 * i + m, :], g == 0 and i == 0, g == 3 and i == 1)
                    if g == 3 and i == 1 and t * m == 0:
                        r.then_inc(s_sum.sem, 1)
                return r

            with e.Fori(0, DEPTH) as l:
                ffn(l, 0, 0, 0, 0)
                e.wait_ge(s_in.sem, 16 * N_IN)
                e.wait_ge(f_sin.sem, f_sin.at(l, 2))
                taps_mm(l, 0)
                norm(l, 1, 1)
                taps_mm(l, 1)
                e.wait_ge(f_hw.sem, f_hw.at(l, 2))
                for i in range(2):
                    rows(l, 1, S_G3 + i, i, 480, (5, 6)).then_inc(s_used.sem, 1)
                for i in range(2):
                    columns(l, 1, S_G2 + i, i, [(128 * n, n) for n in range(4)]).then_inc(s_used.sem, 1)
                e.wait_ge(q_n.sem, q_n.at(l))
                e.wait_ge(q_kr.sem, q_kr.at(l))
                for n in range(2):
                    for t in range(T):
                        r = e.transpose(PS[:, 5, n * SEQ + t * P:n * SEQ + (t + 1) * P], xn[:, t, 256 + n * P:256 + (n + 1) * P], ident)
                r.then_inc(q_tr.sem, 1)
                for t in range(T):
                    e.transpose(PS[:, 6, t * P:(t + 1) * P], xn[:, t, 512:640], ident)
                    r = e.transpose(PS[:, 6, SEQ + t * P:SEQ + (t + 1) * P], xn[:, t, 640:768], ident)
                r.then_inc(q_tr.sem, 1)
                e.wait_ge(s_fil.sem, s_fil.at(l, 64))
                e.wait_ge(f_hs.sem, f_hs.at(l))
                for b, what in ((4, 256), (2, None), (3, None), (0, 0), (1, P)):
                    if b == 2:
                        e.wait_ge(g_qk.sem, g_qk.at(l))
                    if b == 0:
                        e.wait_ge(c_conv.sem, c_conv.at(l, 2))
                    for p in range(T):
                        if what is None:
                            w, h = dft[:, p, (b - 2) * P:(b - 1) * P], HS
                        else:
                            w, h = fil[:, F_DFT + p * 384 + what:F_DFT + p * 384 + what + P], HS if b == 4 else HD
                        r = e.matmul(PS[:, b, :], w, h[:, p, :], start=(p == 0), stop=(p == T - 1))
                    r.then_inc(k_mm.sem, 1)
                    if b == 4:
                        e.wait_ge(g_in.sem, g_in.at(l))
                        for d in range(2):
                            r = e.matmul(PS[:, 7, d * SEQ:(d + 1) * SEQ], wg[64:96, d, :], hid[64:96, 0, :], start=True, stop=True)
                        r.then_inc(g_z.sem, 1)
                e.wait_ge(g_az.sem, g_az.at(l))
                turn_conv(l, 0, 7)
                e.wait_ge(k_ev.sem, k_ev.at(l, 5))
                for i in range(2):
                    columns(l, 1, S_G1 + i, i, [(128 * n, n) for n in range(4)]).then_inc(s_used.sem, 1)
                e.wait_ge(q_lo.sem, q_lo.at(l, 2))
                e.wait_ge(q_krt.sem, q_krt.at(l))
                rows(l, 1, S_G4, 0, 512, (5, 6)).then_inc(s_used.sem, 1)
                e.wait_ge(c_nat.sem, c_nat.at(l, 1))
                e.wait_ge(c_conv.sem, c_conv.at(l, 4))
                turn_conv(l, 0, 7)
                e.wait_ge(c_conv.sem, c_conv.at(l, 6))
                turn_conv(l, 2, 4)
                rows(l, 1, S_G4 + 1, 1, 512, (5, 6)).then_inc(s_used.sem, 1)
                e.wait_ge(c_nat.sem, c_nat.at(l, 2))
                hy_dft(l, 0, 0)
                e.wait_ge(s_lo.sem, s_lo.at(l, S_UQN + 1))
                p = pos(S_UQN)
                for h in range(H):
                    for k in range(2):
                        r = passes(PS[:, 2 + h // 2, (h % 2) * SEQ:(h % 2 + 1) * SEQ], WH[p][:, k, h * P:(h + 1) * P], WL[p][:, k, h * P:(h + 1) * P],
                                   HH[:, k, :], HL[:, k, :], k == 0, k == 1)
                r.then_inc(s_used.sem, 1)
                e.wait_ge(s_lo.sem, s_lo.at(l, S_UQR + 1))
                p = pos(S_UQR)
                for t in range(T):
                    for k in range(2):
                        r = passes(PS[:, 7, t * 256:(t + 1) * 256], HH[:, k, t * P:(t + 1) * P], HL[:, k, t * P:(t + 1) * P],
                                   WH[p][:, k, 0:256], WL[p][:, k, 0:256], k == 0, k == 1)
                r.then_inc(s_used.sem, 1)
                e.wait_ge(s_lo.sem, s_lo.at(l, S_UKV + 1))
                e.wait_ge(c_nat.sem, c_nat.at(l, 3))
                p = pos(S_UKV)

                def keys(heads):
                    for h in heads:
                        r = passes(PS[:, (4, 1)[h // 2], (h % 2) * SEQ:(h % 2 + 1) * SEQ], WH[p][:, 0, h * P:(h + 1) * P],
                                   WL[p][:, 0, h * P:(h + 1) * P], KVH[:], KVL[:], True, True)
                    return r
                keys((0, 1))
                for t in range(T):
                    e.wait_ge(g_vr.sem, g_vr.at(l, t + 1))
                    passes(PS[:, 5 + t, :], KVH[:, t * P:(t + 1) * P], KVL[:, t * P:(t + 1) * P], WH[p][:, 1, :], WL[p][:, 1, :], True, True)
                e.wait_ge(h_pr.sem, h_pr.at(l, 1))
                keys((2, 3)).then_inc(s_used.sem, 1)
                hy_inverse(l, 0, 0).then_inc(h_inv.sem, 1)
                e.wait_ge(a_qr.sem, a_qr.at(l))
                e.wait_ge(a_qn.sem, a_qn.at(l, 2))
                hold(e, "pe")
                for h in range(H):
                    for t in range(T):
                        r = e.transpose(PS[0:DR, 2 + h // 2, (h % 2) * SEQ + t * P:(h % 2) * SEQ + (t + 1) * P],
                                        xn[:, t, 768 + h * DR:768 + (h + 1) * DR], ident)
                r.then_inc(a_qtr.sem, 1)
                e.wait_ge(a_v.sem, a_v.at(l, 2))
                e.wait_ge(h_z.sem, h_z.at(l, 1))
                hy_dft(l, 1, 6)
                e.wait_ge(a_qre.sem, a_qre.at(l, 2))
                scores(l, 0).then_inc(a_s.sem, 1)
                level_scores(l, -1)
                hy_inverse(l, 1, 6, (0,))
                level_scores(l, 0)
                hy_inverse(l, 1, 6, (1,)).then_inc(h_inv.sem, 1)
                level_scores(l, 1)
                turn_probs(l, 0)
                e.wait_ge(h_z.sem, h_z.at(l, 2))
                scores(l, 1, (0,))
                level_scores(l, 2)
                scores(l, 1, (1,))
                e.wait_ge(a_pte.sem, a_pte.at(l, 1))
                e.wait_ge(h_yy.sem, h_yy.at(l))
                turn_group(l, 2, 0, Y_BANKS[0], Y_TILES[0])
                level_scores(l, 3)
                scores(l, 1, (2, 3)).then_inc(a_s.sem, 1)
                level_scores(l, 4)
                attend(l, 0)
                level_scores(l, 5)
                turn_probs(l, 1)
                e.wait_ge(g_la.sem, g_la.at(l, 7))
                e.wait_ge(s_lo.sem, s_lo.at(l, S_WO + 1))
                e.wait_ge(s_xl.sem, s_xl.at(l, 9))
                project(l, 0, 0, 0)
                attend(l, 1)
                project(l, 0, 0, 1)
                e.wait_ge(a_oe.sem, a_oe.at(l, 2))
                level_scores(l, 6, 4)
                project(l, 0, 1, 0)
                level_scores(l, 7, 4)
                project(l, 0, 1, 1).then_inc(s_used.sem, 1)
                e.wait_ge(g_la.sem, g_la.at(l, LEVELS + 1))
                e.wait_ge(a_y.sem, a_y.at(l))
                for g in range(1, 3):
                    turn_group(l, 2, g, Y_BANKS[g], Y_TILES[g])
                for s in range(T):
                    for h in range(H):
                        for t in range(T):
                            a = AD[:, h, s, :] if t == s else AC[:, h, t, :]
                            r = e.matmul(PS[:, 7, s * 256 + h * GDV:s * 256 + (h + 1) * GDV], a, VG[:, t, h * GDV:(h + 1) * GDV],
                                         start=(t == 0), stop=(t == T - 1))
                r.then_inc(g_o.sem, 1)
                for g in range(1, 4):
                    if g == 2:
                        e.wait_ge(g_y.sem, g_y.at(l))
                        turn_group(l, 2, 3, Y_BANKS[3], Y_TILES[3])
                    e.wait_ge(s_lo.sem, s_lo.at(l, S_WO + g + 1))
                    e.wait_ge(s_xl.sem, s_xl.at(l, 8 + g + 1))
                    for t in range(T):
                        for i in range(2):
                            r = project(l, g, t, i)
                    r.then_inc(s_used.sem, 1)
                ffn(l, 1, FFN2, 2, 3)
        assert linked == LINKS, linked


N_IN = 3


def ffn_slots(gate, up, down):
    out, last = [], None
    for c in range(CH):
        at = slice(c * 256, (c + 1) * 256)
        for half in range(2):
            r = slice(at.start + half * P, at.start + (half + 1) * P)
            a = np.stack([gate[:, r].reshape(KD, P, P), up[:, r].reshape(KD, P, P)], 2)
            out.append(a.transpose(1, 0, 2, 3).reshape(P, SLOT))
        if last is not None:
            out.append(last)
        last = down[at].reshape(2, P, D).transpose(1, 0, 2).reshape(P, SLOT)
    return out + [last]


def mix_slots(w_in, w_uq, w_ukv, w_out):
    def two(cols):
        w = np.zeros((D, 512), np.float32)
        at = 0
        for a, b in cols:
            w[:, at:at + b - a] = w_in[:, a:b]
            at += b - a
        w = w.reshape(2, 4, P, 512).transpose(0, 2, 1, 3)
        return [w[0].reshape(P, SLOT), w[1].reshape(P, SLOT)]

    def one(parts):
        w = np.zeros((P, 4, 512), np.float32)
        for n, a in enumerate(parts):
            w[:, n, :a.shape[1]] = a
        return [w.reshape(P, SLOT)]
    out = two([(768, 1216), (1728, 1760)])
    out += two([(512, 768), (1216, 1472)])
    out += two([(0, 512)])
    out += two([(1472, 1728), (1760, 2016)])
    uq = w_uq.reshape(2, P, H, DN + DR)
    out += one([uq[k, :, :, :DN].reshape(P, H * DN) for k in range(2)])
    out += one([uq[k, :, :, DN:].reshape(P, H * DR) for k in range(2)])
    ukv = w_ukv.reshape(P, H, DN + DV)
    out += one([ukv[:, :, :DN].reshape(P, 512), ukv[:, :, DN:].reshape(P, 512)])
    for ks in Y_TILES:
        out.append(np.stack([w_out[k * P:(k + 1) * P] for k in ks], 1).reshape(P, SLOT))
    return out


def shape_constants():
    f32 = np.float32
    f = np.arange(256)
    ang = 2 * np.pi / 512 * ((f[:, None] * f[None, :]) % 512)
    cos, sin = np.cos(ang), np.sin(ang)
    nyq = 1.0 - 2.0 * (f % 2)
    sin_n, cos_n = -sin, cos[:, :P].copy()
    sin_n[:, 0], cos_n[:, 0] = nyq, nyq
    dft = np.concatenate([cos, sin_n], 1).reshape(T, P, 512).transpose(1, 0, 2).reshape(P, 1024)
    w = np.where(f == 0, 1.0, 2.0)[:, None] / 512
    inv_im = -w * sin
    inv_im[0] = nyq / 512
    inv = np.concatenate([w * cos, inv_im]).reshape(4, P, SEQ).transpose(1, 0, 2).reshape(P, 1024)
    fil_dft = np.concatenate([-sin, cos_n], 1).reshape(T, P, 384).transpose(1, 0, 2).reshape(P, 768)

    p = np.arange(SEQ, dtype=f32)
    t = p / f32(SEQ - 1)
    bands = np.linspace(1e-4, 15, 16, dtype=f32)
    a = (f32(2 * math.pi) * p / f32(SEQ))[:, None] * bands[None, :]
    z = np.concatenate([t[:, None], np.cos(a), -np.sin(a)], -1)
    lo_, hi_ = math.log(1e-2) / 1.5, math.log(1e-2) / 0.3
    win = np.exp(-t[:, None] * np.abs(np.linspace(lo_, hi_, HYW, dtype=f32))[None, :])
    win_b = win.copy()
    win_b[0] = 0
    win = np.concatenate([win, win_b], 1).reshape(T, P, 512).transpose(1, 0, 2).reshape(P, 1024)

    inv_f = f32(10000.0) ** (-np.arange(32, dtype=f32) * f32(2.0) / f32(DR))
    a = p[:, None] * inv_f[None, :].astype(f32)
    rope = np.stack([np.concatenate([np.cos(a)] * 2, 1), np.concatenate([-np.sin(a), np.sin(a)], 1)])
    rope = rope.reshape(2, T, P, DR).transpose(2, 0, 1, 3).reshape(P, 2 * T * DR)

    i = np.arange(P)
    mask = np.stack([(i[:, None] >> (b + 1) == i[None, :] >> (b + 1)) & (i[:, None] >> b != i[None, :] >> b)
                     for b in range(LEVELS - 1)], 1).reshape(P, -1)

    cst = np.zeros((P, NCST), f32)
    cst[:, :P] = np.eye(P)
    cst[:, I_D:I_CQ] = D * EPS
    cst[:, I_CQ:I_M] = [1 / 256, 1 / 128, 1 / 256, 1 / 128]
    cst[:, I_M:I_H] = 1 / 512
    cst[:, I_H:I_G] = 1 / 256
    cst[:, I_G:I_EPS] = 1 / 64
    cst[:, I_EPS:I_POW] = EPS
    cst[:, I_POW:] = -0.5
    dft = np.concatenate([dft, inv], 1)
    return {n: a.astype(f32) for n, a in dict(cst=cst, dft=dft, rope=rope, win=win, z=z.T, fil_dft=fil_dft, mask=mask).items()}


def kernel(**inputs):
    import concourse.bacc as _bacc
    from concourse import mybir as _mybir
    from concourse.bass_utils import run_bass_kernel_spmd as _run

    a = {k: np.asarray(v) for k, v in inputs.items()}
    k = shape_constants()
    f32 = np.float32
    slots, par = [], np.zeros((P, DEPTH + 1, NPAR), f32)
    fil, gates = np.zeros((DEPTH, P, NFIL), f32), np.zeros((DEPTH, 32, 2 * P), f32)
    for l in range(DEPTH):
        slots += ffn_slots(a["ffn1_w_gate"][l], a["ffn1_w_up"][l], a["ffn1_w_down"][l])
        slots += mix_slots(a["w_in"][l], a["mla_w_uq"][l], a["mla_w_ukv"][l], a["w_out"][l])
        slots += ffn_slots(a["ffn2_w_gate"][l], a["ffn2_w_up"][l], a["ffn2_w_down"][l])

        def tiles(v):
            return v.reshape(-1, P).T
        q = par[:, l]
        q[:, C_G1:C_GM] = tiles(a["ffn1_norm"][l])
        q[:, C_GM:C_G2] = tiles(a["mix_norm"][l])
        q[:, C_G2:C_QN] = tiles(a["ffn2_norm"][l])
        q[:, C_QN:C_KVN] = tiles(a["mla_q_norm"][l])
        q[:, C_KVN:C_GO] = tiles(a["mla_kv_norm"][l])
        q[:, C_GO:C_W0] = tiles(np.concatenate([a["hy_out_norm"][l], a["mla_out_norm"][l]] + [a["gla_head_norm"][l]] * 4))
        for n, c in enumerate((C_W0, C_W1, C_W2)):
            q[:, c:c + 6] = tiles(a["hy_conv_w"][l, n])
        q[:, C_CB:C_BG] = tiles(a["hy_conv_b"][l])
        q[:, C_BG] = a["gla_b_gate_fwd"][l]
        q[:, C_BG + 1] = a["gla_b_gate_bwd"][l]
        for c, n in ((C_FB1, "b1"), (C_FF1, "freq1"), (C_FB2, "b2"), (C_FF2, "freq2")):
            q[:HYF, c] = a["hy_filt_" + n][l]
        g = fil[l]
        g[:, F_WIN:F_Z] = k["win"]
        g[:HYE, F_Z:F_W1] = k["z"]
        g[:HYE, F_W1:F_W2] = a["hy_filt_w1"][l]
        g[:HYF, F_W2:F_W3] = a["hy_filt_w2"][l]
        g[:HYF, F_W3:F_DFT] = a["hy_filt_w3"][l]
        g[:, F_DFT:F_SKIP] = k["fil_dft"]
        g[0, F_SKIP:] = a["hy_skip"][l].reshape(-1)
        gates[l, 0:16, 0:P] = a["gla_w_gate_fwd"][l]
        gates[l, 16:32, P:] = a["gla_w_gate_bwd"][l]
    arrays = {"x": a["x"][0], "w": np.stack(slots), "par": par.reshape(P, -1), "cst": k["cst"], "fil": fil, "gates": gates,
              "dft": k["dft"], "rope": k["rope"], "mask": k["mask"], "fin": a["final_norm"]}
    arrays = {f"in_{n}_dram": np.ascontiguousarray(v) for n, v in arrays.items()}
    nc = _bacc.Bacc("TRN2", target_bir_lowering=False, num_devices=1)
    args = [nc.dram_tensor(n, v.shape, _mybir.dt.from_np(v.dtype), kind="ExternalInput").ap() for n, v in arrays.items()]
    args.append(nc.dram_tensor("out_0_dram", (SEQ, D), F32, kind="ExternalOutput").ap())
    build(nc, *args)
    r = _run(nc, [arrays], core_ids=[0])
    return r.results[0]["out_0_dram"].reshape(1, SEQ, D)
```
